# Optimizing a Trainium2 kernel written in Bass

```python
import jax, jax.numpy as jnp
from jax import lax
import numpy as np
import math

D_MODEL = 1024
BATCH = 1
SEQ = 256
DEPTH = 2

CTX_LEN = 256
GRID_W = 64
HEAD_DIM = 64
N_Q_HEADS = 8
N_KV_HEADS = 2
GQA_GROUP = N_Q_HEADS // N_KV_HEADS
Q_WIDTH = N_Q_HEADS * HEAD_DIM
KV_WIDTH = N_KV_HEADS * HEAD_DIM
CONV_WIDTH = D_MODEL - Q_WIDTH
CONV_KERNEL = 31
IN_COLS = Q_WIDTH + 2 * KV_WIDTH + 2 * CONV_WIDTH
Q_BLOCK = 128
ROPE_THETA = 10000.0
ATTN_SCALE = HEAD_DIM ** -0.5
PEER_HEADS = 8
PEER_KEYS = 128
PEER_N = PEER_KEYS * PEER_KEYS
PEER_QDIM = 128
PEER_HALF = PEER_QDIM // 2
PEER_TOPK = 16
PEER_CHUNK = 128
EPS = 1e-6


def rms(x):
    xf = x.astype(jnp.float32)
    return (xf * lax.rsqrt(jnp.mean(xf * xf, axis=-1, keepdims=True) + EPS)).astype(x.dtype)

def layer_norm(x, g, b):
    xf = x.astype(jnp.float32)
    mu = jnp.mean(xf, axis=-1, keepdims=True)
    var = jnp.mean(jnp.square(xf - mu), axis=-1, keepdims=True)
    return ((xf - mu) * lax.rsqrt(var + 1e-5)).astype(x.dtype) * g + b

def modulate(x, shift, scale):
    return rms(x) * (1 + scale) + shift

def rope_tables(row, col):
    n = HEAD_DIM // 4
    inv = ROPE_THETA ** (-jnp.arange(n, dtype=jnp.float32) / n)
    ang = jnp.concatenate([row.astype(jnp.float32)[:, None] * inv,
                           col.astype(jnp.float32)[:, None] * inv], axis=-1)
    return jnp.cos(ang), jnp.sin(ang)

def apply_rope(x, cos, sin):
    half = HEAD_DIM // 2
    x1, x2 = x[..., :half], x[..., half:]
    c = cos[None, :, None, :].astype(x.dtype)
    s = sin[None, :, None, :].astype(x.dtype)
    return jnp.concatenate([x1 * c - x2 * s, x1 * s + x2 * c], axis=-1)

def split_cols(p):
    return jnp.split(p, [Q_WIDTH, Q_WIDTH + KV_WIDTH, Q_WIDTH + 2 * KV_WIDTH], axis=-1)

def gqa_core(q, k, v):
    s = jnp.einsum('bqhgd,bkhd->bhgqk', q, k).astype(jnp.float32) * ATTN_SCALE
    p = jax.nn.softmax(s, axis=-1).astype(v.dtype)
    return jnp.einsum('bhgqk,bkhd->bqhgd', p, v)

def attend_latent(q, k_all, v_all):
    B, S = q.shape[:2]
    nb = S // Q_BLOCK
    qb = q.reshape(B, nb, Q_BLOCK, N_KV_HEADS, GQA_GROUP, HEAD_DIM).transpose(1, 0, 2, 3, 4, 5)
    o = lax.map(lambda qi: gqa_core(qi, k_all, v_all), qb)
    return o.transpose(1, 0, 2, 3, 4, 5).reshape(B, S, Q_WIDTH)

def attend_context(q, k, v):
    B, L = q.shape[:2]
    o = gqa_core(q.reshape(B, L, N_KV_HEADS, GQA_GROUP, HEAD_DIM), k, v)
    return o.reshape(B, L, Q_WIDTH)

def conformer_conv(u, conv_w, conv_b, ln_g, ln_b):
    a, gate = jnp.split(u, 2, axis=-1)
    g = a * jax.nn.sigmoid(gate)
    y = lax.conv_general_dilated(
        g, conv_w[:, None, :], window_strides=(1,),
        padding=[(CONV_KERNEL // 2, CONV_KERNEL // 2)],
        dimension_numbers=('NWC', 'WIO', 'NWC'),
        feature_group_count=CONV_WIDTH) + conv_b
    return jax.nn.silu(layer_norm(y, ln_g, ln_b))

def merge_groups(o_attn, o_conv, beta_attn, beta_conv, w_o):
    o = jnp.concatenate([rms(o_attn) * beta_attn, rms(o_conv) * beta_conv], axis=-1)
    return o @ w_o

def peer(h, w_pq, sub_keys, u_tab, v_tab):
    B, T, D = h.shape
    q = (h @ w_pq).reshape(B, T, PEER_HEADS, 2, PEER_HALF)
    s = jnp.einsum('bthcd,hckd->bthck', q, sub_keys).astype(jnp.float32)
    top_s, top_i = lax.top_k(s, PEER_TOPK)
    cand = top_s[..., 0, :, None] + top_s[..., 1, None, :]
    best_s, best_j = lax.top_k(cand.reshape(B, T, PEER_HEADS, PEER_TOPK * PEER_TOPK), PEER_TOPK)
    i1 = jnp.take_along_axis(top_i[..., 0, :], best_j // PEER_TOPK, axis=-1)
    i2 = jnp.take_along_axis(top_i[..., 1, :], best_j % PEER_TOPK, axis=-1)
    expert = i1 * PEER_KEYS + i2
    w = jax.nn.softmax(best_s, axis=-1)
    n_chunks = (B * T) // PEER_CHUNK
    hx = h.reshape(n_chunks, PEER_CHUNK, D)
    ex = expert.reshape(n_chunks, PEER_CHUNK, PEER_HEADS * PEER_TOPK)
    wx = w.reshape(n_chunks, PEER_CHUNK, PEER_HEADS * PEER_TOPK)

    def chunk(args):
        hc, ec, wc = args
        u = jnp.take(u_tab, ec, axis=0)
        act = jax.nn.gelu(jnp.einsum('cd,ced->ce', hc, u), approximate=False)
        v = jnp.take(v_tab, ec, axis=0)
        return jnp.einsum('ce,ced->cd', (act * wc).astype(h.dtype), v)

    return lax.map(chunk, (hx, ex, wx)).reshape(B, T, D)

def first_inputs(seed: int = 0) -> dict:
    key = jax.random.key(seed)
    ks = jax.random.split(key, 22)
    D = D_MODEL

    def nrm(k, shape, s):
        return jax.random.normal(k, shape, jnp.float32) * s

    return {
        "x": nrm(ks[0], (BATCH, SEQ, D), 1.0),
        "c": nrm(ks[1], (BATCH, D), 1.0),
        "ctx": nrm(ks[2], (BATCH, CTX_LEN, D), 1.0),
        "c_ctx": nrm(ks[3], (D,), 1.0),
        "w_mod": nrm(ks[4], (DEPTH, D, 6 * D), 0.5 * D ** -0.5),
        "b_mod": nrm(ks[5], (DEPTH, 6 * D), 0.02),
        "w_in": nrm(ks[6], (DEPTH, D, IN_COLS), D ** -0.5),
        "q_gain": 1.0 + nrm(ks[7], (DEPTH, HEAD_DIM), 0.02),
        "k_gain": 1.0 + nrm(ks[8], (DEPTH, HEAD_DIM), 0.02),
        "conv_w": nrm(ks[9], (DEPTH, CONV_KERNEL, CONV_WIDTH), CONV_KERNEL ** -0.5),
        "conv_b": nrm(ks[10], (DEPTH, CONV_WIDTH), 0.02),
        "ln_g": 1.0 + nrm(ks[11], (DEPTH, CONV_WIDTH), 0.02),
        "ln_b": nrm(ks[12], (DEPTH, CONV_WIDTH), 0.02),
        "beta_attn": 1.0 + nrm(ks[13], (DEPTH, Q_WIDTH), 0.02),
        "beta_conv": 1.0 + nrm(ks[14], (DEPTH, CONV_WIDTH), 0.02),
        "w_o": nrm(ks[15], (DEPTH, D, D), D ** -0.5),
        "peer_wq": nrm(ks[16], (DEPTH, D, PEER_HEADS * PEER_QDIM), D ** -0.5),
        "peer_keys": nrm(ks[17], (DEPTH, PEER_HEADS, 2, PEER_KEYS, PEER_HALF), PEER_HALF ** -0.5),
        "peer_u": nrm(ks[18], (DEPTH, PEER_N, D), D ** -0.5),
        "peer_v": nrm(ks[19], (DEPTH, PEER_N, D), 0.5),
        "final_g": 1.0 + nrm(ks[20], (D,), 0.02),
    }

def first_block(x, c, ctx, c_ctx, w_mod, b_mod, w_in, q_gain, k_gain, conv_w, conv_b, ln_g, ln_b,
              beta_attn, beta_conv, w_o, peer_wq, peer_keys, peer_u, peer_v, final_g):
    B, S, D = x.shape
    L = ctx.shape[1]
    ROWS = S // GRID_W
    row = jnp.repeat(jnp.arange(ROWS), GRID_W)
    col = jnp.tile(jnp.arange(GRID_W), ROWS)
    cos, sin = rope_tables(row, col)
    sc = jax.nn.silu(c)
    sc_ctx = jax.nn.silu(c_ctx)
    h_ctx = ctx
    for l in range(DEPTH):
        last = l == DEPTH - 1
        sh1, s1, g1, sh2, s2, g2 = jnp.split((sc @ w_mod[l] + b_mod[l])[:, None, :], 6, axis=-1)
        csh1, cs1, cg1, csh2, cs2, cg2 = jnp.split(sc_ctx @ w_mod[l] + b_mod[l], 6, axis=-1)

        hc = modulate(h_ctx, csh1, cs1)
        if last:
            kc, vc = jnp.split(hc @ w_in[l][:, Q_WIDTH:Q_WIDTH + 2 * KV_WIDTH], 2, axis=-1)
        else:
            qc, kc, vc, uc = split_cols(hc @ w_in[l])
            qc = rms(qc.reshape(B, L, N_Q_HEADS, HEAD_DIM)) * q_gain[l]
        kc = rms(kc.reshape(B, L, N_KV_HEADS, HEAD_DIM)) * k_gain[l]
        vc = vc.reshape(B, L, N_KV_HEADS, HEAD_DIM)

        hx = modulate(x, sh1, s1)
        q, k, v, u = split_cols(hx @ w_in[l])
        q = apply_rope(rms(q.reshape(B, S, N_Q_HEADS, HEAD_DIM)) * q_gain[l], cos, sin)
        k = apply_rope(rms(k.reshape(B, S, N_KV_HEADS, HEAD_DIM)) * k_gain[l], cos, sin)
        v = v.reshape(B, S, N_KV_HEADS, HEAD_DIM)
        o_attn = attend_latent(q, jnp.concatenate([kc, k], axis=1), jnp.concatenate([vc, v], axis=1))
        o_conv = conformer_conv(u, conv_w[l], conv_b[l], ln_g[l], ln_b[l])
        x = x + g1 * merge_groups(o_attn, o_conv, beta_attn[l], beta_conv[l], w_o[l])

        x = x + g2 * peer(modulate(x, sh2, s2), peer_wq[l], peer_keys[l], peer_u[l], peer_v[l])

        if not last:
            oc_attn = attend_context(qc, kc, vc)
            oc_conv = conformer_conv(uc, conv_w[l], conv_b[l], ln_g[l], ln_b[l])
            h_ctx = h_ctx + cg1 * merge_groups(oc_attn, oc_conv, beta_attn[l], beta_conv[l], w_o[l])
            h_ctx = h_ctx + cg2 * peer(modulate(h_ctx, csh2, cs2), peer_wq[l], peer_keys[l], peer_u[l], peer_v[l])

    return rms(x) * final_g


DEPTH_2 = 1

D_MIX = D_MODEL
D_ATTN = D_MIX // 2
N_Q_HEADS_2 = D_ATTN // HEAD_DIM
Q_PER_KV = N_Q_HEADS_2 // N_KV_HEADS
WINDOW = 128
BLOCK = WINDOW
D_SSM = D_MIX - D_ATTN
SSM_GROUP = 16
N_SSM_GROUPS = D_SSM // SSM_GROUP
STATE = 64
D_KV = N_KV_HEADS * HEAD_DIM
D_IN = D_ATTN + 2 * D_KV + D_SSM
D_FF = ((8 * D_MODEL // 3 + 127) // 128) * 128
N_MOD = 9


def rms_norm(x, g):
    xf = x.astype(jnp.float32)
    y = xf * lax.rsqrt(jnp.mean(xf * xf, axis=-1, keepdims=True) + EPS)
    return (y * g.astype(jnp.float32)).astype(x.dtype)

def modulate_2(h, shift, scale):
    return h * (1.0 + scale[:, None, :]) + shift[:, None, :]

def swiglu(h, w_gate, w_up, w_down):
    return (jax.nn.silu(h @ w_gate) * (h @ w_up)) @ w_down

def alibi_slopes():
    i = jnp.arange(1, N_Q_HEADS_2 + 1, dtype=jnp.float32)
    return jnp.exp2(-8.0 * i / N_Q_HEADS_2)

def sliding_window_attention(q, k, v, sinks):
    b, s = q.shape[0], q.shape[1]
    nb = s // BLOCK
    qb = q.reshape(b, nb, BLOCK, N_KV_HEADS, Q_PER_KV, HEAD_DIM)
    kb = k.reshape(b, nb, BLOCK, N_KV_HEADS, HEAD_DIM)
    vb = v.reshape(b, nb, BLOCK, N_KV_HEADS, HEAD_DIM)
    pad = ((0, 0), (1, 0), (0, 0), (0, 0), (0, 0))
    kk = jnp.concatenate([jnp.pad(kb[:, :-1], pad), kb], axis=2)
    vv = jnp.concatenate([jnp.pad(vb[:, :-1], pad), vb], axis=2)

    scores = jnp.einsum('bnqkgd,bnjkd->bnkgqj', qb, kk).astype(jnp.float32) * (HEAD_DIM ** -0.5)

    qi = jnp.arange(BLOCK)[:, None]
    kj = jnp.arange(2 * BLOCK)[None, :]
    dist = qi + BLOCK - kj
    key_pos = jnp.arange(nb)[:, None, None] * BLOCK + kj[None] - BLOCK
    valid = (dist[None] >= 0) & (dist[None] < WINDOW) & (key_pos >= 0)

    slopes = alibi_slopes().reshape(N_KV_HEADS, Q_PER_KV)
    bias = -slopes[:, :, None, None] * dist.astype(jnp.float32)[None, None]
    scores = jnp.where(valid[None, :, None, None], scores + bias, -jnp.inf)

    sink = sinks.astype(jnp.float32).reshape(N_KV_HEADS, Q_PER_KV)[None, None, :, :, None, None]
    m = jnp.maximum(jnp.max(scores, axis=-1, keepdims=True), sink)
    p = jnp.exp(scores - m)
    p = p / (jnp.sum(p, axis=-1, keepdims=True) + jnp.exp(sink - m))
    out = jnp.einsum('bnkgqj,bnjkd->bnqkgd', p.astype(v.dtype), vv)
    return out.reshape(b, s, N_Q_HEADS_2 * HEAD_DIM)

def s5_ssm(u, a_re, a_im, log_step, b_re, b_im, c_re, c_im, d_skip, w_glu, b_glu):
    f32 = jnp.float32
    bsz, s = u.shape[0], u.shape[1]
    uf = u.astype(f32).reshape(bsz, s, N_SSM_GROUPS, SSM_GROUP)
    lam = lax.complex(a_re.astype(f32), a_im.astype(f32))
    dt = jnp.exp(log_step.astype(f32))[:, None]
    lam_bar = jnp.exp(lam * dt)
    b_mat = lax.complex(b_re.astype(f32), b_im.astype(f32))
    b_bar = ((lam_bar - 1.0) / lam)[:, :, None] * b_mat
    bu = jnp.einsum('bsgh,gph->bsgp', uf.astype(jnp.complex64), b_bar)
    a = jnp.broadcast_to(lam_bar, bu.shape)

    def combine(left, right):
        a_l, b_l = left
        a_r, b_r = right
        return a_r * a_l, a_r * b_l + b_r

    _, states = lax.associative_scan(combine, (a, bu), axis=1)
    c_mat = lax.complex(c_re.astype(f32), c_im.astype(f32))
    y = jnp.real(jnp.einsum('bsgp,ghp->bsgh', states, c_mat))
    y = y + uf * d_skip.astype(f32).reshape(N_SSM_GROUPS, SSM_GROUP)
    y = jax.nn.gelu(y.reshape(bsz, s, D_SSM))
    y = y * jax.nn.sigmoid(y @ w_glu.astype(f32) + b_glu.astype(f32))
    return y.astype(u.dtype)

def second_inputs(seed: int = 0) -> dict:
    key = jax.random.key(seed)
    ks = jax.random.split(key, 40)
    f32 = jnp.float32
    L = DEPTH_2
    nrm = lambda k, shape, s: jax.random.normal(k, shape, f32) * s
    gain = lambda k: 1.0 + 0.05 * jax.random.normal(k, (L, D_MODEL), f32)
    n_idx = jnp.arange(STATE, dtype=f32)
    return {
        "x": jax.random.normal(ks[0], (BATCH, SEQ, D_MODEL), f32),
        "c": jax.random.normal(ks[1], (BATCH, D_MODEL), f32),
        "w_ada": nrm(ks[2], (L, D_MODEL, N_MOD * D_MODEL), 0.5 * D_MODEL ** -0.5),
        "b_ada": nrm(ks[3], (L, N_MOD * D_MODEL), 0.02),
        "g_pre_ff1": gain(ks[4]),
        "g_post_ff1": gain(ks[5]),
        "w1_gate": nrm(ks[6], (L, D_MODEL, D_FF), D_MODEL ** -0.5),
        "w1_up": nrm(ks[7], (L, D_MODEL, D_FF), D_MODEL ** -0.5),
        "w1_down": nrm(ks[8], (L, D_FF, D_MODEL), D_FF ** -0.5),
        "g_pre_mix": gain(ks[9]),
        "g_post_mix": gain(ks[10]),
        "w_in": nrm(ks[11], (L, D_MODEL, D_IN), D_MODEL ** -0.5),
        "attn_sinks": nrm(ks[12], (L, N_Q_HEADS_2), 1.0),
        "ssm_a_re": -0.5 + 0.01 * jax.random.normal(ks[13], (L, N_SSM_GROUPS, STATE), f32),
        "ssm_a_im": math.pi * n_idx + 0.01 * jax.random.normal(ks[14], (L, N_SSM_GROUPS, STATE), f32),
        "ssm_log_step": jax.random.uniform(ks[15], (L, N_SSM_GROUPS), f32, math.log(1e-3), math.log(1e-1)),
        "ssm_b_re": nrm(ks[16], (L, N_SSM_GROUPS, STATE, SSM_GROUP), (2 * SSM_GROUP) ** -0.5),
        "ssm_b_im": nrm(ks[17], (L, N_SSM_GROUPS, STATE, SSM_GROUP), (2 * SSM_GROUP) ** -0.5),
        "ssm_c_re": nrm(ks[18], (L, N_SSM_GROUPS, SSM_GROUP, STATE), (2 * STATE) ** -0.5),
        "ssm_c_im": nrm(ks[19], (L, N_SSM_GROUPS, SSM_GROUP, STATE), (2 * STATE) ** -0.5),
        "ssm_d": nrm(ks[20], (L, D_SSM), 1.0),
        "ssm_w_glu": nrm(ks[21], (L, D_SSM, D_SSM), D_SSM ** -0.5),
        "ssm_b_glu": nrm(ks[22], (L, D_SSM), 0.02),
        "g_attn_out": 1.0 + 0.05 * jax.random.normal(ks[23], (L, D_ATTN), f32),
        "g_ssm_out": 1.0 + 0.05 * jax.random.normal(ks[24], (L, D_SSM), f32),
        "w_out": nrm(ks[25], (L, D_MIX, D_MODEL), D_MIX ** -0.5),
        "g_pre_ff2": gain(ks[26]),
        "g_post_ff2": gain(ks[27]),
        "w2_gate": nrm(ks[28], (L, D_MODEL, D_FF), D_MODEL ** -0.5),
        "w2_up": nrm(ks[29], (L, D_MODEL, D_FF), D_MODEL ** -0.5),
        "w2_down": nrm(ks[30], (L, D_FF, D_MODEL), D_FF ** -0.5),
    }

def second_block(x, c, w_ada, b_ada, g_pre_ff1, g_post_ff1, w1_gate, w1_up, w1_down,
              g_pre_mix, g_post_mix, w_in, attn_sinks, ssm_a_re, ssm_a_im, ssm_log_step,
              ssm_b_re, ssm_b_im, ssm_c_re, ssm_c_im, ssm_d, ssm_w_glu, ssm_b_glu,
              g_attn_out, g_ssm_out, w_out, g_pre_ff2, g_post_ff2, w2_gate, w2_up, w2_down):
    bsz, s = x.shape[0], x.shape[1]
    c_act = jax.nn.silu(c)
    for l in range(DEPTH_2):
        mod = c_act @ w_ada[l] + b_ada[l]
        (sh1, sc1, ga1, sh2, sc2, ga2, sh3, sc3, ga3) = jnp.split(mod, N_MOD, axis=-1)

        h = modulate_2(rms_norm(x, g_pre_ff1[l]), sh1, sc1)
        f = swiglu(h, w1_gate[l], w1_up[l], w1_down[l])
        x = x + 0.5 * ga1[:, None, :] * rms_norm(f, g_post_ff1[l])

        h = modulate_2(rms_norm(x, g_pre_mix[l]), sh2, sc2)
        proj = h @ w_in[l]
        q = proj[..., :D_ATTN].reshape(bsz, s, N_Q_HEADS_2, HEAD_DIM)
        k = proj[..., D_ATTN:D_ATTN + D_KV].reshape(bsz, s, N_KV_HEADS, HEAD_DIM)
        v = proj[..., D_ATTN + D_KV:D_ATTN + 2 * D_KV].reshape(bsz, s, N_KV_HEADS, HEAD_DIM)
        u = proj[..., D_ATTN + 2 * D_KV:]
        attn = sliding_window_attention(q, k, v, attn_sinks[l])
        ssm = s5_ssm(u, ssm_a_re[l], ssm_a_im[l], ssm_log_step[l], ssm_b_re[l], ssm_b_im[l],
                     ssm_c_re[l], ssm_c_im[l], ssm_d[l], ssm_w_glu[l], ssm_b_glu[l])
        mixed = jnp.concatenate([rms_norm(attn, g_attn_out[l]), rms_norm(ssm, g_ssm_out[l])], axis=-1)
        mixed = mixed @ w_out[l]
        x = x + ga2[:, None, :] * rms_norm(mixed, g_post_mix[l])

        h = modulate_2(rms_norm(x, g_pre_ff2[l]), sh3, sc3)
        f = swiglu(h, w2_gate[l], w2_up[l], w2_down[l])
        x = x + 0.5 * ga3[:, None, :] * rms_norm(f, g_post_ff2[l])
    return x


def setup_inputs(seed=0):
    out = dict(first_inputs(seed))
    for name, value in second_inputs(seed + 1).items():
        if name != "x":
            out[name + "_2"] = value
    return out


def reference(
    x, c, ctx, c_ctx, w_mod, b_mod, w_in, q_gain, k_gain, conv_w, conv_b, ln_g, ln_b, beta_attn,
    beta_conv, w_o, peer_wq, peer_keys, peer_u, peer_v, final_g, c_2, w_ada_2, b_ada_2,
    g_pre_ff1_2, g_post_ff1_2, w1_gate_2, w1_up_2, w1_down_2, g_pre_mix_2, g_post_mix_2, w_in_2,
    attn_sinks_2, ssm_a_re_2, ssm_a_im_2, ssm_log_step_2, ssm_b_re_2, ssm_b_im_2, ssm_c_re_2,
    ssm_c_im_2, ssm_d_2, ssm_w_glu_2, ssm_b_glu_2, g_attn_out_2, g_ssm_out_2, w_out_2,
    g_pre_ff2_2, g_post_ff2_2, w2_gate_2, w2_up_2, w2_down_2,
):
    x = first_block(
        x, c, ctx, c_ctx, w_mod, b_mod, w_in, q_gain, k_gain, conv_w, conv_b, ln_g, ln_b,
        beta_attn, beta_conv, w_o, peer_wq, peer_keys, peer_u, peer_v, final_g,
    )
    return second_block(
        x, c_2, w_ada_2, b_ada_2, g_pre_ff1_2, g_post_ff1_2, w1_gate_2, w1_up_2, w1_down_2,
        g_pre_mix_2, g_post_mix_2, w_in_2, attn_sinks_2, ssm_a_re_2, ssm_a_im_2, ssm_log_step_2,
        ssm_b_re_2, ssm_b_im_2, ssm_c_re_2, ssm_c_im_2, ssm_d_2, ssm_w_glu_2, ssm_b_glu_2,
        g_attn_out_2, g_ssm_out_2, w_out_2, g_pre_ff2_2, g_post_ff2_2, w2_gate_2, w2_up_2,
        w2_down_2,
    )


_drawn_inputs = setup_inputs


def setup_inputs(seed=0):
    import zlib

    import numpy as np

    out = dict(_drawn_inputs(seed))
    spreads = {}
    factors = {'q_gain': 8.0,
     'k_gain': 8.0,
     'conv_b': 3.409,
     'ln_g': 4.512,
     'ln_b': 4.835,
     'beta_attn': 4.75,
     'beta_conv': 4.914,
     'final_g': 2.85,
     'g_pre_ff1_2': 5.216,
     'g_post_ff1_2': 7.48,
     'g_pre_mix_2': 3.383,
     'g_post_mix_2': 12.21,
     'attn_sinks_2': 16.012,
     'ssm_a_re_2': 64.0,
     'ssm_a_im_2': 36.12,
     'ssm_log_step_2': 44.72,
     'ssm_b_re_2': 51.664,
     'ssm_b_im_2': 58.36,
     'ssm_c_re_2': 57.12,
     'ssm_c_im_2': 53.408,
     'ssm_b_glu_2': 39.808,
     'g_attn_out_2': 23.726,
     'g_ssm_out_2': 26.055,
     'g_pre_ff2_2': 5.677,
     'g_post_ff2_2': 26.998}
    for name, (base, spread) in spreads.items():
        noise = np.random.default_rng([zlib.crc32(name.encode()), seed]).standard_normal(out[name].shape)
        drawn = base * np.exp(spread * noise) if base else spread * noise
        out[name] = __import__('jax').numpy.asarray(drawn.astype(out[name].dtype))
    for name, factor in factors.items():
        out[name] = (out[name] * factor).astype(out[name].dtype)
    return out
```

```python
from contextlib import ExitStack

import numpy as np

import concourse.bass as bass
from concourse import mybir

F32 = mybir.dt.float32
U32 = mybir.dt.uint32
ALU = mybir.AluOpType
ACT = mybir.ActivationFunctionType
AX = mybir.AxisListType

RING = 4
SLOT = 4096
AREA = 22300
EPS = 1e-6
TWO_PI = 6.283185307179586

VEC = {}


def _layout():
    n = 0
    for l in range(2):
        for name, w in (("b_mod", 48), ("q_gain", 1), ("k_gain", 1), ("conv_w", 124), ("conv_b", 4),
                        ("ln_g", 4), ("ln_b", 4), ("beta_attn", 4), ("beta_conv", 4)):
            VEC[f"{name}{l}"] = (n, w)
            n += w
    for name, w in (("c", 8), ("c_ctx", 8), ("c2", 8), ("final_g", 8), ("b_ada", 72), ("pre1", 8), ("post1", 8),
                    ("prem", 8), ("postm", 8), ("pre2", 8), ("post2", 8), ("ssm_d", 4), ("b_glu", 4), ("g_attn", 4),
                    ("g_ssm", 4), ("a_re", 16), ("a_im", 16), ("log_step", 16), ("sinks", 8)):
        VEC[name] = (n, w)
        n += w
    VEC["n"] = n


_layout()

CON = {}


def _con_layout():
    n = 0
    for name, w in (("ones", 128), ("blk", 128), ("ident", 128), ("rot", 128), ("cos", 256), ("sin", 256),
                    ("iota", 128), ("eps", 2)):
        CON[name] = (n, w)
        n += w
    CON["n"] = n


_con_layout()


class Program:

    def __init__(self, nc, ctx):
        self.nc, self.ctx = nc, ctx
        self.queue = {e: [] for e in ("pe", "act", "dve", "pool", "sp")}
        self.count = {e: 0 for e in self.queue}
        self.sem = {e: ctx.enter_context(nc.semaphore(f"done_{e}")) for e in self.queue}
        self.seen = {e: {} for e in self.queue}
        self.held = {}

    def new_sem(self, name):
        self.sem[name] = self.ctx.enter_context(self.nc.semaphore(name))
        self.count[name] = 0
        return name

    def wait(self, e, waits):
        todo = [waits]
        while todo:
            w = todo.pop()
            if w is None:
                continue
            if isinstance(w, list):
                todo.extend(w)
                continue
            s, v = w
            if self.seen[e].get(s, 0) < v:
                self.seen[e][s] = v
                self.queue[e].append((s, v))

    def put(self, e, make, *waits):
        self.wait(e, list(waits) + [self.held.pop(e, None)])
        self.count[e] += 1
        self.queue[e].append((make, e, 1))
        return (e, self.count[e])

    def dma(self, e, sem, out, in_, *waits):
        self.wait(e, list(waits) + [self.held.pop(e, None)])
        self.count[sem] += 16
        self.queue[e].append((lambda eng: eng.dma_start(out, in_), sem, 16))
        return (sem, self.count[sem])

    def last(self, e):
        return (e, self.count[e])

    def phase(self, engines=("pe", "act", "dve")):
        now = [self.last(e) for e in engines]
        for e in list(engines) + ["pool"]:
            self.held[e] = [self.held.get(e), now]

    def emit(self, e, eng):
        for item in self.queue[e]:
            if len(item) == 2:
                eng.wait_ge(self.sem[item[0]], item[1])
            else:
                make, s, by = item
                make(eng).then_inc(self.sem[s], by)


def build(nc, A, out):
    with ExitStack() as ctx:
        _build(nc, ctx, A, out)


def _build(nc, ctx, A, out):
    pr = Program(nc, ctx)

    def sb(name, n):
        return ctx.enter_context(nc.sbuf_tensor(name, [128, n], F32))

    XT = sb("xT", 4096).rearrange("p (k t) -> p k t", k=8)
    HT = sb("hT", 4096).rearrange("p (k t) -> p k t", k=8)
    ACC = sb("acc", 4096).rearrange("p (k t) -> p k t", k=8)
    con = sb("con", CON["n"])
    vec = sb("vec", VEC["n"])
    mods = sb("mods", 2 * 96 + 72)
    scs = sb("scs", 32)
    ringt = sb("ring", RING * SLOT)
    area = sb("area", AREA)
    PS = [ctx.enter_context(nc.psum_tensor(f"ps{i}", [128, 512], F32)) for i in range(8)]
    scratch = nc.dram_tensor("w_scratch", (32, 128, 16, 128), F32, kind="Internal").ap()

    def C(name):
        o, w = CON[name]
        return con[:, o:o + w]

    def V(name, j=None, w=1):
        o, n = VEC[name]
        return vec[:, o:o + n] if j is None else vec[:, o + j:o + j + w]

    MOD = [mods[:, 96 * l:96 * l + 96].rearrange("p (m s) -> p m s", s=2) for l in range(2)]
    ADA = mods[:, 192:264]

    bank_free = [None] * 8
    bank_next = [0]
    kept = set()

    def bank():
        while bank_next[0] % 7 in kept:
            bank_next[0] += 1
        b = bank_next[0] % 7
        bank_next[0] += 1
        return b

    pieces = []

    class Piece:
        def __init__(self, src, n):
            self.n = len(pieces)
            self.src, self.size = src, n
            self.release = None
            self.slot = self.n % RING
            self.ap = ringt[:, self.slot * SLOT:self.slot * SLOT + n]
            self.here = (slot_sem[self.slot], 16 * (self.n // RING + 1))
            pieces.append(self)

    slot_sem = [pr.new_sem(f"slot{i}") for i in range(RING)]

    def weight(w, c0, cols):
        k = w.shape[0] // 128
        src = w.rearrange("(k p) m -> p k m", p=128)[:, :, c0:c0 + cols]
        p = Piece(src, k * cols)
        p.w = p.ap.rearrange("p (k m) -> p k m", k=k)
        return p

    def mm(b, parts, *waits, first=True):
        def make(eng):
            for o, pairs in parts:
                for n, (lhs, rhs) in enumerate(pairs):
                    ins = eng.matmul(o, lhs, rhs, start=(n == 0), stop=(n == len(pairs) - 1))
            return ins
        return pr.put("pe", make, bank_free[b] if first else None, *waits)

    def tp(b, parts, *waits):
        def make(eng):
            for o, i in parts:
                ins = eng.transpose(o, i, C("ident"))
            return ins
        return pr.put("pe", make, bank_free[b], *waits)

    def act(o, i, f, *waits, **kw):
        return pr.put("act", lambda e: e.activation(o, i, f, **kw), *waits)

    def tt(o, a, b, op, *waits, e="dve"):
        return pr.put(e, lambda g: g.tensor_tensor(o, a, b, op), *waits)

    def ts(o, a, s1, s2, op0, op1, *waits, e="dve"):
        if op1 is None:
            return pr.put(e, lambda g: g.tensor_scalar(o, a, s1, None, op0), *waits)
        return pr.put(e, lambda g: g.tensor_scalar(o, a, s1, s2, op0, op1), *waits)

    def stt(o, a, s, b, op0, op1, *waits):
        return pr.put("dve", lambda g: g.scalar_tensor_tensor(out=o, in0=a, scalar=s, in1=b, op0=op0, op1=op1), *waits)

    def cp(o, i, *waits, e="dve"):
        if e == "act":
            return pr.put(e, lambda g: g.copy(o, i), *waits)
        return pr.put(e, lambda g: g.tensor_copy(o, i), *waits)

    M, AD, SU = ALU.mult, ALU.add, ALU.subtract

    class Lay:
        def __init__(self, base=0):
            self.at = base

        def take(self, n):
            v = area[:, self.at:self.at + n]
            self.at += n
            assert self.at <= AREA, self.at
            return v

    s_con, s_vec, s_x = pr.new_sem("s_con"), pr.new_sem("s_vec"), pr.new_sem("s_x")
    t_vec = pr.dma("act", s_vec, vec[:, :], A["vec"])
    t_con = pr.dma("act", s_con, con[:, :], A["con"])
    t_x = pr.dma("act", s_x, XT, A["xT"].rearrange("(k p) t -> p k t", p=128))
    SC = scs[:, 0:16].rearrange("p (k s) -> p k s", s=2)
    SC2 = scs[:, 16:24]
    t_sc = act(SC[:, :, 0], V("c"), ACT.Silu, t_vec)
    t_sc = act(SC[:, :, 1], V("c_ctx"), ACT.Silu)
    t_sc = act(SC2, V("c2"), ACT.Silu)

    def mod_vectors(w, n, rhs, bias, dst, width):
        o = PS[7][:, 0:n * width].rearrange("p (m s) -> p m s", s=width)
        for j in range(n // 4):
            p = weight(w, 512 * j, 512)
            parts = [(o[:, 4 * j + i, :], [(p.w[:, k, 128 * i:128 * i + 128], rhs(k)) for k in range(8)])
                     for i in range(4)]
            t = mm(7, parts, p.here, t_sc, first=(j == 0))
            p.release = t
            yield None
        t = tt(dst, o, bias, AD, t, t_vec, pr.last("dve"))
        bank_free[7] = t
        yield t

    def mod_layer(l):
        return mod_vectors(A["w_mod"][l], 48, lambda k: SC[:, k, :],
                           V(f"b_mod{l}").unsqueeze(2).to_broadcast([128, 48, 2]), MOD[l], 2)

    def ada_layer():
        return mod_vectors(A["w_ada"], 72, lambda k: SC2[:, k:k + 1], V("b_ada").unsqueeze(2),
                           ADA.unsqueeze(2), 1)

    later = []

    def some(n):
        while n > 0 and later:
            got = next(later[0][0], "end")
            if got == "end":
                later.pop(0)
                continue
            if got is not None:
                later[0][1].append(got)
            n -= 1

    def inverse_root(src, chunks, T, sq, rstd, n, eps_col, *waits, lhs="ones"):
        ts_sq = []
        for k in range(chunks):
            ts_sq.append(act(sq(k), src(k), ACT.Square, *waits))
        b = bank()
        t = mm(b, [(PS[b][:, 0:T], [(C(lhs), sq(k)) for k in range(chunks)])], ts_sq[-1], t_con)
        t = act(rstd, PS[b][:, 0:T], ACT.Sqrt, t, pr.last("dve"), scale=1.0 / n, bias=C("eps")[:, eps_col:eps_col + 1])
        bank_free[b] = t
        return pr.put("dve", lambda g: g.reciprocal(rstd, rstd), t)

    def add1(v):
        return ts(v, v, 1.0, None, AD, None, pr.last("dve"))

    def modulated(streams, T, mult_of, add_of, rstd, gain=None, lo=0):
        t = inverse_root(lambda k: XT[:, k, lo:T], 8, T - lo, lambda k: ACC[:, k, lo:T], rstd[:, lo:T], 1024, 0,
                         t_x, pr.last("dve"), pr.last("pe"))
        for k in range(8):
            if gain is None:
                t1 = tt(HT[:, k, lo:T], XT[:, k, lo:T], rstd[:, lo:T], M, t, pr.last("pe"))
            else:
                t1 = stt(HT[:, k, lo:T], XT[:, k, lo:T], gain(k), rstd[:, lo:T], M, M, t, pr.last("pe"))
            for s, (a, z) in streams:
                t2 = ts(HT[:, k, a:z], HT[:, k, a:z], mult_of(k, s), add_of(k, s), M, AD, t1)
        return t2

    BOTH = [(0, (0, 256)), (1, (256, 512))]

    def attend(q, kT, vtok, dest, lay, tiles, q0, sinks, bias, t_in):
        P2 = [lay.take(512) for _ in range(2)]
        PT2 = [lay.take(1024).rearrange("p (c q) -> p c q", c=4) for _ in range(2)]
        st = lay.take(64)
        n = 0
        p_free = [None, None]
        pt_free = [None, None]
        nq = len(tiles)
        for i in range(4):
            bo = bank()
            kept.add(bo)
            t_o = []
            for kv in range(2):
                base = 64 * kv
                PT = PT2[kv]
                t_pt = []
                for qt, keys in enumerate(tiles):
                    N = 128 * len(keys)
                    k0 = 128 * keys[0]
                    b = bank()
                    t = mm(b, [(PS[b][:, 0:N], [(q[base:base + 64, i, q0 + 128 * qt:q0 + 128 * qt + 128],
                                                 kT[base:base + 64, k0:k0 + N])])], t_in)
                    S = PS[b][:, 0:N]
                    P = P2[n % 2][:, 0:N]
                    c = 8 * (n % 4)
                    mx, nb, den, rec, es = (st[:, c + j:c + j + 1] for j in range(5))
                    if bias is None:
                        t = pr.put("dve", lambda g, mx=mx, S=S: g.tensor_reduce(mx, S, AX.X, ALU.max), t)
                        t = ts(nb, mx, -0.125, None, M, None, t)
                        t = act(P, S, ACT.Exp, t, p_free[n % 2], scale=0.125, bias=nb, accum_out=den)
                        bank_free[b] = t
                    else:
                        h = i + 4 * kv
                        t = stt(P, S, 0.125, bias(h, qt, N), M, AD, t, p_free[n % 2])
                        bank_free[b] = t
                        t = pr.put("dve", lambda g, mx=mx, P=P: g.tensor_reduce(mx, P, AX.X, ALU.max), t)
                        t = ts(nb, mx, sinks(h), -1.0, ALU.max, M, t)
                        t2 = act(P, P, ACT.Exp, t, bias=nb, accum_out=den)
                        t3 = act(es, sinks(h), ACT.Exp, t, bias=nb)
                        t = tt(den, den, es, AD, t2, t3)
                    t = pr.put("dve", lambda g, rec=rec, den=den: g.reciprocal(rec, den), t)
                    t = ts(P, P, rec, None, M, None, t)
                    b = bank()
                    t = tp(b, [(PS[b][:, 128 * j:128 * j + 128], P[:, 128 * j:128 * j + 128])
                               for j in range(len(keys))], t, t_con)
                    p_free[n % 2] = t
                    o = PT[:, 0:len(keys), 128 * qt:128 * qt + 128]
                    t = cp(o, PS[b][:, 0:N].rearrange("p (c q) -> p c q", q=128), t, pt_free[kv], e="act")
                    bank_free[b] = t
                    t_pt.append(t)
                    n += 1
                if all(len(k) == len(tiles[0]) for k in tiles):
                    parts = [(PS[bo][base:base + 64, 0:128 * nq],
                              [(vtok[:, kc, base:base + 64], PT[:, j, 0:128 * nq]) for j, kc in enumerate(tiles[0])])]
                else:
                    parts = [(PS[bo][base:base + 64, 128 * qt:128 * qt + 128],
                              [(vtok[:, kc, base:base + 64], PT[:, j, 128 * qt:128 * qt + 128])
                               for j, kc in enumerate(keys)]) for qt, keys in enumerate(tiles)]
                t = mm(bo, parts, t_pt)
                pt_free[kv] = t
                t_o.append(t)
            t = cp(dest(i), PS[bo][:, 0:128 * nq], t_o)
            bank_free[bo] = t
            kept.discard(bo)
        return t

    def merged(OT, T, beta, sq, rstd, t_in, lo=0):
        for half in range(2):
            t = inverse_root(lambda k: OT[:, 4 * half + k, lo:T], 4, T - lo, lambda k: sq[:, k, lo:T],
                             rstd[:, lo:T], 512, 0, t_in, pr.last("pe"))
            for k in range(4):
                t = stt(OT[:, 4 * half + k, lo:T], OT[:, 4 * half + k, lo:T], beta(half, k), rstd[:, lo:T], M, M, t)
            t_in = t
        return t

    def mixer(l):
        last = l == 1
        T = 512
        Tq = 256 if last else 512
        streams_q = BOTH[:1] if last else BOTH
        lay = Lay()
        q = lay.take(2048).rearrange("p (k t) -> p k t", k=4)
        kk = lay.take(512)
        vT = lay.take(512)
        vtok = lay.take(512).rearrange("p (c d) -> p c d", c=4)
        gp = lay.take(4 * 2 * 286).rearrange("p (c s t) -> p c s t", c=4, s=2)
        y = lay.take(2048).rearrange("p (k t) -> p k t", k=4)
        OT = lay.take(4096).rearrange("p (k t) -> p k t", k=8)
        rstd = lay.take(512)
        tmps = [lay.take(512) for _ in range(4)]
        sq4 = ACC

        t_mod = mod_ready[l][0]
        t = modulated(BOTH, 512, lambda k, s: MOD[l][:, 8 + k, s:s + 1], lambda k, s: MOD[l][:, k, s:s + 1], rstd)
        t_h = [t, t_mod]
        W = A["w_in"][l]
        t_ms = pr.put("pool", lambda g: g.memset(gp, 0.0))

        def project(p, i, lo, hi):
            b = bank()
            t = mm(b, [(PS[b][:, 0:hi - lo], [(p.w[:, k, i:i + 128], HT[:, k, lo:hi]) for k in range(8)])], t_h, p.here)
            p.release = t
            return b, t

        p = weight(W, 0, 512)
        for i in range(4):
            b, t = project(p, 128 * i, 0, Tq)
            t_q = cp(q[:, i, 0:Tq], PS[b][:, 0:Tq], t, e="act")
            bank_free[b] = t_q
        p = weight(W, 512, 256)
        b, t = project(p, 0, 0, 512)
        t_k = cp(kk[:, :], PS[b][:, :], t, e="act")
        bank_free[b] = t_k
        b, t = project(p, 128, 0, 512)
        t_v = cp(vT[:, :], PS[b][:, :], t, e="act")
        bank_free[b] = t_v
        b = bank()
        t = tp(b, [(PS[b][:, 128 * c:128 * c + 128], vT[:, 128 * c:128 * c + 128]) for c in range(4)], t_v)
        t_vt = cp(vtok, PS[b][:, :].rearrange("p (c d) -> p c d", c=4), t, e="act")
        bank_free[b] = t_vt

        pg = [weight(W, 1280, 512), weight(W, 768, 512)]
        for i in range(4):
            bg, tg = project(pg[0], 128 * i, 0, Tq)
            ba, ta = project(pg[1], 128 * i, 0, Tq)
            sg = tmps[i % 2][:, 0:Tq]
            t = act(sg, PS[bg][:, 0:Tq], ACT.Sigmoid, tg, pr.last("dve"))
            bank_free[bg] = t
            for s, (a, z) in streams_q:
                t_g = tt(gp[:, i, s, 15:271], PS[ba][:, a:z], sg[:, a:z], M, t, ta, t_ms)
            bank_free[ba] = t_g

        for i in range(5):
            X = q[:, i, 0:Tq] if i < 4 else kk[:, :]
            TT = Tq if i < 4 else 512
            gain = V(f"q_gain{l}" if i < 4 else f"k_gain{l}")
            t1 = act(tmps[2][:, 0:TT], X, ACT.Square, pr.last("pe"))
            b = bank()
            t1 = mm(b, [(PS[b][:, 0:TT], [(C("blk"), tmps[2][:, 0:TT])])], t1)
            t1 = act(tmps[3][:, 0:TT], PS[b][:, 0:TT], ACT.Sqrt, t1, pr.last("dve"), scale=1.0 / 64, bias=C("eps")[:, 0:1])
            bank_free[b] = t1
            t1 = pr.put("dve", lambda g, TT=TT: g.reciprocal(tmps[3][:, 0:TT], tmps[3][:, 0:TT]), t1)
            t1 = stt(X, X, gain, tmps[3][:, 0:TT], M, M, t1)
            b = bank()
            t2 = mm(b, [(PS[b][:, 0:256], [(C("rot"), X[:, 0:256])])], t1)
            t3 = tt(tmps[0][:, 0:256], PS[b][:, 0:256], C("sin"), M, t2)
            bank_free[b] = t3
            t3 = tt(X[:, 0:256], X[:, 0:256], C("cos"), M, t2)
            t_qk = tt(X[:, 0:256], X[:, 0:256], tmps[0][:, 0:256], AD, t3)

        for i in range(4):
            for j in range(31):
                w = V(f"conv_w{l}", 31 * i + j)
                for_s = gp[:, i, 0:len(streams_q), j:j + 256]
                o = y[:, i, 0:Tq].rearrange("p (s t) -> p s t", t=256)
                if j == 0:
                    t_y = ts(o, for_s, w, V(f"conv_b{l}", i), M, AD, t_g)
                else:
                    t_y = stt(o, for_s, w, o, M, AD, t_y)

        lay_a = Lay(lay.at)
        t_in = [t_qk, t_vt]
        t_o = attend(q, kk, vtok, lambda i: OT[:, i, 0:256], lay_a, [[0, 1, 2, 3]] * 2, 0, None, None, t_in)
        if not last:
            lay_a = Lay(lay.at)
            pr.phase(("pe", "act", "dve"))
            t_o = attend(q, kk, vtok, lambda i: OT[:, i, 256:512], lay_a, [[2, 3]] * 2, 256, None, None, t_in)

        b = bank()
        t = mm(b, [(PS[b][:, 0:Tq], [(C("ones"), y[:, k, 0:Tq]) for k in range(4)])], t_y)
        mu = tmps[0][:, 0:Tq]
        t = ts(mu, PS[b][:, 0:Tq], 1.0 / 512, None, M, None, t)
        bank_free[b] = t
        for k in range(4):
            t1 = tt(y[:, k, 0:Tq], y[:, k, 0:Tq], mu, SU, t)
        t = inverse_root(lambda k: y[:, k, 0:Tq], 4, Tq, lambda k: sq4[:, k, 0:Tq], rstd[:, 0:Tq], 512, 1, t1)
        for k in range(4):
            t1 = stt(y[:, k, 0:Tq], y[:, k, 0:Tq], V(f"ln_g{l}", k), rstd[:, 0:Tq], M, M, t)
            t_c = act(OT[:, 4 + k, 0:Tq], y[:, k, 0:Tq], ACT.Silu, t1, bias=V(f"ln_b{l}", k))
        t = merged(OT, Tq, lambda h, k: V(f"beta_attn{l}" if h == 0 else f"beta_conv{l}", k), sq4, rstd, [t_o, t_c])

        for c in range(2):
            p = weight(A["w_o"][l], 512 * c, 512)
            for i in range(4):
                m = 4 * c + i
                b = bank()
                t1 = mm(b, [(PS[b][:, 0:Tq], [(p.w[:, k, 128 * i:128 * i + 128], OT[:, k, 0:Tq])
                                              for k in range(8)])], t, p.here)
                p.release = t1
                for s, (a, z) in streams_q:
                    t2 = stt(XT[:, m, a:z], PS[b][:, a:z], MOD[l][:, 16 + m, s:s + 1], XT[:, m, a:z], M, AD, t1)
                bank_free[b] = t2
        pr.phase()
        return t2

    s_wst = [pr.new_sem(f"s_wst{i}") for i in range(2)]
    s_wrd = [pr.new_sem(f"s_wrd{i}") for i in range(2)]
    scratch_read = [None]

    def peer(l):
        T = 256 if l == 1 else 512
        nt = T // 128
        streams = BOTH[:1] if l == 1 else BOTH
        lay = Lay()
        iT = lay.take(3 * 512).rearrange("p (c t) -> p c t", c=3)
        rstd = lay.take(512)
        base = lay.at
        qT = lay.take(4096).rearrange("p (k t) -> p k t", k=8)
        SW = [lay.take(256) for _ in range(2)]
        TS_ = lay.take(256).rearrange("p (h r) -> p h r", r=16)
        TI = lay.take(256).bitcast(U32).rearrange("p (h r) -> p h r", r=16)
        TIf = lay.take(256).rearrange("p (h r) -> p h r", r=16)
        cand = lay.take(2048)
        BS, BJ, R1, R2, R1f, R2f, I1, I2, WW = (lay.take(128) for _ in range(9))
        eq = lay.take(2048)
        mxs = lay.take(8)
        sm = lay.take(8)
        OH = lay.take(8 * 256).rearrange("p (q c j) -> p q c j", q=8, c=2)
        stage = [ACC.rearrange("p k t -> p (k t)"), lay.take(4096)]

        t = modulated(streams, T, lambda k, s: MOD[l][:, 32 + k, s:s + 1], lambda k, s: MOD[l][:, 24 + k, s:s + 1], rstd)
        for c in range(2):
            p = weight(A["peer_wq"][l], 512 * c, 512)
            for i in range(4):
                b = bank()
                t1 = mm(b, [(PS[b][:, 0:T], [(p.w[:, k, 128 * i:128 * i + 128], HT[:, k, 0:T]) for k in range(8)])],
                        t, p.here)
                p.release = t1
                t_q = cp(qT[:, 4 * c + i, 0:T], PS[b][:, 0:T], t1, e="act")
                bank_free[b] = t_q
        pk = Piece(A["keysT"][l], 1024)
        keys = lay.take(1024).rearrange("p (h k) -> p h k", h=8)
        t_keys = cp(keys, pk.ap.rearrange("p (h k) -> p h k", h=8), pk.here, e="act")
        pk.release = t_keys

        stage_free = [None, None]
        t_stored = []
        oh_free = [None, None]
        quad = 0
        n_st = 0
        for tt_ in range(nt):
            for h4 in range(4):
                b = bank()
                parts = []
                for j in range(4):
                    h, c = 4 * (h4 // 2) + j, h4 % 2
                    parts.append((PS[b][:, 128 * j:128 * j + 128],
                                  [(qT[64 * c:64 * c + 64, h, 128 * tt_:128 * tt_ + 128], keys[64 * c:64 * c + 64, h, :])]))
                t = mm(b, parts, t_q, t_keys)
                for j in range(4):
                    hc = 2 * (4 * (h4 // 2) + j) + h4 % 2
                    S = PS[b][:, 128 * j:128 * j + 128]
                    W_ = SW[j % 2][:, 0:128]
                    a8, b8 = TS_[:, hc, 0:8], TS_[:, hc, 8:16]
                    t = pr.put("dve", lambda g, o=a8, S=S: g.max(o, S), t, pr.last("dve"))
                    t = pr.put("dve", lambda g, o=TI[:, hc, 0:8], m=a8, S=S: g.max_index(o, m, S), t)
                    t = pr.put("dve", lambda g, o=W_, m=a8, S=S: g.match_replace(o, m, S, -3.0e38), t)
                    t = pr.put("dve", lambda g, o=b8, S=W_: g.max(o, S), t)
                    t = pr.put("dve", lambda g, o=TI[:, hc, 8:16], m=b8, S=W_: g.max_index(o, m, S), t)
                bank_free[b] = t
            t = cp(TIf, TI, t)
            tsv = TS_.rearrange("p (h c) r -> p h c r", c=2)
            tiv = TIf.rearrange("p (h c) r -> p h c r", c=2)
            cv = cand.rearrange("p (h a b) -> p h a b", h=8, a=16)
            t = tt(cv, tsv[:, :, 0, :].unsqueeze(3).to_broadcast([128, 8, 16, 16]),
                   tsv[:, :, 1, :].unsqueeze(2).to_broadcast([128, 8, 16, 16]), AD, t)
            bs = BS.rearrange("p (h r) -> p h r", r=16)
            bj = BJ.bitcast(U32).rearrange("p (h r) -> p h r", r=16)
            for h in range(8):
                S = cand[:, 256 * h:256 * h + 256]
                W_ = SW[h % 2]
                t = pr.put("dve", lambda g, o=bs[:, h, 0:8], S=S: g.max(o, S), t)
                t = pr.put("dve", lambda g, o=bj[:, h, 0:8], m=bs[:, h, 0:8], S=S: g.max_index(o, m, S), t)
                t = pr.put("dve", lambda g, o=W_, m=bs[:, h, 0:8], S=S: g.match_replace(o, m, S, -3.0e38), t)
                t = pr.put("dve", lambda g, o=bs[:, h, 8:16], S=W_: g.max(o, S), t)
                t = pr.put("dve", lambda g, o=bj[:, h, 8:16], m=bs[:, h, 8:16], S=W_: g.max_index(o, m, S), t)
            t1 = ts(R1.bitcast(U32), BJ.bitcast(U32), 4, None, ALU.logical_shift_right, None, t)
            t2 = ts(R2.bitcast(U32), BJ.bitcast(U32), 15, None, ALU.bitwise_and, None, t)
            t1 = cp(R1f, R1.bitcast(U32), t1)
            t2 = cp(R2f, R2.bitcast(U32), t2)
            t3 = cp(mxs, bs[:, :, 0], t)
            ww = WW.rearrange("p (h r) -> p h r", r=16)
            t3 = tt(ww, bs, mxs.unsqueeze(2).to_broadcast([128, 8, 16]), SU, t3, pr.last("pe"))
            t_e = act(WW, WW, ACT.Exp, t3)
            for c, (Rf, I) in enumerate(((R1f, I1), (R2f, I2))):
                ev = eq.rearrange("p (j r) -> p j r", r=16)
                t4 = tt(ev, Rf.unsqueeze(2).to_broadcast([128, 128, 16]),
                        C("iota")[:, 0:16].unsqueeze(1).to_broadcast([128, 128, 16]), ALU.is_equal, t2, pr.last("dve"))
                e4 = eq.rearrange("p (h k r) -> p h k r", h=8, k=16)
                t4 = tt(e4, e4, tiv[:, :, c, :].unsqueeze(2).to_broadcast([128, 8, 16, 16]), M, t4)
                t4 = pr.put("dve", lambda g, I=I, ev=ev: g.tensor_reduce(I, ev, AX.X, ALU.add), t4)
            t5 = pr.put("dve", lambda g: g.tensor_reduce(sm, ww, AX.X, ALU.add), t_e)
            t5 = pr.put("dve", lambda g: g.reciprocal(sm, sm), t5)
            t5 = tt(ww, ww, sm.unsqueeze(2).to_broadcast([128, 8, 16]), M, t5)
            b = bank()
            t = tp(b, [(PS[b][:, 128 * j:128 * j + 128], X) for j, X in enumerate((I1, I2, WW))], t5)
            t_i = cp(iT[:, :, 128 * tt_:128 * tt_ + 128], PS[b][:, 0:384].rearrange("p (c t) -> p c t", c=3), t)
            bank_free[b] = t_i
            some(3)
            for tb in range(4):
                st = stage[n_st % 2]
                sv = st.rearrange("p (a t) -> p a t", t=32)
                for qd in range(8):
                    half = quad % 2
                    for j in range(4):
                        tok = 128 * tt_ + 32 * tb + 4 * qd + j
                        o2, o1 = OH[:, 4 * half + j, 0, :], OH[:, 4 * half + j, 1, :]
                        ts(o2, C("iota"), iT[:, 1, tok:tok + 1], None, ALU.is_equal, None, t_i, oh_free[half])
                        t = ts(o1, C("iota"), iT[:, 0, tok:tok + 1], iT[:, 2, tok:tok + 1], ALU.is_equal, M)
                    b = bank()
                    t = mm(b, [(PS[b][:, 128 * j:128 * j + 128], [(OH[:, 4 * half + j, 0, :], OH[:, 4 * half + j, 1, :])])
                               for j in range(4)], t)
                    oh_free[half] = t
                    quad += 1
                    t = cp(sv[:, :, 4 * qd:4 * qd + 4], PS[b][:, :].rearrange("p (t a) -> p a t", t=4), t,
                           stage_free[n_st % 2], e="act")
                    bank_free[b] = t
                tbn = 4 * tt_ + tb
                t = pr.dma("act", s_wst[n_st % 2], scratch[:, :, tbn, :].rearrange("g b x -> b g x"),
                           st.rearrange("p (g x) -> p g x", g=32), t, scratch_read[0])
                stage_free[n_st % 2] = t
                t_stored.append(t)
                n_st += 1
                some(1)
        some(100)
        pr.phase()
        now = [stage_free[0], stage_free[1]]

        lay = Lay(base)
        WG = [lay.take(2048) for _ in range(2)]
        AG = [lay.take(2048).rearrange("p (a t) -> p a t", a=4) for _ in range(2)]
        G = [lay.take(512) for _ in range(2)]
        ntb = T // 32
        w_read = [now, now]
        a_free = [now, now]
        g_free = [now, now]
        t_w, t_a, vp = {}, {}, {}
        t_h = pr.last("dve")
        prev = None
        for g in range(33):
            if g < 32:
                half = g % 2
                t_w[g] = pr.dma("pool", s_wrd[half], WG[half][:, 0:4 * T].rearrange("p (b x) -> p b x", x=128),
                                scratch[g, :, 0:ntb, :], w_read[half], t_stored)
                scratch_read[0] = t_w[g]
                up = Piece(A["peer_uT"][l, g], 4096)
                uv = up.ap.rearrange("p (a k e) -> p a k e", a=4, k=8)
                wv = WG[half][:, 0:4 * T].rearrange("p (b a t) -> p a b t", a=4, t=32)
                for a in range(4):
                    b = bank()
                    t = mm(b, [(PS[b][:, 0:T], [(uv[:, a, k, :], HT[:, k, 0:T]) for k in range(8)])], up.here, t_h)
                    gg = G[a % 2][:, 0:T]
                    t = act(gg, PS[b][:, 0:T], ACT.Gelu, t, g_free[a % 2])
                    bank_free[b] = t
                    t = tt(AG[half][:, a, 0:T].rearrange("p (b t) -> p b t", t=32),
                           gg.rearrange("p (b t) -> p b t", t=32), wv[:, a], M, t, t_w[g], a_free[half])
                    g_free[a % 2] = t
                up.release = pr.last("pe")
                t_a[g] = t
                w_read[half] = t
                v = Piece(A["peer_v"][l].rearrange("(g a b) d -> g b a d", g=32, a=4)[g], 4096)
                v.w = v.ap.rearrange("p (a d) -> p a d", a=4)
                vp[g] = v
            if g >= 1:
                gq = g - 1
                half = gq % 2
                v = vp[gq]
                for m in range(8):
                    b = bank()
                    t = mm(b, [(PS[b][:, 0:T], [(v.w[:, a, 128 * m:128 * m + 128], AG[half][:, a, 0:T])
                                                for a in range(4)])], v.here, t_a[gq])
                    if gq == 0:
                        t_acc = cp(ACC[:, m, 0:T], PS[b][:, 0:T], t, now)
                    else:
                        t_acc = tt(ACC[:, m, 0:T], ACC[:, m, 0:T], PS[b][:, 0:T], AD, t, prev)
                    bank_free[b] = t_acc
                prev = t_acc
                v.release = t
                a_free[half] = t
        for m in range(8):
            for s, (a, z) in streams:
                t = stt(XT[:, m, a:z], ACC[:, m, a:z], MOD[l][:, 40 + m, s:s + 1], XT[:, m, a:z], M, AD, t_acc)
        pr.phase()
        return t

    mod_ready = [[], []]
    ada_ready = []
    later.append((mod_layer(0), mod_ready[0]))
    some(100)

    def plus_one(l):
        t = None
        for a in (8, 32):
            t = ts(MOD[l][:, a:a + 8, :], MOD[l][:, a:a + 8, :], 1.0, None, AD, None, mod_ready[l][0])
        mod_ready[l][0] = t
        pr.held["dve"] = [pr.held.get("dve"), t]

    plus_one(0)
    later.append((mod_layer(1), mod_ready[1]))
    later.append((ada_layer(), ada_ready))
    mixer(0)
    peer(0)
    plus_one(1)
    mixer(1)
    peer(1)

    t_ada = ada_ready[0]
    for j in (1, 4, 7):
        t_ada = ts(ADA[:, 8 * j:8 * j + 8], ADA[:, 8 * j:8 * j + 8], 1.0, None, AD, None, t_ada)
    pr.held["dve"] = [pr.held.get("dve"), t_ada]
    lay = Lay()
    rstd = lay.take(256)
    t = inverse_root(lambda k: XT[:, k, 0:256], 8, 256, lambda k: ACC[:, k, 0:256], rstd, 1024, 0, pr.last("dve"))
    for k in range(8):
        t = stt(XT[:, k, 0:256], XT[:, k, 0:256], V("final_g", k), rstd, M, M, t)

    def add_normed(src, gain, gate, factor, rstd, t_in):
        t = inverse_root(lambda k: src[:, k, 0:256], 8, 256, lambda k: HT[:, k, 0:256], rstd, 1024, 0, t_in,
                         pr.last("pe"))
        if factor != 1.0:
            t = ts(rstd, rstd, factor, None, M, None, t)
        for k in range(8):
            t1 = stt(src[:, k, 0:256], src[:, k, 0:256], V(gain, k), rstd, M, M, t)
            t2 = stt(XT[:, k, 0:256], src[:, k, 0:256], ADA[:, 8 * gate + k:8 * gate + k + 1], XT[:, k, 0:256],
                     M, AD, t1)
        pr.phase()
        return t2

    X1 = [(0, (0, 256))]

    def feed_forward(n, j0):
        lay = Lay()
        rstd = lay.take(256)
        F = lay.take(22 * 256).rearrange("p (m t) -> p m t", m=22)
        sg = [lay.take(256) for _ in range(2)]
        t_h = modulated(X1, 256, lambda k, s: ADA[:, 8 * (j0 + 1) + k:8 * (j0 + 1) + k + 1],
                        lambda k, s: ADA[:, 8 * j0 + k:8 * j0 + k + 1], rstd, gain=lambda k: V(f"pre{n}", k))
        for c in range(6):
            cols = 512 if c < 5 else 256
            pg = weight(A[f"w{n}_gate"], 512 * c, cols)
            pu = weight(A[f"w{n}_up"], 512 * c, cols)
            for i in range(cols // 128):
                m = 4 * c + i
                b = bank()
                t = mm(b, [(PS[b][:, 256 * s:256 * s + 256],
                            [(p.w[:, k, 128 * i:128 * i + 128], HT[:, k, 0:256]) for k in range(8)])
                           for s, p in enumerate((pg, pu))], t_h, pg.here, pu.here)
                pg.release = pu.release = t
                t1 = act(sg[m % 2], PS[b][:, 0:256], ACT.Silu, t, pr.last("dve"))
                t_f = tt(F[:, m, :], sg[m % 2], PS[b][:, 256:512], M, t1)
                bank_free[b] = t_f
        for m in range(8):
            p = weight(A[f"w{n}_down"], 128 * m, 128)
            b = bank()
            t = mm(b, [(PS[b][:, 0:256], [(p.w[:, k, :], F[:, k, :]) for k in range(22)])], t_f, p.here)
            p.release = t
            t = cp(ACC[:, m, 0:256], PS[b][:, 0:256], t, e="act")
            bank_free[b] = t
        return add_normed(ACC, f"post{n}", j0 + 2, 0.5, rstd, t)

    feed_forward(1, 0)

    lay = Lay()
    rstd = lay.take(256)
    q = lay.take(1024).rearrange("p (k t) -> p k t", k=4)
    kk = lay.take(256)
    vT = lay.take(256)
    vtok = lay.take(256).rearrange("p (c d) -> p c d", c=2)
    uT = lay.take(1024).rearrange("p (k t) -> p k t", k=4)
    OT = lay.take(2048).rearrange("p (k t) -> p k t", k=8)
    base = lay.at
    t_h = modulated(X1, 256, lambda k, s: ADA[:, 32 + k:33 + k], lambda k, s: ADA[:, 24 + k:25 + k], rstd,
                    gain=lambda k: V("prem", k))
    for c in range(3):
        cols = 512 if c < 2 else 256
        p = weight(A["w_in2"], 512 * c, cols)
        for i in range(cols // 128):
            m = 4 * c + i
            b = bank()
            t = mm(b, [(PS[b][:, 0:256], [(p.w[:, k, 128 * i:128 * i + 128], HT[:, k, 0:256]) for k in range(8)])],
                   t_h, p.here)
            p.release = t
            o = q[:, m, :] if m < 4 else kk if m == 4 else vT if m == 5 else uT[:, m - 6, :]
            t_p = cp(o, PS[b][:, 0:256], t, e="act")
            bank_free[b] = t_p
    b = bank()
    t = tp(b, [(PS[b][:, 128 * c:128 * c + 128], vT[:, 128 * c:128 * c + 128]) for c in range(2)], t_p)
    t_vt = cp(vtok, PS[b][:, 0:256].rearrange("p (c d) -> p c d", c=2), t, e="act")
    bank_free[b] = t_vt
    pb = Piece(A["alibi"], 2048)
    al = pb.ap.rearrange("p (h k) -> p h k", h=8)
    lay = Lay(base)
    pr.wait("dve", pb.here)
    t_o = attend(q, kk, vtok, lambda i: OT[:, i, :], lay, [[0], [0, 1]], 0,
                 lambda h: V("sinks", h), lambda h, qt, N: al[:, h, 256 - N:256], [t_p, t_vt])
    pb.release = pr.last("dve")
    pr.phase()

    lay = Lay(base)
    EC = lay.take(4096).rearrange("p (i t) -> p i t", i=16)
    ES = lay.take(4096).rearrange("p (i t) -> p i t", i=16)
    keep = lay.at
    T1 = HT[:, 0:4, :].rearrange("p k t -> p (k t)")
    T2 = HT[:, 4:8, :].rearrange("p k t -> p (k t)")
    names = ["dt", "rr", "th", "kf", "fr", "er", "lr", "li", "a", "b", "n", "cr", "ci", "x", "y"]
    s16 = {n: lay.take(16) for n in names}
    ki = lay.take(16).bitcast(mybir.dt.int32)
    BT = [lay.take(512).rearrange("p (c m) -> p c m", c=4) for _ in range(2)]
    CB = [lay.take(512).rearrange("p (i h) -> p i h", i=16) for _ in range(2)]
    BB = [lay.take(512).rearrange("p (i h) -> p i h", i=16) for _ in range(2)]
    tmpb = [lay.take(256).rearrange("p (i h) -> p i h", i=16) for _ in range(2)]
    pbc = Piece(A["ssm_bc"], 1024)
    bc = pbc.ap.rearrange("p (n i h) -> p n i h", n=4, i=16)
    D = lambda: pr.last("dve")
    g = s16
    t = act(g["dt"], V("log_step"), ACT.Exp)
    t = tt(g["x"], V("a_re"), g["dt"], M, t)
    t = act(g["rr"], g["x"], ACT.Exp, t)
    t_r = t
    t = tt(g["th"], V("a_im"), g["dt"], M, t)
    HI, MID, LO = 6.28125, 0.0019350051879882812, 3.019916e-07
    t = ts(g["y"], g["th"], 1.0 / TWO_PI, None, M, None, t)
    t = ts(g["kf"], g["y"], 12582912.0, -12582912.0, AD, AD, t)
    t = stt(g["fr"], g["kf"], -HI, g["th"], M, AD, t)
    t = stt(g["fr"], g["kf"], -MID, g["fr"], M, AD, t)
    t = stt(g["fr"], g["kf"], -LO, g["fr"], M, AD, t)
    t = ts(g["fr"], g["fr"], 3.1415925, -3.1415925, ALU.min, ALU.max, t)
    t_s = act(g["li"], g["fr"], ACT.Sin, t)
    t = ts(g["y"], g["fr"], -1.0, None, M, None, t)
    t = tt(g["y"], g["y"], g["fr"], ALU.max, t)
    t = ts(g["y"], g["y"], -1.0, 1.5707963267948966, M, AD, t)
    t = act(g["lr"], g["y"], ACT.Sin, t)
    t = cp(EC[:, :, 0], g["lr"], t, t_s)
    t = cp(ES[:, :, 0], g["li"], t)
    t = tt(g["lr"], g["lr"], g["rr"], M, t, t_r)
    t = tt(g["li"], g["li"], g["rr"], M, t)
    t = ts(g["lr"], g["lr"], -1.0, None, AD, None, t)
    t = tt(g["a"], V("a_re"), V("a_re"), M, t)
    t = tt(g["b"], V("a_im"), V("a_im"), M, t)
    t = tt(g["n"], g["a"], g["b"], AD, t)
    t = pr.put("dve", lambda e: e.reciprocal(g["n"], g["n"]), t)
    t = tt(g["a"], g["lr"], V("a_re"), M, t)
    t = tt(g["b"], g["li"], V("a_im"), M, t)
    t = tt(g["cr"], g["a"], g["b"], AD, t)
    t = tt(g["cr"], g["cr"], g["n"], M, t)
    t = tt(g["a"], g["li"], V("a_re"), M, t)
    t = tt(g["b"], g["lr"], V("a_im"), M, t)
    t = tt(g["ci"], g["a"], g["b"], SU, t)
    t = tt(g["ci"], g["ci"], g["n"], M, t)
    cr = g["cr"].unsqueeze(2).to_broadcast([128, 16, 16])
    ci = g["ci"].unsqueeze(2).to_broadcast([128, 16, 16])
    for X in BB + CB:
        t = pr.put("dve", lambda e, X=X: e.memset(X, 0.0), t)

    def blocks(dst, src, t, scale=None):
        for s in range(2):
            t0 = ts(dst[64 * s:64 * s + 64, :, 16 * s:16 * s + 16], src[64 * s:64 * s + 64], scale or 1.0, None, M, None, t)
        return t0

    t = tt(tmpb[0], bc[:, 0], cr, M, t, pbc.here)
    t = tt(tmpb[1], bc[:, 1], ci, M, t)
    t = tt(tmpb[0], tmpb[0], tmpb[1], SU, t)
    t = blocks(BB[0], tmpb[0], t)
    t = tt(tmpb[0], bc[:, 1], cr, M, t)
    t = tt(tmpb[1], bc[:, 0], ci, M, t)
    t = tt(tmpb[0], tmpb[0], tmpb[1], AD, t)
    t = blocks(BB[1], tmpb[0], t)
    t = blocks(CB[0], bc[:, 2], t)
    t = blocks(CB[1], bc[:, 3], t, -1.0)
    pbc.release = t
    for s in range(2):
        b = bank()
        t1 = tp(b, [(PS[b][:, 128 * c:128 * c + 128], BB[s][:, 4 * c:4 * c + 4, :].rearrange("p i h -> p (i h)"))
                    for c in range(4)], t)
        t1 = cp(BT[s], PS[b][:, :].rearrange("p (c m) -> p c m", c=4), t1, e="act")
        bank_free[b] = t1
    t_bt = t1
    n = 1
    t = D()
    while n < 256:
        cN = EC[:, :, n - 1:n].to_broadcast([128, 16, n])
        sN = ES[:, :, n - 1:n].to_broadcast([128, 16, n])
        c0, s0 = EC[:, :, 0:n], ES[:, :, 0:n]
        c1, s1 = EC[:, :, n:2 * n], ES[:, :, n:2 * n]
        a = T1[:, 0:16 * n].rearrange("p (i t) -> p i t", i=16)
        bb = T2[:, 0:16 * n].rearrange("p (i t) -> p i t", i=16)
        t1 = tt(a, s0, sN, M, t)
        t2 = tt(bb, s0, cN, M, t)
        t3 = tt(c1, c0, cN, M, t)
        t4 = tt(s1, c0, sN, M, t)
        tt(c1, c1, a, SU, t3)
        t = tt(s1, s1, bb, AD, t4)
        n *= 2
    pr.held["dve"] = [pr.held.get("dve"), t]
    t_e = t
    lay2 = Lay(lay.at)
    ZA = [lay2.take(512).rearrange("p (s t) -> p s t", s=2) for _ in range(2)]
    ZB = [lay2.take(512).rearrange("p (s t) -> p s t", s=2) for _ in range(2)]
    ZS = [T1[:, 512 * i:512 * i + 512].rearrange("p (s t) -> p s t", s=2) for i in range(2)]
    XS = [T2[:, 512 * i:512 * i + 512].rearrange("p (s t) -> p s t", s=2) for i in range(2)]
    yT = T1[:, 1024:2048].rearrange("p (k t) -> p k t", k=4)
    xs_free = [None, None]
    yb = [bank(), bank()]
    kept.update(yb)
    y_waits = [bank_free[yb[0]], bank_free[yb[1]]]
    for i in range(16):
        ch, lo = i // 4, 32 * (i % 4)
        z = i % 2
        b = bank()
        t = mm(b, [(PS[b][:, 256 * s:256 * s + 256], [(BT[s][lo:lo + 32, ch, :], uT[lo:lo + 32, ch, :])])
                   for s in range(2)], t_bt)
        bu = PS[b][:, :].rearrange("p (s t) -> p s t", s=2)
        cB = EC[:, i:i + 1, :].to_broadcast([128, 2, 256])
        a, bb_, zs, xs = ZA[z], ZB[z], ZS[z], XS[z]
        t1 = tt(a, bu, cB, M, t, D())
        for s in range(2):
            t2 = tt(bb_[:, s, :], bu[:, 1 - s, :], ES[:, i, :], M, t)
        bank_free[b] = t2
        tt(a[:, 0, :], a[:, 0, :], bb_[:, 0, :], AD, t2)
        t2 = tt(a[:, 1, :], a[:, 1, :], bb_[:, 1, :], SU, t2)
        rb = g["rr"][:, i:i + 1].to_broadcast([128, 256])
        for s in range(2):
            t3 = pr.put("dve", lambda e, o=zs[:, s, :], d=a[:, s, :], rb=rb: e.tensor_tensor_scan(o, rb, d, 0.0, M, AD), t2)
        t4 = tt(a, zs, cB, M, t3)
        for s in range(2):
            t4 = tt(bb_[:, s, :], zs[:, 1 - s, :], ES[:, i, :], M, t3)
        tt(xs[:, 0, :], a[:, 0, :], bb_[:, 0, :], SU, t4, xs_free[z])
        t5 = tt(xs[:, 1, :], a[:, 1, :], bb_[:, 1, :], AD, t4)
        o = PS[yb[ch // 2]][lo:lo + 32, 256 * (ch % 2):256 * (ch % 2) + 256]
        t6 = pr.put("pe", lambda e, o=o, i=i, xs=xs: (e.matmul(o, CB[0][:, i, :], xs[:, 0, :], start=True, stop=False),
                                                     e.matmul(o, CB[1][:, i, :], xs[:, 1, :], start=False, stop=True))[1],
                    t5, y_waits)
        xs_free[z] = t6
    for ch in range(4):
        t = stt(yT[:, ch, :], uT[:, ch, :], V("ssm_d", ch), PS[yb[ch // 2]][:, 256 * (ch % 2):256 * (ch % 2) + 256],
                M, AD, t6, D())
        bank_free[yb[ch // 2]] = t
        t_y = act(yT[:, ch, :], yT[:, ch, :], ACT.Gelu_apprx_tanh, t)
    kept.clear()
    p = weight(A["w_glu"], 0, 512)
    for m in range(4):
        b = bank()
        t = mm(b, [(PS[b][:, 0:256], [(p.w[:, k, 128 * m:128 * m + 128], yT[:, k, :]) for k in range(4)])], t_y, p.here)
        sg = ZA[m % 2][:, 0, :]
        t = act(sg, PS[b][:, 0:256], ACT.Sigmoid, t, D(), bias=V("b_glu", m))
        bank_free[b] = t
        t_m = tt(OT[:, 4 + m, :], yT[:, m, :], sg, M, t)
    p.release = pr.last("pe")
    t = merged(OT, 256, lambda h, k: V("g_attn" if h == 0 else "g_ssm", k), ACC, rstd, t_m)
    for c in range(2):
        p = weight(A["w_out"], 512 * c, 512)
        for i in range(4):
            m = 4 * c + i
            b = bank()
            t1 = mm(b, [(PS[b][:, 0:256], [(p.w[:, k, 128 * i:128 * i + 128], OT[:, k, :]) for k in range(8)])], t,
                    p.here)
            p.release = t1
            t2 = cp(ACC[:, m, 0:256], PS[b][:, 0:256], t1, pr.last("pe"), e="act")
            bank_free[b] = t2
    add_normed(ACC, "postm", 5, 1.0, rstd, t2)
    t = feed_forward(2, 6)
    s_out = pr.new_sem("s_out")
    t = pr.dma("act", s_out, out.rearrange("(k p) t -> p k t", p=128), XT[:, :, 0:256], t)
    pr.wait("act", t)

    for p in pieces:
        prev = pieces[p.n - RING].release if p.n >= RING else None
        assert p.n < RING or prev is not None, p.n
        dst = p.ap
        if len(p.src.shape) == 3:
            dst = dst.rearrange("p (k m) -> p k m", k=p.src.shape[1])
        got = pr.dma("sp", slot_sem[p.slot], dst, p.src, prev)
        assert got == p.here

    block = ctx.enter_context(nc.Block())

    @block.sync
    def _(eng):
        pr.emit("sp", eng)

    @block.tensor
    def _(eng):
        pr.emit("pe", eng)

    @block.scalar
    def _(eng):
        pr.emit("act", eng)

    @block.vector
    def _(eng):
        pr.emit("dve", eng)

    @block.gpsimd
    def _(eng):
        pr.emit("pool", eng)


def constants():
    con = np.zeros((128, CON["n"]), np.float32)

    def put(name, a):
        o, w = CON[name]
        con[:, o:o + w] = a

    put("ones", np.ones((128, 128)))
    p = np.arange(128)
    put("blk", (p[:, None] // 64 == p[None, :] // 64))
    put("ident", np.eye(128))
    rot = np.zeros((128, 128), np.float32)
    for m in range(128):
        if m % 64 < 32:
            rot[m + 32, m] = -1.0
        else:
            rot[m - 32, m] = 1.0
    put("rot", rot)
    n = 16
    inv = np.float32(10000.0) ** (-np.arange(n, dtype=np.float32) / np.float32(n))
    tok = np.arange(256)
    ang = np.concatenate([(tok // 64).astype(np.float32)[:, None] * inv, (tok % 64).astype(np.float32)[:, None] * inv], 1)
    cos, sin = np.cos(ang).astype(np.float32), np.sin(ang).astype(np.float32)
    put("cos", cos.T[p % 32])
    put("sin", sin.T[p % 32])
    put("iota", np.arange(128)[None, :])
    put("eps", np.array([[1e-6, 1e-5]]))
    al = np.zeros((128, 8, 256), np.float32)
    dist = np.arange(128)[:, None] + 128 - np.arange(256)[None, :]
    for h in range(8):
        al[:, h] = np.where((dist >= 0) & (dist < 128), -(2.0 ** (-(h + 1))) * dist, -1e30)
    return con, al.reshape(128, 2048)


def kernel(**inputs):
    import concourse.bacc as bacc
    from concourse.bass_utils import run_bass_kernel_spmd

    I = {k: np.asarray(v) for k, v in inputs.items()}

    def cols(v):
        return v.reshape(-1, 128).T

    def heads(v):
        return v.reshape((2, 4, 64) + v.shape[1:]).swapaxes(0, 1).reshape(v.shape)

    parts = []
    for l in range(2):
        parts += [cols(I["b_mod"][l]), np.concatenate([I["q_gain"][l]] * 2)[:, None],
                  np.concatenate([I["k_gain"][l]] * 2)[:, None],
                  I["conv_w"][l].reshape(31, 4, 128).transpose(2, 1, 0).reshape(128, 124),
                  cols(I["conv_b"][l]), cols(I["ln_g"][l]), cols(I["ln_b"][l]), cols(heads(I["beta_attn"][l])),
                  cols(I["beta_conv"][l])]
    st = lambda a: a.reshape(16, 128).T
    ls = np.broadcast_to(I["ssm_log_step_2"][0][:, None], (32, 64))
    parts += [cols(I["c"][0]), cols(I["c_ctx"]), cols(I["c_2"][0]), cols(I["final_g"]), cols(I["b_ada_2"][0]),
              cols(I["g_pre_ff1_2"][0]), cols(I["g_post_ff1_2"][0]), cols(I["g_pre_mix_2"][0]),
              cols(I["g_post_mix_2"][0]), cols(I["g_pre_ff2_2"][0]), cols(I["g_post_ff2_2"][0]),
              cols(I["ssm_d_2"][0]), cols(I["ssm_b_glu_2"][0]), cols(heads(I["g_attn_out_2"][0])),
              cols(I["g_ssm_out_2"][0]), st(I["ssm_a_re_2"][0]), st(I["ssm_a_im_2"][0]), st(ls),
              np.broadcast_to(I["attn_sinks_2"], (128, 8))]
    con, al = constants()

    def in_cols(w):
        return np.concatenate([w[:, 0:512].reshape(-1, 2, 4, 64).swapaxes(1, 2).reshape(-1, 512), w[:, 512:]], 1)

    def out_rows(w):
        return np.concatenate([heads(w[0:512]), w[512:]], 0)

    bsel = lambda a: a.reshape(16, 2, 64, 16).transpose(1, 2, 0, 3).reshape(128, 256)
    csel = lambda a: a.reshape(16, 2, 16, 64).transpose(1, 3, 0, 2).reshape(128, 256)
    arrays = {
        "vec": np.concatenate(parts, 1), "con": con, "alibi": al,
        "xT": np.concatenate([I["x"][0], I["ctx"][0]], 0).T,
        "w_mod": I["w_mod"], "w_ada": I["w_ada_2"][0],
        "w_in": np.stack([in_cols(w) for w in I["w_in"]]),
        "w_o": np.stack([out_rows(w) for w in I["w_o"]]),
        "peer_wq": I["peer_wq"],
        "keysT": I["peer_keys"].transpose(0, 2, 4, 1, 3).reshape(2, 128, 1024),
        "peer_uT": I["peer_u"].reshape(2, 32, 4, 128, 8, 128).transpose(0, 1, 5, 2, 4, 3).reshape(2, 32, 128, 4096),
        "peer_v": I["peer_v"],
        "w1_gate": I["w1_gate_2"][0], "w1_up": I["w1_up_2"][0], "w1_down": I["w1_down_2"][0],
        "w2_gate": I["w2_gate_2"][0], "w2_up": I["w2_up_2"][0], "w2_down": I["w2_down_2"][0],
        "w_in2": in_cols(I["w_in_2"][0]), "w_out": out_rows(I["w_out_2"][0]), "w_glu": I["ssm_w_glu_2"][0],
        "ssm_bc": np.concatenate([bsel(I["ssm_b_re_2"][0]), bsel(I["ssm_b_im_2"][0]),
                                  csel(I["ssm_c_re_2"][0]), csel(I["ssm_c_im_2"][0])], 1),
    }
    arrays = {k: np.ascontiguousarray(v) for k, v in arrays.items()}
    nc = bacc.Bacc("TRN2", target_bir_lowering=False, num_devices=1)
    A = {k: nc.dram_tensor(f"in_{k}", v.shape, mybir.dt.from_np(v.dtype), kind="ExternalInput").ap()
         for k, v in arrays.items()}
    out = nc.dram_tensor("out_T", (1024, 256), F32, kind="ExternalOutput").ap()
    build(nc, A, out)
    r = run_bass_kernel_spmd(nc, [{f"in_{k}": v for k, v in arrays.items()}], core_ids=[0])
    return np.ascontiguousarray(r.results[0]["out_T"].T)[None]
```

```python
from contextlib import ExitStack

import numpy as np

import concourse.bass as bass
from concourse import mybir

F32 = mybir.dt.float32
F32R = mybir.dt.float32r
U32 = mybir.dt.uint32
ALU = mybir.AluOpType
ACT = mybir.ActivationFunctionType
AX = mybir.AxisListType

RING = 4
SLOT = 2048
AREA = 16300
EPS = 1e-6
FILL_TOP = 2
FILL_W = 1
TWO_PI = 6.283185307179586

VEC = {}


def _layout():
    n = 0
    for l in range(2):
        for name, w in (("b_mod", 48), ("q_gain", 1), ("k_gain", 1), ("conv_w", 124), ("conv_b", 4),
                        ("ln_g", 4), ("ln_b", 4), ("beta_attn", 4), ("beta_conv", 4)):
            VEC[f"{name}{l}"] = (n, w)
            n += w
    for name, w in (("c", 8), ("c_ctx", 8), ("c2", 8), ("final_g", 8), ("b_ada", 72), ("pre1", 8), ("post1", 8),
                    ("prem", 8), ("postm", 8), ("pre2", 8), ("post2", 8), ("ssm_d", 4), ("b_glu", 4), ("g_attn", 4),
                    ("g_ssm", 4), ("a_re", 16), ("a_im", 16), ("log_step", 16), ("sinks", 8)):
        VEC[name] = (n, w)
        n += w
    VEC["n"] = n


_layout()

CON = {}


def _con_layout():
    n = 0
    for name, w in (("ones", 128), ("blk", 128), ("ident", 128), ("rot", 128), ("cos", 256), ("sin", 256),
                    ("iota", 128), ("eps", 2), ("sel", 2)):
        CON[name] = (n, w)
        n += w
    CON["n"] = n


_con_layout()


class Program:

    def __init__(self, nc, ctx):
        self.nc, self.ctx = nc, ctx
        self.queue = {e: [] for e in ("pe", "act", "dve", "pool", "sp")}
        self.count = {e: 0 for e in self.queue}
        self.sem = {e: ctx.enter_context(nc.semaphore(f"done_{e}")) for e in self.queue}
        self.seen = {e: {} for e in self.queue}
        self.held = {}

    def new_sem(self, name):
        self.sem[name] = self.ctx.enter_context(self.nc.semaphore(name))
        self.count[name] = 0
        return name

    def wait(self, e, waits):
        todo = [waits]
        while todo:
            w = todo.pop()
            if w is None:
                continue
            if isinstance(w, list):
                todo.extend(w)
                continue
            s, v = w
            if self.seen[e].get(s, 0) < v:
                self.seen[e][s] = v
                self.queue[e].append((s, v))

    def put(self, e, make, *waits):
        self.wait(e, list(waits) + [self.held.pop(e, None)])
        self.count[e] += 1
        self.queue[e].append((make, e, 1))
        return (e, self.count[e])

    def dma(self, e, sem, out, in_, *waits):
        self.wait(e, list(waits) + [self.held.pop(e, None)])
        self.count[sem] += 16
        self.queue[e].append((lambda eng: eng.dma_start(out, in_), sem, 16))
        return (sem, self.count[sem])

    def last(self, e):
        return (e, self.count[e])

    def phase(self, engines=("pe", "act", "dve")):
        now = [self.last(e) for e in engines]
        for e in list(engines) + ["pool"]:
            self.held[e] = [self.held.get(e), now]

    def emit(self, e, eng):
        for item in self.queue[e]:
            if len(item) == 2:
                eng.wait_ge(self.sem[item[0]], item[1])
            else:
                make, s, by = item
                make(eng).then_inc(self.sem[s], by)


def build(nc, A, out):
    with ExitStack() as ctx:
        _build(nc, ctx, A, out)


def _build(nc, ctx, A, out):
    pr = Program(nc, ctx)

    def sb(name, n):
        return ctx.enter_context(nc.sbuf_tensor(name, [128, n], F32))

    XT = sb("xT", 4096).rearrange("p (k t) -> p k t", k=8)
    fr = ctx.enter_context(nc.sbuf_tensor("fr", [128, 16384], F32R))
    HR = fr[:, 0:8192].rearrange("p (s k t) -> p s k t", s=2, k=8)
    SR = [fr[:, 8192 + 2048 * i:8192 + 2048 * i + 2048].rearrange("p (s n) -> p s n", s=2) for i in range(2)]
    AG = [fr[:, 12288 + 2048 * i:12288 + 2048 * i + 2048].rearrange("p (s a t) -> p s a t", s=2, a=2) for i in range(2)]
    ACC = sb("acc", 4096).rearrange("p (k t) -> p k t", k=8)
    con = sb("con", CON["n"])
    vec = sb("vec", VEC["n"])
    mods = sb("mods", 2 * 96 + 72)
    scs = sb("scs", 512)
    mrow = sb("mrow", 512)
    ringt = sb("ring", RING * SLOT)
    area = sb("area", AREA)
    PS = [ctx.enter_context(nc.psum_tensor(f"ps{i}", [128, 512], F32)) for i in range(8)]
    scratch = nc.dram_tensor("w_scratch", (16, 128, 32, 128), F32, kind="Internal").ap()
    gscratch = nc.dram_tensor("g_scratch", (128, 128, 512), F32, kind="Internal").ap()

    def C(name):
        o, w = CON[name]
        return con[:, o:o + w]

    def V(name, j=None, w=1):
        o, n = VEC[name]
        return vec[:, o:o + n] if j is None else vec[:, o + j:o + j + w]

    MOD = [mods[:, 96 * l:96 * l + 96].rearrange("p (m s) -> p m s", s=2) for l in range(2)]
    ADA = mods[:, 192:264]

    bank_free = [None] * 8
    bank_next = [0]
    kept = set()

    def bank():
        while bank_next[0] % 8 in kept:
            bank_next[0] += 1
        b = bank_next[0] % 8
        bank_next[0] += 1
        return b

    pieces = []

    class Piece:
        def __init__(self, src, n):
            self.n = len(pieces)
            self.src, self.size = src, n
            self.release = None
            self.slot = self.n % RING
            self.ap = ringt[:, self.slot * SLOT:self.slot * SLOT + n]
            self.here = (slot_sem[self.slot], 16 * (self.n // RING + 1))
            pieces.append(self)

    slot_sem = [pr.new_sem(f"slot{i}") for i in range(RING)]

    def weight(w, c0, cols):
        k = w.shape[0] // 128
        src = w.rearrange("(k p) m -> p k m", p=128)[:, :, c0:c0 + cols]
        p = Piece(src, k * cols)
        p.w = p.ap.rearrange("p (k m) -> p k m", k=k)
        return p

    def mm(b, parts, *waits, first=True):
        def make(eng):
            for o, pairs in parts:
                for n, (lhs, rhs) in enumerate(pairs):
                    ins = eng.matmul(o, lhs, rhs, start=(n == 0), stop=(n == len(pairs) - 1))
            return ins
        return pr.put("pe", make, bank_free[b] if first else None, *waits)

    def tp(b, parts, *waits):
        def make(eng):
            for o, i in parts:
                ins = eng.transpose(o, i, C("ident"))
            return ins
        return pr.put("pe", make, bank_free[b], *waits)

    def act(o, i, f, *waits, **kw):
        return pr.put("act", lambda e: e.activation(o, i, f, **kw), *waits)

    def tt(o, a, b, op, *waits, e="dve"):
        return pr.put(e, lambda g: g.tensor_tensor(o, a, b, op), *waits)

    def ts(o, a, s1, s2, op0, op1, *waits, e="dve"):
        if op1 is None:
            return pr.put(e, lambda g: g.tensor_scalar(o, a, s1, None, op0), *waits)
        return pr.put(e, lambda g: g.tensor_scalar(o, a, s1, s2, op0, op1), *waits)

    def stt(o, a, s, b, op0, op1, *waits):
        return pr.put("dve", lambda g: g.scalar_tensor_tensor(out=o, in0=a, scalar=s, in1=b, op0=op0, op1=op1), *waits)

    def cp(o, i, *waits, e="dve"):
        if e == "act":
            return pr.put(e, lambda g: g.copy(o, i), *waits)
        return pr.put(e, lambda g: g.tensor_copy(o, i), *waits)

    M, AD, SU = ALU.mult, ALU.add, ALU.subtract

    def two_parts(hi, lo, x, *waits):
        t = cp(hi, x, *waits, e="act")
        return tt(lo, x, hi.bitcast(F32), SU, t, *waits)

    slot_free = [None, None]
    slot_next = [0]

    def split(x, shape, *waits):
        i = slot_next[0] % 2
        slot_next[0] += 1
        t = two_parts(SR[i][:, 0, :], SR[i][:, 1, :], x, slot_free[i], *waits)
        v = [SR[i][:, s, :].rearrange("p (k m) -> p k m", k=shape) for s in range(2)]
        return i, v, t

    def three(lhs, rhs, terms):
        return [(lhs(a, k), rhs(b, k)) for k in terms for a, b in ((0, 0), (0, 1), (1, 0))]

    def project_all(w, order, T, t_in, take, lo=0, K=8):
        todo = []
        for c0 in order:
            cols = min(256, w.shape[1] - c0)
            todo.append((c0, cols))
        made = []

        def ahead():
            if todo:
                c0, cols = todo.pop(0)
                p = weight(w, c0, cols)
                for i in range(cols // 128):
                    made.append((c0 // 128 + i, p, i))

        pending = None
        while True:
            if not made:
                ahead()
            nxt = None
            if made:
                m, p, i = made.pop(0)
                x = p.w[:, :, 128 * i:128 * i + 128]
                sl = slot_next[0] % 2
                slot_next[0] += 1
                hi = SR[sl][:, 0, :].rearrange("p (k m) -> p k m", k=8)
                lw = SR[sl][:, 1, :].rearrange("p (k m) -> p k m", k=8)
                t = two_parts(hi, lw, x, slot_free[sl], p.here)
                p.release = [t, pr.last("act")]
                nxt = (m, sl, (hi, lw), t)
            if pending is not None:
                m, sl, v, t = pending
                b = bank()
                t = mm(b, [(PS[b][:, 0:T - lo], three(lambda a, k: v[a][:, k, :], lambda c, k: HR[:, c, k, lo:T],
                                                      range(8)))], t_in, t)
                slot_free[sl] = t
                take(m, b, t)
            if nxt is None:
                break
            pending = nxt

    class Lay:
        def __init__(self, base=0):
            self.at = base

        def take(self, n):
            v = area[:, self.at:self.at + n]
            self.at += n
            assert self.at <= AREA, self.at
            return v

    s_con, s_vec, s_x = pr.new_sem("s_con"), pr.new_sem("s_vec"), pr.new_sem("s_x")
    t_vec = pr.dma("act", s_vec, vec[:, :], A["vec"])
    t_con = pr.dma("act", s_con, con[:, :], A["con"])
    t_x = pr.dma("act", s_x, XT, A["xT"].rearrange("(k p) t -> p k t", p=128))
    SC = scs[:, 0:256].rearrange("p (k s) -> p k s", s=32)
    SC2 = scs[:, 256:512].rearrange("p (k s) -> p k s", s=32)
    t_z = pr.put("dve", lambda g: g.memset(scs[:, 0:512], 0.0))
    t_sc = act(SC[:, :, 0], V("c"), ACT.Silu, t_vec, t_z)
    t_sc = act(SC[:, :, 1], V("c_ctx"), ACT.Silu)
    t_sc = act(SC2[:, :, 0], V("c2"), ACT.Silu)
    row_free = [None, None]
    row_next = [0]

    def mod_vectors(w, c0, n, rhs, bias, dst, width, got):
        for j in range(n // 2):
            p = weight(w, 128 * c0 + 256 * j, 256)
            b = bank()

            def rows(eng, p=p, b=b):
                for i in range(2):
                    for q in range(4):
                        k = 2 * q + i
                        ins = eng.matmul(PS[b][32 * q:32 * q + 32, 0:256], rhs(k), p.w[:, k, :], start=(i == 0),
                                         stop=(i == 1))
                return ins
            t = pr.put("pe", rows, bank_free[b], p.here, t_sc)
            p.release = t
            r = row_next[0] % 2
            row_next[0] += 1
            mr = mrow[:, 256 * r:256 * r + 256]
            t = cp(mr, PS[b][:, 0:256], t, row_free[r], e="act")
            bank_free[b] = t
            yield
            b = bank()
            t = mm(b, [(PS[b][:, width * i:width * i + width], [(mr[:, 128 * i:128 * i + 128], C("sel")[:, 0:width])])
                       for i in range(2)], t, t_con)
            row_free[r] = t
            m = 2 * j
            o = PS[b][:, 0:2 * width]
            if width == 2:
                o = o.rearrange("p (m s) -> p m s", s=2)
            t = tt(dst[:, m:m + 2], o, bias[:, m:m + 2], AD, t, t_vec)
            bank_free[b] = t
        got.append(t)
        yield

    def mod_layer(l, c0, n, got):
        return mod_vectors(A["w_mod"][l], c0, n, lambda k: SC[:, k, :],
                           V(f"b_mod{l}", c0, n).unsqueeze(2).to_broadcast([128, n, 2]), MOD[l][:, c0:c0 + n, :], 2, got)

    def ada_layer(got):
        return mod_vectors(A["w_ada"], 0, 72, lambda k: SC2[:, k, :], V("b_ada"), ADA, 1, got)

    later = []

    def some(n):
        while n > 0 and later:
            if next(later[0], "end") == "end":
                later.pop(0)
                continue
            n -= 1

    def inverse_root(src, chunks, T, sq, rstd, n, eps_col, *waits, lhs="ones"):
        ts_sq = []
        for k in range(chunks):
            ts_sq.append(act(sq(k), src(k), ACT.Square, *waits))
        b = bank()
        t = mm(b, [(PS[b][:, 0:T], [(C(lhs), sq(k)) for k in range(chunks)])], ts_sq[-1], t_con)
        t = act(rstd, PS[b][:, 0:T], ACT.Sqrt, t, pr.last("dve"), scale=1.0 / n, bias=C("eps")[:, eps_col:eps_col + 1])
        bank_free[b] = t
        return pr.put("dve", lambda g: g.reciprocal(rstd, rstd), t)

    def add1(v):
        return ts(v, v, 1.0, None, AD, None, pr.last("dve"))

    def modulated(streams, T, mult_of, add_of, rstd, *waits, gain=None):
        t = inverse_root(lambda k: XT[:, k, 0:T], 8, T, lambda k: ACC[:, k, 0:T], rstd[:, 0:T], 1024, 0,
                         t_x, pr.last("dve"), pr.last("pe"))
        t_pe = pr.last("pe")
        done = []
        for k in range(8):
            h = ACC[:, k, 0:T]
            if gain is None:
                t1 = tt(h, XT[:, k, 0:T], rstd[:, 0:T], M, t, t_pe)
            else:
                t1 = stt(h, XT[:, k, 0:T], gain(k), rstd[:, 0:T], M, M, t, t_pe)
            done.append(t1)
        for k in range(8):
            for s, (a, z) in streams:
                done[k] = ts(ACC[:, k, a:z], ACC[:, k, a:z], mult_of(k, s), add_of(k, s), M, AD, done[k], *waits)
        for k in range(8):
            t2 = two_parts(HR[:, 0, k, 0:T], HR[:, 1, k, 0:T], ACC[:, k, 0:T], done[k])
        return t2

    BOTH = [(0, (0, 256)), (1, (256, 512))]

    def attend(q, kT, vtok, dest, lay, tiles, q0, sinks, bias, t_in, side=lambda: None):
        P2 = [lay.take(512) for _ in range(2)]
        PT2 = [lay.take(1024).rearrange("p (c q) -> p c q", c=4) for _ in range(2)]
        st = lay.take(64)
        n = 0
        p_free = [None, None]
        pt_free = [None, None]
        nq = len(tiles)
        for i in range(4):
            bo = bank()
            kept.add(bo)
            t_o = []
            for kv in range(2):
                base = 64 * kv
                PT = PT2[kv]
                t_pt = []
                for qt, keys in enumerate(tiles):
                    N = 128 * len(keys)
                    k0 = 128 * keys[0]
                    b = bank()
                    t = mm(b, [(PS[b][:, 0:N], [(q[base:base + 64, i, q0 + 128 * qt:q0 + 128 * qt + 128],
                                                 kT[base:base + 64, k0:k0 + N])])], t_in)
                    S = PS[b][:, 0:N]
                    P = P2[n % 2][:, 0:N]
                    c = 8 * (n % 4)
                    mx, nb, den, rec, es = (st[:, c + j:c + j + 1] for j in range(5))
                    if bias is None:
                        t = pr.put("dve", lambda g, mx=mx, S=S: g.tensor_reduce(mx, S, AX.X, ALU.max), t)
                        t = ts(nb, mx, -0.125, None, M, None, t)
                        t = act(P, S, ACT.Exp, t, p_free[n % 2], scale=0.125, bias=nb, accum_out=den)
                        bank_free[b] = t
                    else:
                        h = i + 4 * kv
                        t = stt(P, S, 0.125, bias(h, qt, N), M, AD, t, p_free[n % 2])
                        bank_free[b] = t
                        t = pr.put("dve", lambda g, mx=mx, P=P: g.tensor_reduce(mx, P, AX.X, ALU.max), t)
                        t = ts(nb, mx, sinks(h), -1.0, ALU.max, M, t)
                        t2 = act(P, P, ACT.Exp, t, bias=nb, accum_out=den)
                        t3 = act(es, sinks(h), ACT.Exp, t, bias=nb)
                        t = tt(den, den, es, AD, t2, t3)
                    t = pr.put("dve", lambda g, rec=rec, den=den: g.reciprocal(rec, den), t)
                    t = ts(P, P, rec, None, M, None, t)
                    b = bank()
                    t = tp(b, [(PS[b][:, 128 * j:128 * j + 128], P[:, 128 * j:128 * j + 128])
                               for j in range(len(keys))], t, t_con)
                    p_free[n % 2] = t
                    o = PT[:, 0:len(keys), 128 * qt:128 * qt + 128]
                    t = cp(o, PS[b][:, 0:N].rearrange("p (c q) -> p c q", q=128), t, pt_free[kv], e="act")
                    bank_free[b] = t
                    t_pt.append(t)
                    n += 1
                    side()
                if all(len(k) == len(tiles[0]) for k in tiles):
                    parts = [(PS[bo][base:base + 64, 0:128 * nq],
                              [(vtok[:, kc, base:base + 64], PT[:, j, 0:128 * nq]) for j, kc in enumerate(tiles[0])])]
                else:
                    parts = [(PS[bo][base:base + 64, 128 * qt:128 * qt + 128],
                              [(vtok[:, kc, base:base + 64], PT[:, j, 128 * qt:128 * qt + 128])
                               for j, kc in enumerate(keys)]) for qt, keys in enumerate(tiles)]
                t = mm(bo, parts, t_pt)
                pt_free[kv] = t
                t_o.append(t)
            t = cp(dest(i), PS[bo][:, 0:128 * nq], t_o)
            bank_free[bo] = t
            kept.discard(bo)
        return t

    def merged(parts_of, T, beta, sq, rstd, t_ins):
        for half in range(2):
            t = inverse_root(lambda k: parts_of(half, k), 4, T, lambda k: sq[:, 4 * half + k, 0:T],
                             rstd[:, 0:T], 512, 0, t_ins[half], pr.last("pe"))
            ds = []
            for k in range(4):
                o = parts_of(half, k)
                ds.append(stt(o, o, beta(half, k), rstd[:, 0:T], M, M, t))
            for k in range(4):
                t = two_parts(HR[:, 0, 4 * half + k, 0:T], HR[:, 1, 4 * half + k, 0:T], parts_of(half, k), ds[k])
        return t

    def mixer(l):
        last = l == 1
        T = 512
        Tq = 256 if last else 512
        streams_q = BOTH[:1] if last else BOTH
        lay = Lay()
        q = lay.take(2048).rearrange("p (k t) -> p k t", k=4)
        kk = lay.take(512)
        vT = lay.take(512)
        vtok = lay.take(512).rearrange("p (c d) -> p c d", c=4)
        gp = lay.take(4 * 2 * 286).rearrange("p (c s t) -> p c s t", c=4, s=2)
        y = lay.take(2048).rearrange("p (k t) -> p k t", k=4)
        OT = lay.take(2048).rearrange("p (k t) -> p k t", k=4)
        rstd = lay.take(512)
        tmps = [lay.take(512) for _ in range(4)]
        t = modulated(BOTH, 512, lambda k, s: MOD[l][:, 8 + k, s:s + 1], lambda k, s: MOD[l][:, k, s:s + 1], rstd,
                      mod1[l])
        t_h = [t]
        W = A["w_in"][l]
        t_ms = pr.put("pool", lambda g: g.memset(gp, 0.0))

        got = {}

        def take_qk(m, b, t):
            o = q[:, m, 0:Tq] if m < 4 else kk[:, :] if m == 4 else vT[:, :]
            t = cp(o, PS[b][:, 0:Tq if m < 4 else 512], t, e="act")
            bank_free[b] = t
            got[m] = t

        project_all(W, [0, 256], Tq, t_h, take_qk)
        project_all(W, [512], 512, t_h, take_qk)
        t_q, t_v = got[3], got[5]
        b = bank()
        t = tp(b, [(PS[b][:, 128 * c:128 * c + 128], vT[:, 128 * c:128 * c + 128]) for c in range(4)], t_v)
        t_vt = cp(vtok, PS[b][:, :].rearrange("p (c d) -> p c d", c=4), t, e="act")
        bank_free[b] = t_vt

        sgs = {}

        def take_u(m, b, t):
            if m >= 10:
                sg = tmps[m % 2][:, 0:Tq]
                t = act(sg, PS[b][:, 0:Tq], ACT.Sigmoid, t, sgs.get(("free", m % 2)))
                sgs[m - 10] = (sg, t)
                bank_free[b] = t
            else:
                i = m - 6
                sg, t1 = sgs[i]
                for s, (a, z) in streams_q:
                    got["g"] = tt(gp[:, i, s, 15:271], PS[b][:, a:z], sg[:, a:z], M, t, t1, t_ms)
                sgs[("free", m % 2)] = got["g"]
                bank_free[b] = got["g"]

        project_all(W, [1280, 768, 1536, 1024], Tq, t_h, take_u)
        t_g = got["g"]

        for i in range(5):
            X = q[:, i, 0:Tq] if i < 4 else kk[:, :]
            TT = Tq if i < 4 else 512
            gain = V(f"q_gain{l}" if i < 4 else f"k_gain{l}")
            t1 = act(tmps[2][:, 0:TT], X, ACT.Square, pr.last("pe"))
            b = bank()
            t1 = mm(b, [(PS[b][:, 0:TT], [(C("blk"), tmps[2][:, 0:TT])])], t1)
            t1 = act(tmps[3][:, 0:TT], PS[b][:, 0:TT], ACT.Sqrt, t1, pr.last("dve"), scale=1.0 / 64, bias=C("eps")[:, 0:1])
            bank_free[b] = t1
            t1 = pr.put("dve", lambda g, TT=TT: g.reciprocal(tmps[3][:, 0:TT], tmps[3][:, 0:TT]), t1)
            t1 = stt(X, X, gain, tmps[3][:, 0:TT], M, M, t1)
            b = bank()
            t2 = mm(b, [(PS[b][:, 0:256], [(C("rot"), X[:, 0:256])])], t1)
            t3 = tt(tmps[0][:, 0:256], PS[b][:, 0:256], C("sin"), M, t2)
            bank_free[b] = t3
            t3 = tt(X[:, 0:256], X[:, 0:256], C("cos"), M, t2)
            t_qk = tt(X[:, 0:256], X[:, 0:256], tmps[0][:, 0:256], AD, t3)

        t_conv = {}

        def taps():
            for j in range(31):
                for i in range(4):
                    w = V(f"conv_w{l}", 31 * i + j)
                    for_s = gp[:, i, 0:len(streams_q), j:j + 256]
                    o = y[:, i, 0:Tq].rearrange("p (s t) -> p s t", t=256)
                    if j == 0:
                        t_conv[i] = ts(o, for_s, w, V(f"conv_b{l}", i), M, AD, t_g)
                    else:
                        t_conv[i] = stt(o, for_s, w, o, M, AD, t_conv[i])
                    yield

        tap = taps()

        def side(n=4 if not last else 8):
            for _ in range(n):
                next(tap, None)
            some(2)

        lay_a = Lay(lay.at)
        t_in = [t_qk, t_vt]
        t_o = attend(q, kk, vtok, lambda i: OT[:, i, 0:256], lay_a, [[0, 1, 2, 3]] * 2, 0, None, None, t_in, side)
        if not last:
            lay_a = Lay(lay.at)
            pr.phase(("pe", "act", "dve"))
            t_o = attend(q, kk, vtok, lambda i: OT[:, i, 256:512], lay_a, [[2, 3]] * 2, 256, None, None, t_in, side)

        for _ in tap:
            pass
        t_y = list(t_conv.values())

        b = bank()
        t = mm(b, [(PS[b][:, 0:Tq], [(C("ones"), y[:, k, 0:Tq]) for k in range(4)])], t_y)
        mu = tmps[0][:, 0:Tq]
        t = ts(mu, PS[b][:, 0:Tq], 1.0 / 512, None, M, None, t)
        bank_free[b] = t
        for k in range(4):
            t1 = tt(y[:, k, 0:Tq], y[:, k, 0:Tq], mu, SU, t)
        t = inverse_root(lambda k: y[:, k, 0:Tq], 4, Tq, lambda k: ACC[:, k, 0:Tq], rstd[:, 0:Tq], 512, 1, t1)
        for k in range(4):
            t1 = stt(y[:, k, 0:Tq], y[:, k, 0:Tq], V(f"ln_g{l}", k), rstd[:, 0:Tq], M, M, t)
            t_c = act(y[:, k, 0:Tq], y[:, k, 0:Tq], ACT.Silu, t1, bias=V(f"ln_b{l}", k))
        t = merged(lambda h, k: (OT if h == 0 else y)[:, k, 0:Tq], Tq,
                   lambda h, k: V(f"beta_attn{l}" if h == 0 else f"beta_conv{l}", k), ACC, rstd, [t_o, t_c])

        def take_o(m, b, t):
            for s, (a, z) in streams_q:
                t2 = stt(XT[:, m, a:z], PS[b][:, a:z], MOD[l][:, 16 + m, s:s + 1], XT[:, m, a:z], M, AD, t, mod2[l])
            bank_free[b] = t2

        project_all(A["w_o"][l], [0, 256, 512, 768], Tq, t, take_o)
        pr.phase()

    s_wst = [pr.new_sem(f"s_wst{i}") for i in range(2)]
    s_wrd = [pr.new_sem(f"s_wrd{i}") for i in range(2)]
    scratch_read = [None]

    s_gst = [pr.new_sem(f"s_gst{i}") for i in range(2)]
    s_grd = [pr.new_sem(f"s_grd{i}") for i in range(2)]

    def peer(l):
        T = 256 if l == 1 else 512
        nt = T // 128
        streams = BOTH[:1] if l == 1 else BOTH
        lay = Lay()
        GS = [lay.take(512) for _ in range(2)]
        rstd = lay.take(512)
        base = lay.at
        iT = lay.take(3 * 512).rearrange("p (c t) -> p c t", c=3)
        qT = lay.take(4096).rearrange("p (k t) -> p k t", k=8)
        SW = [lay.take(256) for _ in range(4)]
        TS_ = lay.take(256).rearrange("p (h r) -> p h r", r=16)
        TI = lay.take(256).bitcast(U32).rearrange("p (h r) -> p h r", r=16)
        TIf = lay.take(256).rearrange("p (h r) -> p h r", r=16)
        cand = lay.take(1024)
        BS, BJ, R1, R2, R1f, R2f, I1, I2, WW = (lay.take(128) for _ in range(9))
        eq = lay.take(1024)
        mxs = lay.take(8)
        sm = lay.take(8)
        OH = lay.take(8 * 256).rearrange("p (h c q j) -> p h c q j", h=2, c=2, q=4)
        stage = [ACC[:, 4 * i:4 * i + 4, :].rearrange("p k t -> p (k t)") for i in range(2)]
        keys = lay.take(1024).rearrange("p (h k) -> p h k", h=8)

        t_h = modulated(streams, T, lambda k, s: MOD[l][:, 32 + k, s:s + 1], lambda k, s: MOD[l][:, 24 + k, s:s + 1],
                        rstd, mod2[l])
        got = {}

        def take_q(m, b, t):
            t = cp(qT[:, m, 0:T], PS[b][:, 0:T], t, e="act")
            bank_free[b] = t
            got["q"] = t

        some(100)
        project_all(A["peer_wq"][l], [0, 256, 512, 768], T, t_h, take_q)
        t_q = got["q"]
        pk = Piece(A["keysT"][l], 1024)
        t_keys = cp(keys, pk.ap.rearrange("p (h k) -> p h k", h=8), pk.here, e="act")
        pk.release = t_keys

        u_piece = {}
        u_made = {}

        def u_split(a):
            if a % 2 == 0:
                u_piece[a // 2] = Piece(A["peer_uT"][l, a // 2], 2048)
            p = u_piece[a // 2]
            u_made[a] = split(p.ap[:, 1024 * (a % 2):1024 * (a % 2) + 1024], 8, p.here)
            p.release = [u_made[a][2], pr.last("act")]

        def u_product(a, steps):
            i, v, t = u_made.pop(a)
            b = bank()
            kept.add(b)
            pairs = three(lambda s, k: v[s][:, k, :], lambda s, k: HR[:, s, k, 0:T], range(8))
            per = -(-len(pairs) // steps)
            for n in range(0, len(pairs), per):
                def make(eng, n=n):
                    for m in range(n, min(n + per, len(pairs))):
                        ins = eng.matmul(PS[b][:, 0:T], pairs[m][0], pairs[m][1], start=(m == 0),
                                         stop=(m == len(pairs) - 1))
                    return ins
                t = pr.put("pe", make, t, t_h, bank_free[b])
                yield None
            kept.discard(b)
            slot_free[i] = t
            yield (b, t)

        spilled = {}
        gs_free = [None, None]

        def spill(a, b, t):
            g = GS[a % 2][:, 0:T]
            t = act(g, PS[b][:, 0:T], ACT.Gelu, t, gs_free[a % 2])
            bank_free[b] = t
            spilled[a] = gs_free[a % 2] = pr.dma("pool", s_gst[a % 2], gscratch[a, :, 0:T], g, t)

        def early():
            u_split(0)
            a = 0
            while a in u_made:
                if a < 125 and not ending:
                    u_split(a + 1)
                for got_ in u_product(a, 4):
                    if got_ is None:
                        yield
                b, t = got_
                spill(a, b, t)
                a += 1
                yield
            while True:
                yield

        ending = []
        filling = early()

        def fill(n):
            for _ in range(n):
                next(filling)

        stage_free = [None, None]
        t_stored = []
        oh_free = [None, None]
        quad = 0
        n_st = 0
        tsv = TS_.rearrange("p (h c) r -> p h c r", c=2)
        tiv = TIf.rearrange("p (h c) r -> p h c r", c=2)

        def best16(sets):
            def each(f, waits):
                return [pr.put("dve", f(*x), w) for x, w in zip(sets, waits)]
            w0 = [x[4] for x in sets]
            t = each(lambda S, W, v, i, _: lambda g: g.max(v[:, 0:8], S), w0)
            t1 = each(lambda S, W, v, i, _: lambda g: g.match_replace(W, v[:, 0:8], S, -3.0e38), t)
            t = each(lambda S, W, v, i, _: lambda g: g.max_index(i[:, 0:8], v[:, 0:8], S), t)
            t2 = each(lambda S, W, v, i, _: lambda g: g.max(v[:, 8:16], W), t1)
            return each(lambda S, W, v, i, _: lambda g: g.max_index(i[:, 8:16], v[:, 8:16], W), t2)

        for tt_ in range(nt):
            for h4 in range(4):
                b = bank()
                parts = []
                for j in range(4):
                    h, c = 4 * (h4 // 2) + j, h4 % 2
                    parts.append((PS[b][:, 128 * j:128 * j + 128],
                                  [(qT[64 * c:64 * c + 64, h, 128 * tt_:128 * tt_ + 128], keys[64 * c:64 * c + 64, h, :])]))
                t = mm(b, parts, t_q, t_keys)
                sets = []
                for j in range(4):
                    hc = 2 * (4 * (h4 // 2) + j) + h4 % 2
                    sets.append((PS[b][:, 128 * j:128 * j + 128], SW[j][:, 0:128], TS_[:, hc, :], TI[:, hc, :],
                                 [t, pr.last("dve")]))
                t = best16(sets)
                bank_free[b] = t
                fill(FILL_TOP)
            t = cp(TIf, TI, t)
            bs = BS.rearrange("p (h r) -> p h r", r=16)
            bj = BJ.bitcast(U32).rearrange("p (h r) -> p h r", r=16)
            for h0 in (0, 4):
                cv = cand.rearrange("p (h a b) -> p h a b", h=4, a=16)
                t = tt(cv, tsv[:, h0:h0 + 4, 0, :].unsqueeze(3).to_broadcast([128, 4, 16, 16]),
                       tsv[:, h0:h0 + 4, 1, :].unsqueeze(2).to_broadcast([128, 4, 16, 16]), AD, t, pr.last("dve"))
                t = best16([(cand[:, 256 * j:256 * j + 256], SW[j], bs[:, h0 + j, :], bj[:, h0 + j, :], t)
                            for j in range(4)])
                fill(FILL_TOP)
            t1 = ts(R1.bitcast(U32), BJ.bitcast(U32), 4, None, ALU.logical_shift_right, None, t)
            t2 = ts(R2.bitcast(U32), BJ.bitcast(U32), 15, None, ALU.bitwise_and, None, t)
            t3 = cp(mxs, bs[:, :, 0], t)
            t1 = cp(R1f, R1.bitcast(U32), t1)
            t2 = cp(R2f, R2.bitcast(U32), t2)
            ww = WW.rearrange("p (h r) -> p h r", r=16)
            t3 = tt(ww, bs, mxs.unsqueeze(2).to_broadcast([128, 8, 16]), SU, t3, pr.last("pe"))
            t_e = act(WW, WW, ACT.Exp, t3)
            for c, (Rf, I) in enumerate(((R1f, I1), (R2f, I2))):
                for h0 in (0, 4):
                    ev = eq.rearrange("p (j r) -> p j r", r=16)
                    t4 = tt(ev, Rf[:, 16 * h0:16 * h0 + 64].unsqueeze(2).to_broadcast([128, 64, 16]),
                            C("iota")[:, 0:16].unsqueeze(1).to_broadcast([128, 64, 16]), ALU.is_equal, t1, t2,
                            pr.last("dve"))
                    e4 = eq.rearrange("p (h k r) -> p h k r", h=4, k=16)
                    t4 = tt(e4, e4, tiv[:, h0:h0 + 4, c, :].unsqueeze(2).to_broadcast([128, 4, 16, 16]), M, t4)
                    t4 = pr.put("dve", lambda g, I=I, ev=ev, h0=h0: g.tensor_reduce(I[:, 16 * h0:16 * h0 + 64], ev,
                                                                                   AX.X, ALU.add), t4)
            t5 = pr.put("dve", lambda g: g.tensor_reduce(sm, ww, AX.X, ALU.add), t_e)
            t5 = pr.put("dve", lambda g: g.reciprocal(sm, sm), t5)
            t5 = tt(ww, ww, sm.unsqueeze(2).to_broadcast([128, 8, 16]), M, t5)
            b = bank()
            t = tp(b, [(PS[b][:, 128 * j:128 * j + 128], X) for j, X in enumerate((I1, I2, WW))], t5)
            t_i = cp(iT[:, :, 128 * tt_:128 * tt_ + 128], PS[b][:, 0:384].rearrange("p (c t) -> p c t", c=3), t)
            bank_free[b] = t_i
            fill(FILL_TOP)
            for tb in range(8):
                st = stage[n_st % 2]
                sv = st.rearrange("p (a t) -> p a t", t=16)
                for qd in range(4):
                    half = quad % 2
                    tok = 128 * tt_ + 16 * tb + 4 * qd
                    tt(OH[:, half, 0], C("iota").unsqueeze(1).to_broadcast([128, 4, 128]),
                       iT[:, 1, tok:tok + 4].unsqueeze(2).to_broadcast([128, 4, 128]), ALU.is_equal, t_i, oh_free[half])
                    for j in range(4):
                        t = ts(OH[:, half, 1, j, :], C("iota"), iT[:, 0, tok + j:tok + j + 1],
                               iT[:, 2, tok + j:tok + j + 1], ALU.is_equal, M)
                    b = bank()
                    t = mm(b, [(PS[b][:, 128 * j:128 * j + 128], [(OH[:, half, 0, j, :], OH[:, half, 1, j, :])])
                               for j in range(4)], t)
                    oh_free[half] = t
                    quad += 1
                    t = cp(sv[:, :, 4 * qd:4 * qd + 4], PS[b][:, :].rearrange("p (t a) -> p a t", t=4), t,
                           stage_free[n_st % 2], t_h, e="act")
                    bank_free[b] = t
                    fill(FILL_W)
                tbn = 8 * tt_ + tb
                t = pr.dma("pool", s_wst[n_st % 2], scratch[:, :, tbn, :].rearrange("g b x -> b g x"),
                           st.rearrange("p (g x) -> p g x", g=16), t, scratch_read[0])
                stage_free[n_st % 2] = t
                t_stored.append(t)
                n_st += 1
        ending.append(True)
        while u_made or kept:
            fill(1)
        if len(spilled) % 2:
            u_split(len(spilled))
            for got_ in u_product(len(spilled), 1):
                pass
            spill(len(spilled), *got_)
        na = len(spilled)
        pr.phase()
        now = [stage_free[0], stage_free[1]]

        lay = Lay(base)
        WG = [lay.take(4096) for _ in range(2)]
        GL = [lay.take(1024).rearrange("p (a t) -> p a t", a=2) for _ in range(2)]
        ntb = T // 16
        w_read = [now, now]
        a_free = [now, now]
        gl_free = [now, now]
        t_w, t_a, vp, t_gl = {}, {}, {}, {}
        yb = []
        if l == 1:
            yb = [bank() for _ in range(4)]
            kept.update(yb)
        t_acc = None

        def load_w(g8):
            if g8 < 16:
                t_w[g8] = pr.dma("pool", s_wrd[g8 % 2], WG[g8 % 2][:, 0:8 * T].rearrange("p (b x) -> p b x", x=128),
                                 scratch[g8, :, 0:ntb, :], w_read[g8 % 2], t_stored)
                scratch_read[0] = t_w[g8]

        def load_g(g):
            if 2 * g < na:
                n = min(2, na - 2 * g)
                t_gl[g] = pr.dma("pool", s_grd[g % 2], GL[g % 2][:, 0:n, 0:T],
                                 gscratch[2 * g:2 * g + n, :, 0:T].rearrange("a b t -> b a t"), gl_free[g % 2],
                                 [spilled[x] for x in range(2 * g, 2 * g + n)], pr.last("dve"))

        def weigh(a, b, t):
            g, j = a // 2, a % 2
            x = GL[g % 2][:, j, 0:T]
            if b is not None:
                t = act(x, PS[b][:, 0:T], ACT.Gelu, t, gl_free[g % 2])
                bank_free[b] = t
            wv = WG[(a // 8) % 2][:, 0:8 * T].rearrange("p (b a t) -> p a b t", a=8, t=16)[:, a % 8]
            t = tt(x.rearrange("p (b t) -> p b t", t=16), x.rearrange("p (b t) -> p b t", t=16), wv, M, t,
                   t_w[a // 8])
            w_read[(a // 8) % 2] = t
            t = two_parts(AG[g % 2][:, 0, j, 0:T], AG[g % 2][:, 1, j, 0:T], x, t, a_free[g % 2])
            t_a[a] = t
            gl_free[g % 2] = t

        units = []
        for g in range(65):
            if g < 64:
                for a in (2 * g, 2 * g + 1):
                    units.append(("u", a))
            if g >= 1:
                units += [("v", g - 1, 0), ("v", g - 1, 1)]

        def prepare(u):
            if u[0] == "u":
                if u[1] >= na and u[1] not in u_made:
                    u_split(u[1])
            else:
                g, mh = u[1], u[2]
                if mh == 0:
                    p = Piece(A["peer_v"][l].rearrange("(g a b) d -> g b a d", g=64, a=2)[g], 2048)
                    vp[g] = p
                p = vp[g]
                src = p.ap.rearrange("p (a d) -> p a d", a=2)[:, :, 512 * mh:512 * mh + 512]
                sl = slot_next[0] % 2
                slot_next[0] += 1
                v = [SR[sl][:, s, :].rearrange("p (a d) -> p a d", a=2) for s in range(2)]
                t = two_parts(v[0], v[1], src, slot_free[sl], p.here)
                p.release = [t, pr.last("act")]
                vp[(g, mh)] = (sl, v, t)

        load_w(0)
        load_w(1)
        load_g(0)
        load_g(1)
        work = [u for u in units if u[0] == "v" or u[1] >= na]
        loaded = iter(u for u in units)
        prepare(work[0])
        n = 0
        for u in units:
            if u[0] == "u" and u[1] < na:
                weigh(u[1], None, t_gl[u[1] // 2])
            else:
                if n + 1 < len(work):
                    prepare(work[n + 1])
                n += 1
            if u[0] == "u":
                a = u[1]
                if a >= na:
                    for got_ in u_product(a, 1):
                        pass
                    weigh(a, *got_)
                if a % 8 == 7:
                    load_w(a // 8 + 2)
                if a % 2 == 1 and a >= 3:
                    load_g(a // 2 + 1)
            else:
                g, mh = u[1], u[2]
                sl, v, tv = vp[(g, mh)]
                for mi in range(4):
                    m = 4 * mh + mi
                    pairs = three(lambda s, a: v[s][:, a, 128 * mi:128 * mi + 128],
                                  lambda s, a: AG[g % 2][:, s, a, 0:T], range(2))
                    if l == 1:
                        o = PS[yb[m // 2]][:, 256 * (m % 2):256 * (m % 2) + 256]

                        def make(eng, o=o, pairs=pairs, g=g, m=m):
                            for n_, (x, y_) in enumerate(pairs):
                                ins = eng.matmul(o, x, y_, start=(g == 0 and n_ == 0 and m % 2 == 0),
                                                 stop=(g == 63 and n_ == 5 and m % 2 == 1), skip_group_check=True)
                            return ins
                        t = pr.put("pe", make, tv, t_a[2 * g + 1], bank_free[yb[m // 2]] if g == 0 else None)
                    else:
                        b = bank()
                        t = mm(b, [(PS[b][:, 0:T], pairs)], tv, t_a[2 * g + 1])
                        if g == 0:
                            t_acc = cp(ACC[:, m, 0:T], PS[b][:, 0:T], t, now)
                        else:
                            t_acc = tt(ACC[:, m, 0:T], ACC[:, m, 0:T], PS[b][:, 0:T], AD, t)
                        bank_free[b] = t_acc
                slot_free[sl] = t
                a_free[g % 2] = t
        for m in range(8):
            for s, (a, z) in streams:
                src = PS[yb[m // 2]][:, 256 * (m % 2):256 * (m % 2) + 256] if l == 1 else ACC[:, m, a:z]
                t2 = stt(XT[:, m, a:z], src, MOD[l][:, 40 + m, s:s + 1], XT[:, m, a:z], M, AD,
                         t if l == 1 else t_acc)
        for b in yb:
            kept.discard(b)
            bank_free[b] = t2
        pr.phase()

    mod1, mod2, ada_ready = [[], []], [[], []], []

    def plus_one(l, a, got):
        got.append(ts(MOD[l][:, a:a + 8, :], MOD[l][:, a:a + 8, :], 1.0, None, AD, None, got[-1]))

    later.append(mod_layer(0, 0, 16, mod1[0]))
    some(100)
    plus_one(0, 8, mod1[0])
    later.append(mod_layer(0, 16, 32, mod2[0]))
    some(100)
    plus_one(0, 32, mod2[0])
    later.append(mod_layer(1, 0, 16, mod1[1]))
    later.append(mod_layer(1, 16, 32, mod2[1]))
    later.append(ada_layer(ada_ready))
    mixer(0)
    peer(0)
    plus_one(1, 8, mod1[1])
    plus_one(1, 32, mod2[1])
    mixer(1)
    peer(1)

    t_ada = ada_ready[-1]
    for j in (1, 4, 7):
        t_ada = ts(ADA[:, 8 * j:8 * j + 8], ADA[:, 8 * j:8 * j + 8], 1.0, None, AD, None, t_ada)
    pr.held["dve"] = [pr.held.get("dve"), t_ada]
    lay = Lay()
    rstd = lay.take(256)
    t = inverse_root(lambda k: XT[:, k, 0:256], 8, 256, lambda k: ACC[:, k, 0:256], rstd, 1024, 0, pr.last("dve"))
    for k in range(8):
        t = stt(XT[:, k, 0:256], XT[:, k, 0:256], V("final_g", k), rstd, M, M, t)

    sqb = area[:, AREA - 2048:AREA].rearrange("p (k t) -> p k t", k=8)

    def add_normed(src, gain, gate, factor, rstd, t_in):
        t = inverse_root(lambda k: src[:, k, 0:256], 8, 256, lambda k: sqb[:, k, :], rstd, 1024, 0, t_in,
                         pr.last("pe"))
        if factor != 1.0:
            t = ts(rstd, rstd, factor, None, M, None, t)
        for k in range(8):
            t1 = stt(src[:, k, 0:256], src[:, k, 0:256], V(gain, k), rstd, M, M, t)
            t2 = stt(XT[:, k, 0:256], src[:, k, 0:256], ADA[:, 8 * gate + k:8 * gate + k + 1], XT[:, k, 0:256],
                     M, AD, t1)
        pr.phase()
        return t2

    X1 = [(0, (0, 256))]

    def feed_forward(n, j0):
        lay = Lay()
        rstd = lay.take(256)
        F = lay.take(22 * 256).rearrange("p (m t) -> p m t", m=22)
        sg = [lay.take(256) for _ in range(2)]
        t_h = modulated(X1, 256, lambda k, s: ADA[:, 8 * (j0 + 1) + k:8 * (j0 + 1) + k + 1],
                        lambda k, s: ADA[:, 8 * j0 + k:8 * j0 + k + 1], rstd, gain=lambda k: V(f"pre{n}", k))
        wg, wu = A[f"w{n}_gate"], A[f"w{n}_up"]
        pend = []
        tf = [None]

        def finish(m, bg, tg, bu, tu):
            t1 = act(sg[m % 2], PS[bg][:, 0:256], ACT.Silu, tg, tf[0])
            bank_free[bg] = t1
            tf[0] = tt(F[:, m, :], sg[m % 2], PS[bu][:, 0:256], M, t1, tu)
            bank_free[bu] = tf[0]

        def take_gate(m, b, t):
            pend.append((m, b, t))

        def take_up(m, b, t):
            m_, bg, tg = pend.pop(0)
            assert m_ == m
            finish(m, bg, tg, b, t)

        seq = []
        for c in range(11):
            for w in (wg, wu):
                seq += [(w, c, 0), (w, c, 1)]
        cur = {}
        queued = None
        for item in seq + [None]:
            nxt = None
            if item is not None:
                w, c, i = item
                if i == 0:
                    cur["p"] = weight(w, 256 * c, 256)
                p = cur["p"]
                sl = slot_next[0] % 2
                slot_next[0] += 1
                v = [SR[sl][:, s_, :].rearrange("p (k m) -> p k m", k=8) for s_ in range(2)]
                t = two_parts(v[0], v[1], p.w[:, :, 128 * i:128 * i + 128], slot_free[sl], p.here)
                p.release = [t, pr.last("act")]
                nxt = (w is wg, 2 * c + i, sl, v, t)
            if queued is not None:
                is_gate, m, sl, v, t = queued
                b = bank()
                t = mm(b, [(PS[b][:, 0:256], three(lambda a, k: v[a][:, k, :], lambda c_, k: HR[:, c_, k, 0:256],
                                                   range(8)))], t_h, t)
                slot_free[sl] = t
                (take_gate if is_gate else take_up)(m, b, t)
            queued = nxt
        t_f = tf[0]
        for m in range(8):
            b = bank()
            for kh in range(2):
                src = A[f"w{n}_down"].rearrange("(k p) m -> p k m", p=128)[:, 11 * kh:11 * kh + 11,
                                                                            128 * m:128 * m + 128]
                p = Piece(src, 1408)
                p.w = p.ap.rearrange("p (k m) -> p k m", k=11)

                def make(eng, p=p, kh=kh, b=b):
                    for k in range(11):
                        ins = eng.matmul(PS[b][:, 0:256], p.w[:, k, :], F[:, 11 * kh + k, :],
                                         start=(kh == 0 and k == 0), stop=(kh == 1 and k == 10))
                    return ins
                t = pr.put("pe", make, t_f, p.here, bank_free[b])
                p.release = t
            t = cp(ACC[:, m, 0:256], PS[b][:, 0:256], t, e="act")
            bank_free[b] = t
        return add_normed(ACC, f"post{n}", j0 + 2, 0.5, rstd, t)

    feed_forward(1, 0)

    lay = Lay()
    rstd = lay.take(256)
    uT = lay.take(1024).rearrange("p (k t) -> p k t", k=4)
    OT = lay.take(2048).rearrange("p (k t) -> p k t", k=8)
    base = lay.at
    q = lay.take(1024).rearrange("p (k t) -> p k t", k=4)
    kk = lay.take(256)
    vT = lay.take(256)
    vtok = lay.take(256).rearrange("p (c d) -> p c d", c=2)
    base_a = lay.at
    t_h = modulated(X1, 256, lambda k, s: ADA[:, 32 + k:33 + k], lambda k, s: ADA[:, 24 + k:25 + k], rstd,
                    gain=lambda k: V("prem", k))
    got2 = {}

    def take_p(m, b, t):
        o = q[:, m, :] if m < 4 else kk if m == 4 else vT if m == 5 else uT[:, m - 6, :]
        got2["p"] = cp(o, PS[b][:, 0:256], t, e="act")
        bank_free[b] = got2["p"]

    project_all(A["w_in2"], [0, 256, 512, 768, 1024], 256, t_h, take_p)
    t_p = got2["p"]
    b = bank()
    t = tp(b, [(PS[b][:, 128 * c:128 * c + 128], vT[:, 128 * c:128 * c + 128]) for c in range(2)], t_p)
    t_vt = cp(vtok, PS[b][:, 0:256].rearrange("p (c d) -> p c d", c=2), t, e="act")
    bank_free[b] = t_vt
    pb = Piece(A["alibi"], 2048)
    al = pb.ap.rearrange("p (h k) -> p h k", h=8)
    lay = Lay(base_a)
    pr.wait("dve", pb.here)
    t_o = attend(q, kk, vtok, lambda i: OT[:, i, :], lay, [[0], [0, 1]], 0,
                 lambda h: V("sinks", h), lambda h, qt, N: al[:, h, 256 - N:256], [t_p, t_vt])
    pb.release = pr.last("dve")
    pr.phase()

    lay = Lay(base)
    EC = lay.take(4096).rearrange("p (i t) -> p i t", i=16)
    ES = lay.take(4096).rearrange("p (i t) -> p i t", i=16)
    keep = lay.at
    T1 = ACC[:, 0:4, :].rearrange("p k t -> p (k t)")
    T2 = ACC[:, 4:8, :].rearrange("p k t -> p (k t)")
    names = ["dt", "rr", "th", "kf", "fr", "er", "lr", "li", "a", "b", "n", "cr", "ci", "x", "y"]
    s16 = {n: lay.take(16) for n in names}
    ki = lay.take(16).bitcast(mybir.dt.int32)
    BT = [lay.take(512).rearrange("p (c m) -> p c m", c=4) for _ in range(2)]
    CB = [lay.take(512).rearrange("p (i h) -> p i h", i=16) for _ in range(2)]
    keep = lay.at
    BB = [lay.take(512).rearrange("p (i h) -> p i h", i=16) for _ in range(2)]
    tmpb = [lay.take(256).rearrange("p (i h) -> p i h", i=16) for _ in range(2)]
    pbc = Piece(A["ssm_bc"], 1024)
    bc = pbc.ap.rearrange("p (n i h) -> p n i h", n=4, i=16)
    D = lambda: pr.last("dve")
    g = s16
    t = act(g["dt"], V("log_step"), ACT.Exp)
    t = tt(g["x"], V("a_re"), g["dt"], M, t)
    t = act(g["rr"], g["x"], ACT.Exp, t)
    t_r = t
    t = tt(g["th"], V("a_im"), g["dt"], M, t)
    HI, MID, LO = 6.28125, 0.0019350051879882812, 3.019916e-07
    t = ts(g["y"], g["th"], 1.0 / TWO_PI, None, M, None, t)
    t = ts(g["kf"], g["y"], 12582912.0, -12582912.0, AD, AD, t)
    t = stt(g["fr"], g["kf"], -HI, g["th"], M, AD, t)
    t = stt(g["fr"], g["kf"], -MID, g["fr"], M, AD, t)
    t = stt(g["fr"], g["kf"], -LO, g["fr"], M, AD, t)
    t = ts(g["fr"], g["fr"], 3.1415925, -3.1415925, ALU.min, ALU.max, t)
    t_s = act(g["li"], g["fr"], ACT.Sin, t)
    t = ts(g["y"], g["fr"], -1.0, None, M, None, t)
    t = tt(g["y"], g["y"], g["fr"], ALU.max, t)
    t = ts(g["y"], g["y"], -1.0, 1.5707963267948966, M, AD, t)
    t = act(g["lr"], g["y"], ACT.Sin, t)
    t = cp(EC[:, :, 0], g["lr"], t, t_s)
    t = cp(ES[:, :, 0], g["li"], t)
    t = tt(g["lr"], g["lr"], g["rr"], M, t, t_r)
    t = tt(g["li"], g["li"], g["rr"], M, t)
    t = ts(g["lr"], g["lr"], -1.0, None, AD, None, t)
    t = tt(g["a"], V("a_re"), V("a_re"), M, t)
    t = tt(g["b"], V("a_im"), V("a_im"), M, t)
    t = tt(g["n"], g["a"], g["b"], AD, t)
    t = pr.put("dve", lambda e: e.reciprocal(g["n"], g["n"]), t)
    t = tt(g["a"], g["lr"], V("a_re"), M, t)
    t = tt(g["b"], g["li"], V("a_im"), M, t)
    t = tt(g["cr"], g["a"], g["b"], AD, t)
    t = tt(g["cr"], g["cr"], g["n"], M, t)
    t = tt(g["a"], g["li"], V("a_re"), M, t)
    t = tt(g["b"], g["lr"], V("a_im"), M, t)
    t = tt(g["ci"], g["a"], g["b"], SU, t)
    t = tt(g["ci"], g["ci"], g["n"], M, t)
    cr = g["cr"].unsqueeze(2).to_broadcast([128, 16, 16])
    ci = g["ci"].unsqueeze(2).to_broadcast([128, 16, 16])
    for X in BB + CB:
        t = pr.put("dve", lambda e, X=X: e.memset(X, 0.0), t)

    def blocks(dst, src, t, scale=None):
        for s in range(2):
            t0 = ts(dst[64 * s:64 * s + 64, :, 16 * s:16 * s + 16], src[64 * s:64 * s + 64], scale or 1.0, None, M, None, t)
        return t0

    t = tt(tmpb[0], bc[:, 0], cr, M, t, pbc.here)
    t = tt(tmpb[1], bc[:, 1], ci, M, t)
    t = tt(tmpb[0], tmpb[0], tmpb[1], SU, t)
    t = blocks(BB[0], tmpb[0], t)
    t = tt(tmpb[0], bc[:, 1], cr, M, t)
    t = tt(tmpb[1], bc[:, 0], ci, M, t)
    t = tt(tmpb[0], tmpb[0], tmpb[1], AD, t)
    t = blocks(BB[1], tmpb[0], t)
    t = blocks(CB[0], bc[:, 2], t)
    t = blocks(CB[1], bc[:, 3], t, -1.0)
    pbc.release = t
    for s in range(2):
        b = bank()
        t1 = tp(b, [(PS[b][:, 128 * c:128 * c + 128], BB[s][:, 4 * c:4 * c + 4, :].rearrange("p i h -> p (i h)"))
                    for c in range(4)], t)
        t1 = cp(BT[s], PS[b][:, :].rearrange("p (c m) -> p c m", c=4), t1, e="act")
        bank_free[b] = t1
    t_bt = t1
    n = 1
    t = D()
    while n < 256:
        cN = EC[:, :, n - 1:n].to_broadcast([128, 16, n])
        sN = ES[:, :, n - 1:n].to_broadcast([128, 16, n])
        c0, s0 = EC[:, :, 0:n], ES[:, :, 0:n]
        c1, s1 = EC[:, :, n:2 * n], ES[:, :, n:2 * n]
        a = T1[:, 0:16 * n].rearrange("p (i t) -> p i t", i=16)
        bb = T2[:, 0:16 * n].rearrange("p (i t) -> p i t", i=16)
        t1 = tt(a, s0, sN, M, t)
        t2 = tt(bb, s0, cN, M, t)
        t3 = tt(c1, c0, cN, M, t)
        t4 = tt(s1, c0, sN, M, t)
        tt(c1, c1, a, SU, t3)
        t = tt(s1, s1, bb, AD, t4)
        n *= 2
    pr.held["dve"] = [pr.held.get("dve"), t]
    t_e = t
    lay2 = Lay(keep)
    pr.held["dve"] = [pr.held.get("dve"), t_bt]
    ZA = [lay2.take(512).rearrange("p (s t) -> p s t", s=2) for _ in range(2)]
    ZB = [lay2.take(512).rearrange("p (s t) -> p s t", s=2) for _ in range(2)]
    ZS = [T1[:, 512 * i:512 * i + 512].rearrange("p (s t) -> p s t", s=2) for i in range(2)]
    XS = [T2[:, 512 * i:512 * i + 512].rearrange("p (s t) -> p s t", s=2) for i in range(2)]
    yT = T1[:, 1024:2048].rearrange("p (k t) -> p k t", k=4)
    xs_free = [None, None]
    yb = [bank(), bank()]
    kept.update(yb)
    y_waits = [bank_free[yb[0]], bank_free[yb[1]]]
    for i in range(16):
        ch, lo = i // 4, 32 * (i % 4)
        z = i % 2
        b = bank()
        t = mm(b, [(PS[b][:, 256 * s:256 * s + 256], [(BT[s][lo:lo + 32, ch, :], uT[lo:lo + 32, ch, :])])
                   for s in range(2)], t_bt)
        bu = PS[b][:, :].rearrange("p (s t) -> p s t", s=2)
        cB = EC[:, i:i + 1, :].to_broadcast([128, 2, 256])
        a, bb_, zs, xs = ZA[z], ZB[z], ZS[z], XS[z]
        t1 = tt(a, bu, cB, M, t, D())
        for s in range(2):
            t2 = tt(bb_[:, s, :], bu[:, 1 - s, :], ES[:, i, :], M, t)
        bank_free[b] = t2
        tt(a[:, 0, :], a[:, 0, :], bb_[:, 0, :], AD, t2)
        t2 = tt(a[:, 1, :], a[:, 1, :], bb_[:, 1, :], SU, t2)
        rb = g["rr"][:, i:i + 1].to_broadcast([128, 256])
        for s in range(2):
            t3 = pr.put("dve", lambda e, o=zs[:, s, :], d=a[:, s, :], rb=rb: e.tensor_tensor_scan(o, rb, d, 0.0, M, AD), t2)
        t4 = tt(a, zs, cB, M, t3)
        for s in range(2):
            t4 = tt(bb_[:, s, :], zs[:, 1 - s, :], ES[:, i, :], M, t3)
        tt(xs[:, 0, :], a[:, 0, :], bb_[:, 0, :], SU, t4, xs_free[z])
        t5 = tt(xs[:, 1, :], a[:, 1, :], bb_[:, 1, :], AD, t4)
        o = PS[yb[ch // 2]][lo:lo + 32, 256 * (ch % 2):256 * (ch % 2) + 256]
        t6 = pr.put("pe", lambda e, o=o, i=i, xs=xs: (e.matmul(o, CB[0][:, i, :], xs[:, 0, :], start=True, stop=False),
                                                     e.matmul(o, CB[1][:, i, :], xs[:, 1, :], start=False, stop=True))[1],
                    t5, y_waits)
        xs_free[z] = t6
    for ch in range(4):
        t = stt(yT[:, ch, :], uT[:, ch, :], V("ssm_d", ch), PS[yb[ch // 2]][:, 256 * (ch % 2):256 * (ch % 2) + 256],
                M, AD, t6, D())
        bank_free[yb[ch // 2]] = t
        t_y = act(yT[:, ch, :], yT[:, ch, :], ACT.Gelu_apprx_tanh, t)
    kept.clear()
    for mh in range(2):
        p = weight(A["w_glu"], 256 * mh, 256)
        for mi in range(2):
            m = 2 * mh + mi
            b = bank()
            t = mm(b, [(PS[b][:, 0:256], [(p.w[:, k, 128 * mi:128 * mi + 128], yT[:, k, :]) for k in range(4)])], t_y,
                   p.here)
            p.release = t
            sg = ZA[m % 2][:, 0, :]
            t = act(sg, PS[b][:, 0:256], ACT.Sigmoid, t, D(), bias=V("b_glu", m))
            bank_free[b] = t
            t_m = tt(OT[:, 4 + m, :], yT[:, m, :], sg, M, t)
    t = merged(lambda h, k: OT[:, 4 * h + k, :], 256, lambda h, k: V("g_attn" if h == 0 else "g_ssm", k), ACC, rstd,
               [t_m, t_m])

    def take_w(m, b, t):
        got2["w"] = cp(ACC[:, m, 0:256], PS[b][:, 0:256], t, e="act")
        bank_free[b] = got2["w"]

    project_all(A["w_out"], [0, 256, 512, 768], 256, t, take_w)
    t2 = got2["w"]
    add_normed(ACC, "postm", 5, 1.0, rstd, t2)
    t = feed_forward(2, 6)
    s_out = pr.new_sem("s_out")
    t = pr.dma("act", s_out, out.rearrange("(k p) t -> p k t", p=128), XT[:, :, 0:256], t)
    pr.wait("act", t)

    for p in pieces:
        prev = pieces[p.n - RING].release if p.n >= RING else None
        assert p.n < RING or prev is not None, p.n
        dst = p.ap
        if len(p.src.shape) == 3:
            dst = dst.rearrange("p (k m) -> p k m", k=p.src.shape[1])
        got = pr.dma("sp", slot_sem[p.slot], dst, p.src, prev)
        assert got == p.here

    block = ctx.enter_context(nc.Block())

    @block.sync
    def _(eng):
        pr.emit("sp", eng)

    @block.tensor
    def _(eng):
        pr.emit("pe", eng)

    @block.scalar
    def _(eng):
        pr.emit("act", eng)

    @block.vector
    def _(eng):
        pr.emit("dve", eng)

    @block.gpsimd
    def _(eng):
        pr.emit("pool", eng)


def constants():
    con = np.zeros((128, CON["n"]), np.float32)

    def put(name, a):
        o, w = CON[name]
        con[:, o:o + w] = a

    put("ones", np.ones((128, 128)))
    p = np.arange(128)
    put("blk", (p[:, None] // 64 == p[None, :] // 64))
    put("ident", np.eye(128))
    rot = np.zeros((128, 128), np.float32)
    for m in range(128):
        if m % 64 < 32:
            rot[m + 32, m] = -1.0
        else:
            rot[m - 32, m] = 1.0
    put("rot", rot)
    n = 16
    inv = np.float32(10000.0) ** (-np.arange(n, dtype=np.float32) / np.float32(n))
    tok = np.arange(256)
    ang = np.concatenate([(tok // 64).astype(np.float32)[:, None] * inv, (tok % 64).astype(np.float32)[:, None] * inv], 1)
    cos, sin = np.cos(ang).astype(np.float32), np.sin(ang).astype(np.float32)
    put("cos", cos.T[p % 32])
    put("sin", sin.T[p % 32])
    put("iota", np.arange(128)[None, :])
    put("eps", np.array([[1e-6, 1e-5]]))
    sel = np.zeros((128, 2), np.float32)
    for i in range(4):
        sel[32 * i, 0] = sel[32 * i + 1, 1] = 1.0
    put("sel", sel)
    al = np.zeros((128, 8, 256), np.float32)
    dist = np.arange(128)[:, None] + 128 - np.arange(256)[None, :]
    for h in range(8):
        al[:, h] = np.where((dist >= 0) & (dist < 128), -(2.0 ** (-(h + 1))) * dist, -1e30)
    return con, al.reshape(128, 2048)


def kernel(**inputs):
    import concourse.bacc as bacc
    from concourse.bass_utils import run_bass_kernel_spmd

    I = {k: np.asarray(v) for k, v in inputs.items()}

    def cols(v):
        return v.reshape(-1, 128).T

    def heads(v):
        return v.reshape((2, 4, 64) + v.shape[1:]).swapaxes(0, 1).reshape(v.shape)

    parts = []
    for l in range(2):
        parts += [cols(I["b_mod"][l]), np.concatenate([I["q_gain"][l]] * 2)[:, None],
                  np.concatenate([I["k_gain"][l]] * 2)[:, None],
                  I["conv_w"][l].reshape(31, 4, 128).transpose(2, 1, 0).reshape(128, 124),
                  cols(I["conv_b"][l]), cols(I["ln_g"][l]), cols(I["ln_b"][l]), cols(heads(I["beta_attn"][l])),
                  cols(I["beta_conv"][l])]
    st = lambda a: a.reshape(16, 128).T
    ls = np.broadcast_to(I["ssm_log_step_2"][0][:, None], (32, 64))
    parts += [cols(I["c"][0]), cols(I["c_ctx"]), cols(I["c_2"][0]), cols(I["final_g"]), cols(I["b_ada_2"][0]),
              cols(I["g_pre_ff1_2"][0]), cols(I["g_post_ff1_2"][0]), cols(I["g_pre_mix_2"][0]),
              cols(I["g_post_mix_2"][0]), cols(I["g_pre_ff2_2"][0]), cols(I["g_post_ff2_2"][0]),
              cols(I["ssm_d_2"][0]), cols(I["ssm_b_glu_2"][0]), cols(heads(I["g_attn_out_2"][0])),
              cols(I["g_ssm_out_2"][0]), st(I["ssm_a_re_2"][0]), st(I["ssm_a_im_2"][0]), st(ls),
              np.broadcast_to(I["attn_sinks_2"], (128, 8))]
    con, al = constants()

    def in_cols(w):
        return np.concatenate([w[:, 0:512].reshape(-1, 2, 4, 64).swapaxes(1, 2).reshape(-1, 512), w[:, 512:]], 1)

    def out_rows(w):
        return np.concatenate([heads(w[0:512]), w[512:]], 0)

    bsel = lambda a: a.reshape(16, 2, 64, 16).transpose(1, 2, 0, 3).reshape(128, 256)
    csel = lambda a: a.reshape(16, 2, 16, 64).transpose(1, 3, 0, 2).reshape(128, 256)
    arrays = {
        "vec": np.concatenate(parts, 1), "con": con, "alibi": al,
        "xT": np.concatenate([I["x"][0], I["ctx"][0]], 0).T,
        "w_mod": I["w_mod"], "w_ada": I["w_ada_2"][0],
        "w_in": np.stack([in_cols(w) for w in I["w_in"]]),
        "w_o": np.stack([out_rows(w) for w in I["w_o"]]),
        "peer_wq": I["peer_wq"],
        "keysT": I["peer_keys"].transpose(0, 2, 4, 1, 3).reshape(2, 128, 1024),
        "peer_uT": I["peer_u"].reshape(2, 64, 2, 128, 8, 128).transpose(0, 1, 5, 2, 4, 3).reshape(2, 64, 128, 2048),
        "peer_v": I["peer_v"],
        "w1_gate": I["w1_gate_2"][0], "w1_up": I["w1_up_2"][0], "w1_down": I["w1_down_2"][0],
        "w2_gate": I["w2_gate_2"][0], "w2_up": I["w2_up_2"][0], "w2_down": I["w2_down_2"][0],
        "w_in2": in_cols(I["w_in_2"][0]), "w_out": out_rows(I["w_out_2"][0]), "w_glu": I["ssm_w_glu_2"][0],
        "ssm_bc": np.concatenate([bsel(I["ssm_b_re_2"][0]), bsel(I["ssm_b_im_2"][0]),
                                  csel(I["ssm_c_re_2"][0]), csel(I["ssm_c_im_2"][0])], 1),
    }
    arrays = {k: np.ascontiguousarray(v) for k, v in arrays.items()}
    nc = bacc.Bacc("TRN2", target_bir_lowering=False, num_devices=1)
    A = {k: nc.dram_tensor(f"in_{k}", v.shape, mybir.dt.from_np(v.dtype), kind="ExternalInput").ap()
         for k, v in arrays.items()}
    out = nc.dram_tensor("out_T", (1024, 256), F32, kind="ExternalOutput").ap()
    build(nc, A, out)
    r = run_bass_kernel_spmd(nc, [{f"in_{k}": v for k, v in arrays.items()}], core_ids=[0])
    return np.ascontiguousarray(r.results[0]["out_T"].T)[None]
```

```python
from contextlib import ExitStack

import numpy as np

import concourse.bass as bass
from concourse import mybir

F32 = mybir.dt.float32
F32R = mybir.dt.float32r
U32 = mybir.dt.uint32
ALU = mybir.AluOpType
ACT = mybir.ActivationFunctionType
AX = mybir.AxisListType

RING = 4
SLOT = 2048
AREA = 16300
EPS = 1e-6
FILL_A = (5, 5)
FILL_B = (9, 9)
FILL_C = (7, 7)
FILL_W = (1, 1)
TWO_PI = 6.283185307179586

VEC = {}


def _layout():
    n = 0
    for l in range(2):
        for name, w in (("b_mod", 48), ("q_gain", 1), ("k_gain", 1), ("conv_w", 124), ("conv_b", 4),
                        ("ln_g", 4), ("ln_b", 4), ("beta_attn", 4), ("beta_conv", 4)):
            VEC[f"{name}{l}"] = (n, w)
            n += w
    for name, w in (("c", 8), ("c_ctx", 8), ("c2", 8), ("final_g", 8), ("b_ada", 72), ("pre1", 8), ("post1", 8),
                    ("prem", 8), ("postm", 8), ("pre2", 8), ("post2", 8), ("ssm_d", 4), ("b_glu", 4), ("g_attn", 4),
                    ("g_ssm", 4), ("a_re", 16), ("a_im", 16), ("log_step", 16), ("sinks", 8)):
        VEC[name] = (n, w)
        n += w
    VEC["n"] = n


_layout()

CON = {}


def _con_layout():
    n = 0
    for name, w in (("ones", 128), ("blk", 128), ("ident", 128), ("rot", 128), ("cos", 256), ("sin", 256),
                    ("iota", 128), ("eps", 2), ("sel", 2)):
        CON[name] = (n, w)
        n += w
    CON["n"] = n


_con_layout()


class Program:

    def __init__(self, nc, ctx):
        self.nc, self.ctx = nc, ctx
        self.queue = {e: [] for e in ("pe", "act", "dve", "pool", "sp")}
        self.count = {e: 0 for e in self.queue}
        self.sem = {e: ctx.enter_context(nc.semaphore(f"done_{e}")) for e in self.queue}
        self.seen = {e: {} for e in self.queue}
        self.held = {}

    def new_sem(self, name):
        self.sem[name] = self.ctx.enter_context(self.nc.semaphore(name))
        self.count[name] = 0
        return name

    def wait(self, e, waits):
        todo = [waits]
        while todo:
            w = todo.pop()
            if w is None:
                continue
            if isinstance(w, list):
                todo.extend(w)
                continue
            s, v = w
            if self.seen[e].get(s, 0) < v:
                self.seen[e][s] = v
                self.queue[e].append((s, v))

    def put(self, e, make, *waits):
        self.wait(e, list(waits) + [self.held.pop(e, None)])
        self.count[e] += 1
        self.queue[e].append((make, e, 1))
        return (e, self.count[e])

    def dma(self, e, sem, out, in_, *waits):
        self.wait(e, list(waits) + [self.held.pop(e, None)])
        self.count[sem] += 16
        self.queue[e].append((lambda eng: eng.dma_start(out, in_), sem, 16))
        return (sem, self.count[sem])

    def last(self, e):
        return (e, self.count[e])

    def phase(self, engines=("pe", "act", "dve")):
        now = [self.last(e) for e in engines]
        for e in list(engines) + ["pool"]:
            self.held[e] = [self.held.get(e), now]

    def emit(self, e, eng):
        for item in self.queue[e]:
            if len(item) == 2:
                eng.wait_ge(self.sem[item[0]], item[1])
            else:
                make, s, by = item
                make(eng).then_inc(self.sem[s], by)


def build(nc, A, out):
    with ExitStack() as ctx:
        _build(nc, ctx, A, out)


def _build(nc, ctx, A, out):
    pr = Program(nc, ctx)

    def sb(name, n):
        return ctx.enter_context(nc.sbuf_tensor(name, [128, n], F32))

    XT = sb("xT", 4096).rearrange("p (k t) -> p k t", k=8)
    fr = ctx.enter_context(nc.sbuf_tensor("fr", [128, 16384], F32R))
    HRs = [fr[:, 0:8192].rearrange("p (s k t) -> p s k t", s=2, k=8)]
    SR = [fr[:, 8192 + 2048 * i:8192 + 2048 * i + 2048].rearrange("p (s n) -> p s n", s=2) for i in range(2)]
    AG = [fr[:, 12288 + 2048 * i:12288 + 2048 * i + 2048].rearrange("p (s a t) -> p s a t", s=2, a=2) for i in range(2)]
    ACC = sb("acc", 4096).rearrange("p (k t) -> p k t", k=8)
    con = sb("con", CON["n"])
    vec = sb("vec", VEC["n"])
    mods = sb("mods", 2 * 96 + 72)
    scs = sb("scs", 512)
    mrow = sb("mrow", 512)
    ringt = sb("ring", RING * SLOT)
    area = sb("area", AREA)
    PS = [ctx.enter_context(nc.psum_tensor(f"ps{i}", [128, 512], F32)) for i in range(8)]
    scratch = nc.dram_tensor("w_scratch", (16, 128, 32, 128), F32, kind="Internal").ap()
    gscratch = nc.dram_tensor("g_scratch", (128, 128, 512), F32, kind="Internal").ap()

    def C(name):
        o, w = CON[name]
        return con[:, o:o + w]

    def V(name, j=None, w=1):
        o, n = VEC[name]
        return vec[:, o:o + n] if j is None else vec[:, o + j:o + j + w]

    MOD = [mods[:, 96 * l:96 * l + 96].rearrange("p (m s) -> p m s", s=2) for l in range(2)]
    ADA = mods[:, 192:264]

    bank_free = [None] * 8
    bank_next = [0]
    kept = set()

    def bank():
        while bank_next[0] % 8 in kept:
            bank_next[0] += 1
        b = bank_next[0] % 8
        bank_next[0] += 1
        return b

    pieces = []

    class Piece:
        def __init__(self, src, n):
            self.n = len(pieces)
            self.src, self.size = src, n
            self.release = None
            self.slot = self.n % RING
            self.ap = ringt[:, self.slot * SLOT:self.slot * SLOT + n]
            self.here = (slot_sem[self.slot], 16 * (self.n // RING + 1))
            pieces.append(self)

    slot_sem = [pr.new_sem(f"slot{i}") for i in range(RING)]

    def weight(w, c0, cols):
        k = w.shape[0] // 128
        src = w.rearrange("(k p) m -> p k m", p=128)[:, :, c0:c0 + cols]
        p = Piece(src, k * cols)
        p.w = p.ap.rearrange("p (k m) -> p k m", k=k)
        return p

    def mm(b, parts, *waits, first=True):
        def make(eng):
            for o, pairs in parts:
                for n, (lhs, rhs) in enumerate(pairs):
                    ins = eng.matmul(o, lhs, rhs, start=(n == 0), stop=(n == len(pairs) - 1))
            return ins
        return pr.put("pe", make, bank_free[b] if first else None, *waits)

    def tp(b, parts, *waits):
        def make(eng):
            for o, i in parts:
                ins = eng.transpose(o, i, C("ident"))
            return ins
        return pr.put("pe", make, bank_free[b], *waits)

    def act(o, i, f, *waits, **kw):
        return pr.put("act", lambda e: e.activation(o, i, f, **kw), *waits)

    def tt(o, a, b, op, *waits, e="dve"):
        return pr.put(e, lambda g: g.tensor_tensor(o, a, b, op), *waits)

    def ts(o, a, s1, s2, op0, op1, *waits, e="dve"):
        if op1 is None:
            return pr.put(e, lambda g: g.tensor_scalar(o, a, s1, None, op0), *waits)
        return pr.put(e, lambda g: g.tensor_scalar(o, a, s1, s2, op0, op1), *waits)

    def stt(o, a, s, b, op0, op1, *waits):
        return pr.put("dve", lambda g: g.scalar_tensor_tensor(out=o, in0=a, scalar=s, in1=b, op0=op0, op1=op1), *waits)

    def cp(o, i, *waits, e="dve"):
        if e == "act":
            return pr.put(e, lambda g: g.copy(o, i), *waits)
        return pr.put(e, lambda g: g.tensor_copy(o, i), *waits)

    M, AD, SU = ALU.mult, ALU.add, ALU.subtract

    def two_parts(hi, lo, x, *waits):
        t = cp(hi, x, *waits, e="act")
        return tt(lo, x, hi.bitcast(F32), SU, t, *waits)

    slot_free = [None] * 4
    slot_next = [0]

    def take_slot():
        i = slot_next[0] % len(SR)
        slot_next[0] += 1
        return i

    def split(x, shape, *waits):
        i = take_slot()
        t = two_parts(SR[i][:, 0, :], SR[i][:, 1, :], x, slot_free[i], *waits)
        v = [SR[i][:, s, :].rearrange("p (k m) -> p k m", k=shape) for s in range(2)]
        return i, v, t

    def three(lhs, rhs, terms):
        return [(lhs(a, k), rhs(b, k)) for k in terms for a, b in ((0, 0), (0, 1), (1, 0))]

    def project_all(w, order, T, t_in, take, lo=0, K=8):
        todo = []
        for c0 in order:
            cols = min(256, w.shape[1] - c0)
            todo.append((c0, cols))
        made = []

        def ahead():
            if todo:
                c0, cols = todo.pop(0)
                p = weight(w, c0, cols)
                for i in range(cols // 128):
                    made.append((c0 // 128 + i, p, i))

        pending = None
        while True:
            if not made:
                ahead()
            nxt = None
            if made:
                m, p, i = made.pop(0)
                x = p.w[:, :, 128 * i:128 * i + 128]
                sl = take_slot()
                hi = SR[sl][:, 0, :].rearrange("p (k m) -> p k m", k=8)
                lw = SR[sl][:, 1, :].rearrange("p (k m) -> p k m", k=8)
                t = two_parts(hi, lw, x, slot_free[sl], p.here)
                p.release = [t, pr.last("act")]
                nxt = (m, sl, (hi, lw), t)
            if pending is not None:
                m, sl, v, t = pending
                b = bank()
                t = mm(b, [(PS[b][:, 0:T - lo], three(lambda a, k: v[a][:, k, :], lambda c, k: HRs[0][:, c, k, lo:T],
                                                      range(8)))], t_in, t)
                slot_free[sl] = t
                take(m, b, t)
            if nxt is None:
                break
            pending = nxt

    class Lay:
        def __init__(self, base=0):
            self.at = base

        def take(self, n):
            v = area[:, self.at:self.at + n]
            self.at += n
            assert self.at <= AREA, self.at
            return v

    s_con, s_vec, s_x = pr.new_sem("s_con"), pr.new_sem("s_vec"), pr.new_sem("s_x")
    t_vec = pr.dma("act", s_vec, vec[:, :], A["vec"])
    t_con = pr.dma("act", s_con, con[:, :], A["con"])
    t_x = pr.dma("act", s_x, XT, A["xT"].rearrange("(k p) t -> p k t", p=128))
    SC = scs[:, 0:256].rearrange("p (k s) -> p k s", s=32)
    SC2 = scs[:, 256:512].rearrange("p (k s) -> p k s", s=32)
    t_z = pr.put("dve", lambda g: g.memset(scs[:, 0:512], 0.0))
    t_sc = act(SC[:, :, 0], V("c"), ACT.Silu, t_vec, t_z)
    t_sc = act(SC[:, :, 1], V("c_ctx"), ACT.Silu)
    t_sc = act(SC2[:, :, 0], V("c2"), ACT.Silu)
    row_free = [None, None]
    row_next = [0]

    def mod_vectors(w, c0, n, rhs, bias, dst, width, got):
        for j in range(n // 2):
            p = weight(w, 128 * c0 + 256 * j, 256)
            b = bank()

            def rows(eng, p=p, b=b):
                for i in range(2):
                    for q in range(4):
                        k = 2 * q + i
                        ins = eng.matmul(PS[b][32 * q:32 * q + 32, 0:256], rhs(k), p.w[:, k, :], start=(i == 0),
                                         stop=(i == 1))
                return ins
            t = pr.put("pe", rows, bank_free[b], p.here, t_sc)
            p.release = t
            r = row_next[0] % 2
            row_next[0] += 1
            mr = mrow[:, 256 * r:256 * r + 256]
            t = cp(mr, PS[b][:, 0:256], t, row_free[r], e="act")
            bank_free[b] = t
            yield
            b = bank()
            t = mm(b, [(PS[b][:, width * i:width * i + width], [(mr[:, 128 * i:128 * i + 128], C("sel")[:, 0:width])])
                       for i in range(2)], t, t_con)
            row_free[r] = t
            m = 2 * j
            o = PS[b][:, 0:2 * width]
            if width == 2:
                o = o.rearrange("p (m s) -> p m s", s=2)
            t = tt(dst[:, m:m + 2], o, bias[:, m:m + 2], AD, t, t_vec)
            bank_free[b] = t
        got.append(t)
        yield

    def mod_layer(l, c0, n, got):
        return mod_vectors(A["w_mod"][l], c0, n, lambda k: SC[:, k, :],
                           V(f"b_mod{l}", c0, n).unsqueeze(2).to_broadcast([128, n, 2]), MOD[l][:, c0:c0 + n, :], 2, got)

    def ada_layer(got):
        return mod_vectors(A["w_ada"], 0, 72, lambda k: SC2[:, k, :], V("b_ada"), ADA, 1, got)

    later = []

    def some(n):
        while n > 0 and later:
            if next(later[0], "end") == "end":
                later.pop(0)
                continue
            n -= 1

    def inverse_root(src, chunks, T, sq, rstd, n, eps_col, *waits, lhs="ones"):
        ts_sq = []
        for k in range(chunks):
            ts_sq.append(act(sq(k), src(k), ACT.Square, *waits))
        b = bank()
        t = mm(b, [(PS[b][:, 0:T], [(C(lhs), sq(k)) for k in range(chunks)])], ts_sq[-1], t_con)
        t = act(rstd, PS[b][:, 0:T], ACT.Sqrt, t, pr.last("dve"), scale=1.0 / n, bias=C("eps")[:, eps_col:eps_col + 1])
        bank_free[b] = t
        return pr.put("dve", lambda g: g.reciprocal(rstd, rstd), t)

    def add1(v):
        return ts(v, v, 1.0, None, AD, None, pr.last("dve"))

    def modulated(streams, T, mult_of, add_of, rstd, *waits, gain=None):
        t = inverse_root(lambda k: XT[:, k, 0:T], 8, T, lambda k: ACC[:, k, 0:T], rstd[:, 0:T], 1024, 0,
                         t_x, pr.last("dve"), pr.last("pe"))
        t_pe = pr.last("pe")
        done = []
        for k in range(8):
            h = ACC[:, k, 0:T]
            if gain is None:
                t1 = tt(h, XT[:, k, 0:T], rstd[:, 0:T], M, t, t_pe)
            else:
                t1 = stt(h, XT[:, k, 0:T], gain(k), rstd[:, 0:T], M, M, t, t_pe)
            done.append(t1)
        for k in range(8):
            for s, (a, z) in streams:
                done[k] = ts(ACC[:, k, a:z], ACC[:, k, a:z], mult_of(k, s), add_of(k, s), M, AD, done[k], *waits)
        for k in range(8):
            t2 = two_parts(HRs[0][:, 0, k, 0:T], HRs[0][:, 1, k, 0:T], ACC[:, k, 0:T], done[k])
        return t2

    BOTH = [(0, (0, 256)), (1, (256, 512))]

    def attend(q, kT, vtok, dest, lay, tiles, q0, sinks, bias, t_in, side=lambda: None):
        W_ = 128 * max(len(k) for k in tiles)
        nq = len(tiles)
        P3 = [lay.take(W_) for _ in range(4)]
        PT2 = [lay.take(W_ * nq).rearrange("p (c q) -> p c q", q=128 * nq) for _ in range(2)]
        st = lay.take(64)
        p_free = [None] * 4
        pt_free = [None, None]
        todo = [(i, kv, qt) for i in range(4) for kv in range(2) for qt in range(nq)]
        live = {}
        outs = {}

        def scores(n):
            i, kv, qt = todo[n]
            base = 64 * kv
            keys = tiles[qt]
            N = 128 * len(keys)
            k0 = 128 * keys[0]
            b = bank()
            t = mm(b, [(PS[b][:, 0:N], [(q[base:base + 64, i, q0 + 128 * qt:q0 + 128 * qt + 128],
                                         kT[base:base + 64, k0:k0 + N])])], t_in)
            S = PS[b][:, 0:N]
            P = P3[n % 4][:, 0:N]
            c = 8 * (n % 8)
            mx, nb, den, rec, es = (st[:, c + j:c + j + 1] for j in range(5))
            if bias is None:
                t = pr.put("dve", lambda g: g.tensor_reduce(mx, S, AX.X, ALU.max), t)
                t = ts(nb, mx, -0.125, None, M, None, t)
                t = act(P, S, ACT.Exp, t, p_free[n % 4], scale=0.125, bias=nb, accum_out=den)
                bank_free[b] = t
            else:
                h = i + 4 * kv
                t = stt(P, S, 0.125, bias(h, qt, N), M, AD, t, p_free[n % 4])
                bank_free[b] = t
                t = pr.put("dve", lambda g: g.tensor_reduce(mx, P, AX.X, ALU.max), t)
                t = ts(nb, mx, sinks(h), -1.0, ALU.max, M, t)
                t2 = act(P, P, ACT.Exp, t, bias=nb, accum_out=den)
                t = [t2, act(es, sinks(h), ACT.Exp, t, bias=nb)]
            live[n] = (P, N, den, rec, es, t)

        def turn(n):
            i, kv, qt = todo[n]
            base = 64 * kv
            P, N, den, rec, es, t = live.pop(n)
            PT = PT2[kv]
            if bias is not None:
                t = tt(den, den, es, AD, t)
            t = pr.put("dve", lambda g: g.reciprocal(rec, den), t)
            t = ts(P, P, rec, None, M, None, t)
            b = bank()
            t = tp(b, [(PS[b][:, 128 * j:128 * j + 128], P[:, 128 * j:128 * j + 128]) for j in range(N // 128)], t,
                   t_con)
            p_free[n % 4] = t
            o = PT[:, 0:N // 128, 128 * qt:128 * qt + 128]
            t = cp(o, PS[b][:, 0:N].rearrange("p (c q) -> p c q", q=128), t, pt_free[kv], e="act")
            bank_free[b] = t
            live[("t", i, kv, qt)] = t

        def values(i, kv):
            base = 64 * kv
            PT = PT2[kv]
            t_pt = [live.pop(("t", i, kv, qt)) for qt in range(nq)]
            if kv == 0:
                outs[i] = bank()
                kept.add(outs[i])
            bo = outs[i]
            if all(len(k) == len(tiles[0]) for k in tiles):
                parts = [(PS[bo][base:base + 64, 0:128 * nq],
                          [(vtok[:, kc, base:base + 64], PT[:, j, 0:128 * nq]) for j, kc in enumerate(tiles[0])])]
            else:
                parts = [(PS[bo][base:base + 64, 128 * qt:128 * qt + 128],
                          [(vtok[:, kc, base:base + 64], PT[:, j, 128 * qt:128 * qt + 128])
                           for j, kc in enumerate(keys)]) for qt, keys in enumerate(tiles)]
            t = mm(bo, parts, t_pt)
            pt_free[kv] = t
            if kv == 1:
                t = cp(dest(i), PS[bo][:, 0:128 * nq], t)
                bank_free[bo] = t
                kept.discard(bo)
            return t

        LAG = 3
        for n in range(len(todo) + LAG + 1):
            if n < len(todo):
                scores(n)
            side()
            if 0 <= n - LAG < len(todo):
                turn(n - LAG)
            m = n - LAG - 1
            if m >= 0 and todo[m][2] == nq - 1:
                t = values(todo[m][0], todo[m][1])
        return t

    def merged(parts_of, T, beta, sq, rstd, t_ins):
        for half in range(2):
            t = inverse_root(lambda k: parts_of(half, k), 4, T, lambda k: sq[:, 4 * half + k, 0:T],
                             rstd[:, 0:T], 512, 0, t_ins[half], pr.last("pe"))
            ds = []
            for k in range(4):
                o = parts_of(half, k)
                ds.append(stt(o, o, beta(half, k), rstd[:, 0:T], M, M, t))
            for k in range(4):
                t = two_parts(HRs[0][:, 0, 4 * half + k, 0:T], HRs[0][:, 1, 4 * half + k, 0:T], parts_of(half, k), ds[k])
        return t

    def mixer(l):
        last = l == 1
        T = 512
        Tq = 256 if last else 512
        streams_q = BOTH[:1] if last else BOTH
        lay = Lay()
        q = lay.take(2048).rearrange("p (k t) -> p k t", k=4)
        kk = lay.take(512)
        vT = lay.take(512)
        vtok = lay.take(512).rearrange("p (c d) -> p c d", c=4)
        gp = lay.take(4 * 2 * 286).rearrange("p (c s t) -> p c s t", c=4, s=2)
        y = lay.take(2048).rearrange("p (k t) -> p k t", k=4)
        OT = lay.take(2048).rearrange("p (k t) -> p k t", k=4)
        rstd = lay.take(512)
        tmps = [lay.take(512) for _ in range(2)]
        t = modulated(BOTH, 512, lambda k, s: MOD[l][:, 8 + k, s:s + 1], lambda k, s: MOD[l][:, k, s:s + 1], rstd,
                      mod1[l])
        t_h = [t]
        W = A["w_in"][l]
        t_ms = pr.put("pool", lambda g: g.memset(gp, 0.0))

        got = {}

        def take_qk(m, b, t):
            o = q[:, m, 0:Tq] if m < 4 else kk[:, :] if m == 4 else vT[:, :]
            t = cp(o, PS[b][:, 0:Tq if m < 4 else 512], t, e="act")
            bank_free[b] = t
            got[m] = t

        project_all(W, [0, 256], Tq, t_h, take_qk)
        project_all(W, [512], 512, t_h, take_qk)
        t_q, t_v = got[3], got[5]
        b = bank()
        t = tp(b, [(PS[b][:, 128 * c:128 * c + 128], vT[:, 128 * c:128 * c + 128]) for c in range(4)], t_v)
        t_vt = cp(vtok, PS[b][:, :].rearrange("p (c d) -> p c d", c=4), t, e="act")
        bank_free[b] = t_vt

        sgs = {}

        def turned():
            sizes = [Tq] * 4 + [512]
            X = [q[:, i, 0:Tq] for i in range(4)] + [kk[:, :]]
            gains = [V(f"q_gain{l}")] * 4 + [V(f"k_gain{l}")]
            sq, rs, rot = y[:, 0:2, :], y[:, 2:4, :], OT[:, 0, 0:256]
            t_sq, t_x, sq_free, rs_free = {}, {}, {}, {}
            for n in range(7):
                if n < 5:
                    t_sq[n] = act(sq[:, n % 2, 0:sizes[n]], X[n], ACT.Square, [got.get(min(n, 3)), got[4]], sq_free.get(n - 2))
                if 0 <= n - 1 < 5:
                    i, TT = n - 1, sizes[n - 1]
                    b = bank()
                    t = mm(b, [(PS[b][:, 0:TT], [(C("blk"), sq[:, i % 2, 0:TT])])], t_sq[i])
                    sq_free[i] = t
                    r_ = rs[:, i % 2, 0:TT]
                    t = act(r_, PS[b][:, 0:TT], ACT.Sqrt, t, rs_free.get(i - 2), scale=1.0 / 64, bias=C("eps")[:, 0:1])
                    bank_free[b] = t
                    t = pr.put("dve", lambda g, r_=r_: g.reciprocal(r_, r_), t)
                    t_x[i] = rs_free[i] = stt(X[i], X[i], gains[i], r_, M, M, t)
                if n >= 2:
                    i = n - 2
                    b = bank()
                    t = mm(b, [(PS[b][:, 0:256], [(C("rot"), X[i][:, 0:256])])], t_x[i])
                    t3 = tt(rot, PS[b][:, 0:256], C("sin"), M, t, got.get("qk"))
                    bank_free[b] = t3
                    t3 = tt(X[i][:, 0:256], X[i][:, 0:256], C("cos"), M, t)
                    got["qk"] = tt(X[i][:, 0:256], X[i][:, 0:256], rot, AD, t3)
                yield

        turning = turned()

        def take_u(m, b, t):
            if m >= 10:
                sg = tmps[m % 2][:, 0:Tq]
                t = act(sg, PS[b][:, 0:Tq], ACT.Sigmoid, t, sgs.get(("free", m % 2)))
                sgs[m - 10] = (sg, t)
                bank_free[b] = t
            else:
                i = m - 6
                sg, t1 = sgs[i]
                for s, (a, z) in streams_q:
                    got["g"] = tt(gp[:, i, s, 15:271], PS[b][:, a:z], sg[:, a:z], M, t, t1, t_ms)
                sgs[("free", m % 2)] = got["g"]
                bank_free[b] = got["g"]

        def take_u_and_turn(m, b, t):
            take_u(m, b, t)
            next(turning, None)

        project_all(W, [1280, 768, 1536, 1024], Tq, t_h, take_u_and_turn)
        for _ in turning:
            pass
        t_g, t_qk = got["g"], got["qk"]

        t_conv = {}

        def taps():
            for j in range(31):
                for i in range(4):
                    w = V(f"conv_w{l}", 31 * i + j)
                    for_s = gp[:, i, 0:len(streams_q), j:j + 256]
                    o = y[:, i, 0:Tq].rearrange("p (s t) -> p s t", t=256)
                    if j == 0:
                        t_conv[i] = ts(o, for_s, w, V(f"conv_b{l}", i), M, AD, t_g, t_qk)
                    else:
                        t_conv[i] = stt(o, for_s, w, o, M, AD, t_conv[i])
                    yield

        tap = taps()

        def side(n=4 if not last else 6):
            for _ in range(n):
                next(tap, None)
            some(2)

        lay_a = Lay(lay.at)
        t_in = [t_qk, t_vt]
        t_o = attend(q, kk, vtok, lambda i: OT[:, i, 0:256], lay_a, [[0, 1, 2, 3]] * 2, 0, None, None, t_in, side)
        if not last:
            lay_a = Lay(lay.at)
            pr.phase(("pe", "act", "dve"))
            t_o = attend(q, kk, vtok, lambda i: OT[:, i, 256:512], lay_a, [[2, 3]] * 2, 256, None, None, t_in, side)

        for _ in tap:
            pass
        t_y = list(t_conv.values())

        b = bank()
        t = mm(b, [(PS[b][:, 0:Tq], [(C("ones"), y[:, k, 0:Tq]) for k in range(4)])], t_y)
        mu = tmps[0][:, 0:Tq]
        t = ts(mu, PS[b][:, 0:Tq], 1.0 / 512, None, M, None, t)
        bank_free[b] = t
        for k in range(4):
            t1 = tt(y[:, k, 0:Tq], y[:, k, 0:Tq], mu, SU, t)
        t = inverse_root(lambda k: y[:, k, 0:Tq], 4, Tq, lambda k: ACC[:, k, 0:Tq], rstd[:, 0:Tq], 512, 1, t1)
        for k in range(4):
            t1 = stt(y[:, k, 0:Tq], y[:, k, 0:Tq], V(f"ln_g{l}", k), rstd[:, 0:Tq], M, M, t)
            t_c = act(y[:, k, 0:Tq], y[:, k, 0:Tq], ACT.Silu, t1, bias=V(f"ln_b{l}", k))
        t = merged(lambda h, k: (OT if h == 0 else y)[:, k, 0:Tq], Tq,
                   lambda h, k: V(f"beta_attn{l}" if h == 0 else f"beta_conv{l}", k), ACC, rstd, [t_o, t_c])

        def take_o(m, b, t):
            for s, (a, z) in streams_q:
                t2 = stt(XT[:, m, a:z], PS[b][:, a:z], MOD[l][:, 16 + m, s:s + 1], XT[:, m, a:z], M, AD, t, mod2[l])
            bank_free[b] = t2

        project_all(A["w_o"][l], [0, 256, 512, 768], Tq, t, take_o)
        pr.phase()

    s_wst = [pr.new_sem(f"s_wst{i}") for i in range(2)]
    s_wrd = [pr.new_sem(f"s_wrd{i}") for i in range(2)]
    scratch_read = [None]

    s_gst = [pr.new_sem(f"s_gst{i}") for i in range(2)]
    s_grd = [pr.new_sem(f"s_grd{i}") for i in range(2)]

    def peer(l):
        T = 256 if l == 1 else 512
        if l == 1:
            HRs[0] = fr[:, 0:4096].rearrange("p (s k t) -> p s k t", s=2, k=8)
            for i in range(2):
                SR.append(fr[:, 4096 + 2048 * i:4096 + 2048 * i + 2048].rearrange("p (s n) -> p s n", s=2))
                slot_free[2 + i] = pr.last("pe")
        nt = T // 128
        streams = BOTH[:1] if l == 1 else BOTH
        lay = Lay()
        GS = [lay.take(512) for _ in range(2)]
        rstd = lay.take(512)
        base = lay.at
        iT = lay.take(3 * 512).rearrange("p (c t) -> p c t", c=3)
        qT = lay.take(4096).rearrange("p (k t) -> p k t", k=8)
        SW = [lay.take(256) for _ in range(4)]
        TS_ = lay.take(256).rearrange("p (h r) -> p h r", r=16)
        TI = lay.take(256).bitcast(U32).rearrange("p (h r) -> p h r", r=16)
        TIf = lay.take(256).rearrange("p (h r) -> p h r", r=16)
        cand = lay.take(1024)
        BS, BJ, R1, R2, R1f, R2f, I1, I2, WW = (lay.take(128) for _ in range(9))
        eq = lay.take(1024)
        mxs = lay.take(8)
        sm = lay.take(8)
        OH = lay.take(8 * 256).rearrange("p (h c q j) -> p h c q j", h=2, c=2, q=4)
        stage = [ACC[:, 4 * i:4 * i + 4, :].rearrange("p k t -> p (k t)") for i in range(2)]
        keys = lay.take(1024).rearrange("p (h k) -> p h k", h=8)

        t_h = modulated(streams, T, lambda k, s: MOD[l][:, 32 + k, s:s + 1], lambda k, s: MOD[l][:, 24 + k, s:s + 1],
                        rstd, mod2[l])
        got = {}

        def take_q(m, b, t):
            t = cp(qT[:, m, 0:T], PS[b][:, 0:T], t, e="act")
            bank_free[b] = t
            got["q"] = t

        some(100)
        project_all(A["peer_wq"][l], [0, 256, 512, 768], T, t_h, take_q)
        t_q = got["q"]
        pk = Piece(A["keysT"][l], 1024)
        t_keys = cp(keys, pk.ap.rearrange("p (h k) -> p h k", h=8), pk.here, e="act")
        pk.release = t_keys

        u_piece = {}
        u_made = {}

        def u_split(a):
            if a % 2 == 0:
                u_piece[a // 2] = Piece(A["peer_uT"][l, a // 2], 2048)
            p = u_piece[a // 2]
            u_made[a] = split(p.ap[:, 1024 * (a % 2):1024 * (a % 2) + 1024], 8, p.here)
            p.release = [p.release, u_made[a][2], pr.last("act")]

        def u_high(a):
            if a % 2 == 0:
                u_piece[a // 2] = Piece(A["peer_uT"][l, a // 2], 2048)
            p = u_piece[a // 2]
            i = take_slot()
            x = p.ap[:, 1024 * (a % 2):1024 * (a % 2) + 1024]
            u_made[a] = (i, x, cp(SR[i][:, 0, :], x, slot_free[i], p.here, e="act"))

        def u_low(a):
            i, x, t = u_made[a]
            p = u_piece[a // 2]
            t = tt(SR[i][:, 1, :], x, SR[i][:, 0, :].bitcast(F32), SU, t, p.here, e="pool")
            p.release = [p.release, t, pr.last("act")]
            u_made[a] = (i, [SR[i][:, s, :].rearrange("p (k m) -> p k m", k=8) for s in range(2)], t)

        def u_product(a, steps):
            i, v, t = u_made.pop(a)
            b = bank()
            kept.add(b)
            pairs = three(lambda s, k: v[s][:, k, :], lambda s, k: HRs[0][:, s, k, 0:T], range(8))
            per = -(-len(pairs) // steps)
            for n in range(0, len(pairs), per):
                def make(eng, n=n):
                    for m in range(n, min(n + per, len(pairs))):
                        ins = eng.matmul(PS[b][:, 0:T], pairs[m][0], pairs[m][1], start=(m == 0),
                                         stop=(m == len(pairs) - 1))
                    return ins
                t = pr.put("pe", make, t, t_h, bank_free[b])
                yield None
            kept.discard(b)
            slot_free[i] = t
            yield (b, t)

        spilled = {}
        gs_free = [None, None]

        def spill(a, b, t):
            g = GS[a % 2][:, 0:T]
            t = act(g, PS[b][:, 0:T], ACT.Gelu, t, gs_free[a % 2])
            bank_free[b] = t
            spilled[a] = gs_free[a % 2] = pr.dma("pool", s_gst[a % 2], gscratch[a, :, 0:T], g, t)

        def early():
            u_split(0)
            a = 0
            while a in u_made:
                more = a < 125 and not ending
                for n, got_ in enumerate(u_product(a, 4)):
                    if got_ is None:
                        if n == 0 and more:
                            u_high(a + 1)
                        if n == 2 and more:
                            u_low(a + 1)
                        yield
                b, t = got_
                spill(a, b, t)
                a += 1
                yield
            while True:
                yield

        ending = []
        filling = early()

        def fill(n):
            for _ in range(n):
                next(filling)

        stage_free = [None, None]
        t_stored = []
        oh_free = [None, None]
        quad = 0
        n_st = 0
        tsv = TS_.rearrange("p (h c) r -> p h c r", c=2)
        tiv = TIf.rearrange("p (h c) r -> p h c r", c=2)

        def best16(sets):
            def each(f, waits):
                return [pr.put("dve", f(*x), w) for x, w in zip(sets, waits)]
            w0 = [x[4] for x in sets]
            t = each(lambda S, W, v, i, _: lambda g: g.max(v[:, 0:8], S), w0)
            t1 = each(lambda S, W, v, i, _: lambda g: g.match_replace(W, v[:, 0:8], S, -3.0e38), t)
            t = each(lambda S, W, v, i, _: lambda g: g.max_index(i[:, 0:8], v[:, 0:8], S), t)
            t2 = each(lambda S, W, v, i, _: lambda g: g.max(v[:, 8:16], W), t1)
            return each(lambda S, W, v, i, _: lambda g: g.max_index(i[:, 8:16], v[:, 8:16], W), t2)

        for tt_ in range(nt):
            for h4 in range(4):
                b = bank()
                parts = []
                for j in range(4):
                    h, c = 4 * (h4 // 2) + j, h4 % 2
                    parts.append((PS[b][:, 128 * j:128 * j + 128],
                                  [(qT[64 * c:64 * c + 64, h, 128 * tt_:128 * tt_ + 128], keys[64 * c:64 * c + 64, h, :])]))
                t = mm(b, parts, t_q, t_keys)
                sets = []
                for j in range(4):
                    hc = 2 * (4 * (h4 // 2) + j) + h4 % 2
                    sets.append((PS[b][:, 128 * j:128 * j + 128], SW[j][:, 0:128], TS_[:, hc, :], TI[:, hc, :],
                                 [t, pr.last("dve")]))
                t = best16(sets)
                bank_free[b] = t
                fill(FILL_A[l])
            t = cp(TIf, TI, t)
            bs = BS.rearrange("p (h r) -> p h r", r=16)
            bj = BJ.bitcast(U32).rearrange("p (h r) -> p h r", r=16)
            for h0 in (0, 4):
                cv = cand.rearrange("p (h a b) -> p h a b", h=4, a=16)
                t = tt(cv, tsv[:, h0:h0 + 4, 0, :].unsqueeze(3).to_broadcast([128, 4, 16, 16]),
                       tsv[:, h0:h0 + 4, 1, :].unsqueeze(2).to_broadcast([128, 4, 16, 16]), AD, t, pr.last("dve"))
                t = best16([(cand[:, 256 * j:256 * j + 256], SW[j], bs[:, h0 + j, :], bj[:, h0 + j, :], t)
                            for j in range(4)])
                fill(FILL_B[l])
            t1 = ts(R1.bitcast(U32), BJ.bitcast(U32), 4, None, ALU.logical_shift_right, None, t)
            t2 = ts(R2.bitcast(U32), BJ.bitcast(U32), 15, None, ALU.bitwise_and, None, t)
            t3 = cp(mxs, bs[:, :, 0], t)
            t1 = cp(R1f, R1.bitcast(U32), t1)
            t2 = cp(R2f, R2.bitcast(U32), t2)
            ww = WW.rearrange("p (h r) -> p h r", r=16)
            t3 = tt(ww, bs, mxs.unsqueeze(2).to_broadcast([128, 8, 16]), SU, t3, pr.last("pe"))
            t_e = act(WW, WW, ACT.Exp, t3)
            for c, (Rf, I) in enumerate(((R1f, I1), (R2f, I2))):
                for h0 in (0, 4):
                    ev = eq.rearrange("p (j r) -> p j r", r=16)
                    t4 = tt(ev, Rf[:, 16 * h0:16 * h0 + 64].unsqueeze(2).to_broadcast([128, 64, 16]),
                            C("iota")[:, 0:16].unsqueeze(1).to_broadcast([128, 64, 16]), ALU.is_equal, t1, t2,
                            pr.last("dve"))
                    e4 = eq.rearrange("p (h k r) -> p h k r", h=4, k=16)
                    t4 = tt(e4, e4, tiv[:, h0:h0 + 4, c, :].unsqueeze(2).to_broadcast([128, 4, 16, 16]), M, t4)
                    t4 = pr.put("dve", lambda g, I=I, ev=ev, h0=h0: g.tensor_reduce(I[:, 16 * h0:16 * h0 + 64], ev,
                                                                                   AX.X, ALU.add), t4)
                fill(FILL_C[l])
            t5 = pr.put("dve", lambda g: g.tensor_reduce(sm, ww, AX.X, ALU.add), t_e)
            t5 = pr.put("dve", lambda g: g.reciprocal(sm, sm), t5)
            t5 = tt(ww, ww, sm.unsqueeze(2).to_broadcast([128, 8, 16]), M, t5)
            b = bank()
            t = tp(b, [(PS[b][:, 128 * j:128 * j + 128], X) for j, X in enumerate((I1, I2, WW))], t5)
            t_i = cp(iT[:, :, 128 * tt_:128 * tt_ + 128], PS[b][:, 0:384].rearrange("p (c t) -> p c t", c=3), t)
            bank_free[b] = t_i
            fill(FILL_C[l])
            for tb in range(8):
                st = stage[n_st % 2]
                sv = st.rearrange("p (a t) -> p a t", t=16)
                for qd in range(4):
                    half = quad % 2
                    tok = 128 * tt_ + 16 * tb + 4 * qd
                    tt(OH[:, half, 0], C("iota").unsqueeze(1).to_broadcast([128, 4, 128]),
                       iT[:, 1, tok:tok + 4].unsqueeze(2).to_broadcast([128, 4, 128]), ALU.is_equal, t_i, oh_free[half])
                    for j in range(4):
                        t = ts(OH[:, half, 1, j, :], C("iota"), iT[:, 0, tok + j:tok + j + 1],
                               iT[:, 2, tok + j:tok + j + 1], ALU.is_equal, M)
                    b = bank()
                    t = mm(b, [(PS[b][:, 128 * j:128 * j + 128], [(OH[:, half, 0, j, :], OH[:, half, 1, j, :])])
                               for j in range(4)], t)
                    oh_free[half] = t
                    quad += 1
                    t = cp(sv[:, :, 4 * qd:4 * qd + 4], PS[b][:, :].rearrange("p (t a) -> p a t", t=4), t,
                           stage_free[n_st % 2], t_h, e="act")
                    bank_free[b] = t
                    fill(FILL_W[l])
                tbn = 8 * tt_ + tb
                t = pr.dma("pool", s_wst[n_st % 2], scratch[:, :, tbn, :].rearrange("g b x -> b g x"),
                           st.rearrange("p (g x) -> p g x", g=16), t, scratch_read[0])
                stage_free[n_st % 2] = t
                t_stored.append(t)
                n_st += 1
        ending.append(True)
        while u_made or kept:
            fill(1)
        if len(spilled) % 2:
            u_split(len(spilled))
            for got_ in u_product(len(spilled), 1):
                pass
            spill(len(spilled), *got_)
        na = len(spilled)
        pr.phase()
        now = [stage_free[0], stage_free[1]]

        lay = Lay(base)
        WG = [lay.take(4096) for _ in range(2)]
        GL = [lay.take(1024).rearrange("p (a t) -> p a t", a=2) for _ in range(2)]
        ntb = T // 16
        w_read = [now, now]
        a_free = [now, now]
        gl_free = [now, now]
        t_w, t_a, vp, t_gl = {}, {}, {}, {}
        yb = []
        if l == 1:
            yb = [bank() for _ in range(4)]
            kept.update(yb)
        t_acc = None
        acc_there = {}
        held = max(na // 2 - 1, 0) if l == 0 else 0
        while bank_next[0] % 8:
            bank_next[0] += 1

        def load_w(g8):
            if g8 < 16:
                t_w[g8] = pr.dma("pool", s_wrd[g8 % 2], WG[g8 % 2][:, 0:8 * T].rearrange("p (b x) -> p b x", x=128),
                                 scratch[g8, :, 0:ntb, :], w_read[g8 % 2], t_stored)
                scratch_read[0] = t_w[g8]

        def load_g(g):
            if 2 * g < na:
                n = min(2, na - 2 * g)
                t_gl[g] = pr.dma("pool", s_grd[g % 2], GL[g % 2][:, 0:n, 0:T],
                                 gscratch[2 * g:2 * g + n, :, 0:T].rearrange("a b t -> b a t"), gl_free[g % 2],
                                 [spilled[x] for x in range(2 * g, 2 * g + n)], pr.last("dve"))

        def weigh(a, b, t):
            g, j = a // 2, a % 2
            x = GL[g % 2][:, j, 0:T]
            if b is not None:
                t = act(x, PS[b][:, 0:T], ACT.Gelu, t, gl_free[g % 2])
                bank_free[b] = t
            wv = WG[(a // 8) % 2][:, 0:8 * T].rearrange("p (b a t) -> p a b t", a=8, t=16)[:, a % 8]
            t = tt(x.rearrange("p (b t) -> p b t", t=16), x.rearrange("p (b t) -> p b t", t=16), wv, M, t,
                   t_w[a // 8])
            w_read[(a // 8) % 2] = t
            t = two_parts(AG[g % 2][:, 0, j, 0:T], AG[g % 2][:, 1, j, 0:T], x, t, a_free[g % 2])
            t_a[a] = t
            gl_free[g % 2] = t

        units = []
        for g in range(65):
            if g < 64:
                for a in (2 * g, 2 * g + 1):
                    units.append(("u", a))
            if g >= 1:
                units += [("v", g - 1, 0), ("v", g - 1, 1)]

        def prepare(u):
            if u[0] == "u":
                if u[1] >= na and u[1] not in u_made:
                    u_split(u[1])
            else:
                g, mh = u[1], u[2]
                if mh == 0:
                    p = Piece(A["peer_v"][l].rearrange("(g a b) d -> g b a d", g=64, a=2)[g], 2048)
                    vp[g] = p
                p = vp[g]
                src = p.ap.rearrange("p (a d) -> p a d", a=2)[:, :, 512 * mh:512 * mh + 512]
                sl = take_slot()
                v = [SR[sl][:, s, :].rearrange("p (a d) -> p a d", a=2) for s in range(2)]
                t = two_parts(v[0], v[1], src, slot_free[sl], p.here)
                p.release = [t, pr.last("act")]
                vp[(g, mh)] = (sl, v, t)

        load_w(0)
        load_w(1)
        load_g(0)
        load_g(1)
        work = [u for u in units if u[0] == "v" or u[1] >= na]
        ahead = 1 if l == 0 else 2
        for u in work[:ahead]:
            prepare(u)
        n = 0
        for u in units:
            if u[0] == "u" and u[1] < na:
                weigh(u[1], None, t_gl[u[1] // 2])
            else:
                if n + ahead < len(work):
                    prepare(work[n + ahead])
                n += 1
            if u[0] == "u":
                a = u[1]
                if a >= na:
                    for got_ in u_product(a, 1):
                        pass
                    weigh(a, *got_)
                if a % 8 == 7:
                    load_w(a // 8 + 2)
                if a % 2 == 1 and a >= 3:
                    load_g(a // 2 + 1)
            else:
                g, mh = u[1], u[2]
                sl, v, tv = vp[(g, mh)]
                for mi in range(4):
                    m = 4 * mh + mi
                    pairs = three(lambda s, a: v[s][:, a, 128 * mi:128 * mi + 128],
                                  lambda s, a: AG[g % 2][:, s, a, 0:T], range(2))
                    if l == 1:
                        o = PS[yb[m // 2]][:, 256 * (m % 2):256 * (m % 2) + 256]

                        def make(eng, o=o, pairs=pairs, g=g, m=m):
                            for n_, (x, y_) in enumerate(pairs):
                                ins = eng.matmul(o, x, y_, start=(g == 0 and n_ == 0 and m % 2 == 0),
                                                 stop=(g == 63 and n_ == 5 and m % 2 == 1), skip_group_check=True)
                            return ins
                        t = pr.put("pe", make, tv, t_a[2 * g + 1], bank_free[yb[m // 2]] if g == 0 else None)
                    elif g < held:
                        def make(eng, m=m, pairs=pairs, g=g):
                            for n_, (x, y_) in enumerate(pairs):
                                ins = eng.matmul(PS[m][:, 0:T], x, y_, start=(g == 0 and n_ == 0),
                                                 stop=(g == held - 1 and n_ == 5), skip_group_check=True)
                            return ins
                        t = pr.put("pe", make, tv, t_a[2 * g + 1], bank_free[m] if g == 0 else None)
                        if g == held - 1:
                            bank_free[m] = t_acc = cp(ACC[:, m, 0:T], PS[m][:, 0:T], t, now,
                                                      e="act" if m % 2 else "dve")
                            acc_there[m] = t_acc
                    else:
                        b = bank()
                        t = mm(b, [(PS[b][:, 0:T], pairs)], tv, t_a[2 * g + 1])
                        if g == 0:
                            t_acc = cp(ACC[:, m, 0:T], PS[b][:, 0:T], t, now)
                        else:
                            t_acc = tt(ACC[:, m, 0:T], ACC[:, m, 0:T], PS[b][:, 0:T], AD, t, acc_there.get(m))
                        bank_free[b] = t_acc
                slot_free[sl] = t
                a_free[g % 2] = t
        for m in range(8):
            for s, (a, z) in streams:
                src = PS[yb[m // 2]][:, 256 * (m % 2):256 * (m % 2) + 256] if l == 1 else ACC[:, m, a:z]
                t2 = stt(XT[:, m, a:z], src, MOD[l][:, 40 + m, s:s + 1], XT[:, m, a:z], M, AD,
                         t if l == 1 else t_acc)
        for b in yb:
            kept.discard(b)
            bank_free[b] = t2
        pr.phase()

    mod1, mod2, ada_ready = [[], []], [[], []], []

    def plus_one(l, a, got):
        got.append(ts(MOD[l][:, a:a + 8, :], MOD[l][:, a:a + 8, :], 1.0, None, AD, None, got[-1]))

    def plus_one_later(l, a, got):
        plus_one(l, a, got)
        yield

    later.append(mod_layer(0, 0, 16, mod1[0]))
    some(100)
    plus_one(0, 8, mod1[0])
    later.append(mod_layer(0, 16, 32, mod2[0]))
    later.append(plus_one_later(0, 32, mod2[0]))
    later.append(mod_layer(1, 0, 16, mod1[1]))
    later.append(mod_layer(1, 16, 32, mod2[1]))
    later.append(ada_layer(ada_ready))
    mixer(0)
    peer(0)
    plus_one(1, 8, mod1[1])
    plus_one(1, 32, mod2[1])
    mixer(1)
    peer(1)

    t_ada = ada_ready[-1]
    for j in (1, 4, 7):
        t_ada = ts(ADA[:, 8 * j:8 * j + 8], ADA[:, 8 * j:8 * j + 8], 1.0, None, AD, None, t_ada)
    pr.held["dve"] = [pr.held.get("dve"), t_ada]
    lay = Lay()
    rstd = lay.take(256)
    t = inverse_root(lambda k: XT[:, k, 0:256], 8, 256, lambda k: ACC[:, k, 0:256], rstd, 1024, 0, pr.last("dve"))
    for k in range(8):
        t = stt(XT[:, k, 0:256], XT[:, k, 0:256], V("final_g", k), rstd, M, M, t)

    sqb = ACC[:, :, 256:512]

    def add_normed(src, gain, gate, factor, rstd, t_in):
        t = inverse_root(lambda k: src[:, k, 0:256], 8, 256, lambda k: sqb[:, k, :], rstd, 1024, 0, t_in,
                         pr.last("pe"))
        if factor != 1.0:
            t = ts(rstd, rstd, factor, None, M, None, t)
        for k in range(8):
            t1 = stt(src[:, k, 0:256], src[:, k, 0:256], V(gain, k), rstd, M, M, t)
            t2 = stt(XT[:, k, 0:256], src[:, k, 0:256], ADA[:, 8 * gate + k:8 * gate + k + 1], XT[:, k, 0:256],
                     M, AD, t1)
        pr.phase()
        return t2

    X1 = [(0, (0, 256))]

    tab = Lay(AREA - 8192 - 15 * 16 - 1024)
    BB = [tab.take(512).rearrange("p (k i h) -> p k i h", k=2, i=8) for _ in range(2)]
    kept_from = tab.at
    EC = tab.take(4096).rearrange("p (i t) -> p i t", i=16)
    ES = tab.take(4096).rearrange("p (i t) -> p i t", i=16)

    def tables():
        names = ["dt", "rr", "th", "kf", "fr", "er", "lr", "li", "a", "b", "n", "cr", "ci", "x", "y"]
        s16 = {n: tab.take(16) for n in names}
        BT = [XT[:, 2 * s:2 * s + 2, 256:512].rearrange("p k (c m) -> p k c m", c=2) for s in range(2)]
        CB = [XT[:, 4 + 2 * s:6 + 2 * s, 256:512].rearrange("p k (i h) -> p k i h", i=8) for s in range(2)]
        tmpb = [ACC[:, s, 256:512].rearrange("p (i h) -> p i h", i=16) for s in range(2)]
        pbc = Piece(A["ssm_bc"], 1024)
        bc = pbc.ap.rearrange("p (n i h) -> p n i h", n=4, i=16)
        D = lambda: pr.last("dve")
        g = s16
        t = act(g["dt"], V("log_step"), ACT.Exp)
        t = tt(g["x"], V("a_re"), g["dt"], M, t)
        t = act(g["rr"], g["x"], ACT.Exp, t)
        t_r = t
        t = tt(g["th"], V("a_im"), g["dt"], M, t)
        HI, MID, LO = 6.28125, 0.0019350051879882812, 3.019916e-07
        t = ts(g["y"], g["th"], 1.0 / TWO_PI, None, M, None, t)
        t = ts(g["kf"], g["y"], 12582912.0, -12582912.0, AD, AD, t)
        t = stt(g["fr"], g["kf"], -HI, g["th"], M, AD, t)
        t = stt(g["fr"], g["kf"], -MID, g["fr"], M, AD, t)
        t = stt(g["fr"], g["kf"], -LO, g["fr"], M, AD, t)
        t = ts(g["fr"], g["fr"], 3.1415925, -3.1415925, ALU.min, ALU.max, t)
        t_s = act(g["li"], g["fr"], ACT.Sin, t)
        t = ts(g["y"], g["fr"], -1.0, None, M, None, t)
        t = tt(g["y"], g["y"], g["fr"], ALU.max, t)
        t = ts(g["y"], g["y"], -1.0, 1.5707963267948966, M, AD, t)
        t = act(g["lr"], g["y"], ACT.Sin, t)
        t = cp(EC[:, :, 0], g["lr"], t, t_s)
        t = cp(ES[:, :, 0], g["li"], t)
        t = tt(g["lr"], g["lr"], g["rr"], M, t, t_r)
        t = tt(g["li"], g["li"], g["rr"], M, t)
        t = ts(g["lr"], g["lr"], -1.0, None, AD, None, t)
        t = tt(g["a"], V("a_re"), V("a_re"), M, t)
        t = tt(g["b"], V("a_im"), V("a_im"), M, t)
        t = tt(g["n"], g["a"], g["b"], AD, t)
        t = pr.put("dve", lambda e: e.reciprocal(g["n"], g["n"]), t)
        t = tt(g["a"], g["lr"], V("a_re"), M, t)
        t = tt(g["b"], g["li"], V("a_im"), M, t)
        t = tt(g["cr"], g["a"], g["b"], AD, t)
        t = tt(g["cr"], g["cr"], g["n"], M, t)
        t = tt(g["a"], g["li"], V("a_re"), M, t)
        t = tt(g["b"], g["lr"], V("a_im"), M, t)
        t = tt(g["ci"], g["a"], g["b"], SU, t)
        t = tt(g["ci"], g["ci"], g["n"], M, t)
        cr = g["cr"].unsqueeze(2).to_broadcast([128, 16, 16])
        ci = g["ci"].unsqueeze(2).to_broadcast([128, 16, 16])
        for X in BB + CB:
            t = pr.put("dve", lambda e, X=X: e.memset(X, 0.0), t)

        def blocks(dst, src, t, scale=None):
            for s in range(2):
                t0 = ts(dst[64 * s:64 * s + 64, :, :, 16 * s:16 * s + 16],
                        src[64 * s:64 * s + 64].rearrange("p (k i) h -> p k i h", k=2), scale or 1.0, None, M, None, t)
            return t0

        t = tt(tmpb[0], bc[:, 0], cr, M, t, pbc.here)
        t = tt(tmpb[1], bc[:, 1], ci, M, t)
        t = tt(tmpb[0], tmpb[0], tmpb[1], SU, t)
        t = blocks(BB[0], tmpb[0], t)
        t = tt(tmpb[0], bc[:, 1], cr, M, t)
        t = tt(tmpb[1], bc[:, 0], ci, M, t)
        t = tt(tmpb[0], tmpb[0], tmpb[1], AD, t)
        t = blocks(BB[1], tmpb[0], t)
        t = blocks(CB[0], bc[:, 2], t)
        t = blocks(CB[1], bc[:, 3], t, -1.0)
        pbc.release = t
        for s in range(2):
            b = bank()
            t1 = tp(b, [(PS[b][:, 128 * c:128 * c + 128], BB[s][:, c // 2, 4 * (c % 2):4 * (c % 2) + 4, :].rearrange("p i h -> p (i h)"))
                        for c in range(4)], t)
            t1 = cp(BT[s], PS[b][:, :].rearrange("p (k c m) -> p k c m", k=2, c=2), t1, e="act")
            bank_free[b] = t1
        t_bt = t1
        n = 1
        t = D()
        while n < 256:
            for i0, ni in ((0, 16),) if n < 128 else ((0, 8), (8, 8)):
                cN = EC[:, i0:i0 + ni, n - 1:n].to_broadcast([128, ni, n])
                sN = ES[:, i0:i0 + ni, n - 1:n].to_broadcast([128, ni, n])
                c0, s0 = EC[:, i0:i0 + ni, 0:n], ES[:, i0:i0 + ni, 0:n]
                c1, s1 = EC[:, i0:i0 + ni, n:2 * n], ES[:, i0:i0 + ni, n:2 * n]
                r_ = 256 * 4 // ni if n == 128 else 64
                a, bb = ([ACC[:, 4 * s:4 * s + 4, 256:512].rearrange("p k (i t) -> p k i t", t=r_)[:, :, :, 0:n]
                          for s in range(2)])
                v = lambda x: x.rearrange("p (k i) t -> p k i t", k=4)
                t1 = tt(a, v(s0), v(sN), M, t)
                t2 = tt(bb, v(s0), v(cN), M, t)
                t3 = tt(c1, c0, cN, M, t)
                t4 = tt(s1, c0, sN, M, t)
                t3 = tt(v(c1), v(c1), a, SU, t4)
                t = tt(v(s1), v(s1), bb, AD, t3)
            n *= 2
        return t, t_bt, BT, CB, g["rr"]

    def feed_forward(n, j0, beside=None):
        lay = Lay()
        rstd = lay.take(256)
        F = lay.take(22 * 256).rearrange("p (m t) -> p m t", m=22)
        sg = [lay.take(256) for _ in range(2)]
        t_h = modulated(X1, 256, lambda k, s: ADA[:, 8 * (j0 + 1) + k:8 * (j0 + 1) + k + 1],
                        lambda k, s: ADA[:, 8 * j0 + k:8 * j0 + k + 1], rstd, gain=lambda k: V(f"pre{n}", k))
        done = [None]
        wg, wu = A[f"w{n}_gate"], A[f"w{n}_up"]
        pend = []
        tf = [None]

        def finish(m, bg, tg, bu, tu):
            t1 = act(sg[m % 2], PS[bg][:, 0:256], ACT.Silu, tg, tf[0])
            bank_free[bg] = t1
            tf[0] = tt(F[:, m, :], sg[m % 2], PS[bu][:, 0:256], M, t1, tu)
            bank_free[bu] = tf[0]

        def take_gate(m, b, t):
            pend.append((m, b, t))

        def take_up(m, b, t):
            m_, bg, tg = pend.pop(0)
            assert m_ == m
            finish(m, bg, tg, b, t)

        seq = []
        for c in range(11):
            for w in (wg, wu):
                seq += [(w, c, 0), (w, c, 1)]
        cur = {}
        queued = None
        for item in seq + [None]:
            nxt = None
            if item is not None:
                w, c, i = item
                if i == 0:
                    cur["p"] = weight(w, 256 * c, 256)
                p = cur["p"]
                sl = take_slot()
                v = [SR[sl][:, s_, :].rearrange("p (k m) -> p k m", k=8) for s_ in range(2)]
                t = two_parts(v[0], v[1], p.w[:, :, 128 * i:128 * i + 128], slot_free[sl], p.here)
                p.release = [t, pr.last("act")]
                nxt = (w is wg, 2 * c + i, sl, v, t)
            if queued is not None:
                is_gate, m, sl, v, t = queued
                b = bank()
                t = mm(b, [(PS[b][:, 0:256], three(lambda a, k: v[a][:, k, :], lambda c_, k: HRs[0][:, c_, k, 0:256],
                                                   range(8)))], t_h, t)
                slot_free[sl] = t
                (take_gate if is_gate else take_up)(m, b, t)
            queued = nxt
        t_f = tf[0]
        for m in range(8):
            if m == 1 and beside is not None:
                done = beside()
            b = bank()
            for kh in range(2):
                src = A[f"w{n}_down"].rearrange("(k p) m -> p k m", p=128)[:, 11 * kh:11 * kh + 11,
                                                                            128 * m:128 * m + 128]
                p = Piece(src, 1408)
                p.w = p.ap.rearrange("p (k m) -> p k m", k=11)

                def make(eng, p=p, kh=kh, b=b):
                    for k in range(11):
                        ins = eng.matmul(PS[b][:, 0:256], p.w[:, k, :], F[:, 11 * kh + k, :],
                                         start=(kh == 0 and k == 0), stop=(kh == 1 and k == 10))
                    return ins
                t = pr.put("pe", make, t_f, p.here, bank_free[b])
                p.release = t
            t = cp(ACC[:, m, 0:256], PS[b][:, 0:256], t, e="act")
            bank_free[b] = t
        t = add_normed(ACC, f"post{n}", j0 + 2, 0.5, rstd, [t, done[0]])
        return t if beside is None else done

    t_e, t_bt, BT, CB, rr = feed_forward(1, 0, tables)

    lay = Lay()
    rstd = lay.take(256)
    uT = lay.take(1024).rearrange("p (k t) -> p k t", k=4)
    OT = lay.take(2048).rearrange("p (k t) -> p k t", k=8)
    base = lay.at
    q = lay.take(1024).rearrange("p (k t) -> p k t", k=4)
    kk = lay.take(256)
    vT = lay.take(256)
    vtok = lay.take(256).rearrange("p (c d) -> p c d", c=2)
    base_a = lay.at
    t_h = modulated(X1, 256, lambda k, s: ADA[:, 32 + k:33 + k], lambda k, s: ADA[:, 24 + k:25 + k], rstd,
                    gain=lambda k: V("prem", k))
    got2 = {}

    def take_p(m, b, t):
        o = q[:, m, :] if m < 4 else kk if m == 4 else vT if m == 5 else uT[:, m - 6, :]
        got2["p"] = cp(o, PS[b][:, 0:256], t, e="act")
        bank_free[b] = got2["p"]

    project_all(A["w_in2"], [0, 256, 512, 768, 1024], 256, t_h, take_p)
    t_p = got2["p"]
    b = bank()
    t = tp(b, [(PS[b][:, 128 * c:128 * c + 128], vT[:, 128 * c:128 * c + 128]) for c in range(2)], t_p)
    t_vt = cp(vtok, PS[b][:, 0:256].rearrange("p (c d) -> p c d", c=2), t, e="act")
    bank_free[b] = t_vt
    pb = Piece(A["alibi"], 2048)
    al = pb.ap.rearrange("p (h k) -> p h k", h=8)
    lay = Lay(base_a)
    pr.wait("dve", pb.here)
    T1 = ACC[:, 0:4, :].rearrange("p k t -> p (k t)")
    T2 = ACC[:, 4:8, :].rearrange("p k t -> p (k t)")
    two = lambda x: [x[:, 512 * i:512 * i + 512].rearrange("p (s t) -> p s t", s=2) for i in range(2)]
    ZS, XS, ZA = two(T1[:, 0:1024]), two(T2[:, 0:1024]), two(T2[:, 1024:2048])
    ZB = two(OT[:, 4:8, :].rearrange("p k t -> p (k t)"))
    yT = T1[:, 1024:2048].rearrange("p (k t) -> p k t", k=4)
    y_banks = [bank(), bank()]
    kept.update(y_banks)
    y_waits = [bank_free[x] for x in y_banks]
    scanned = []

    def scans():
        xs_free = [None, None]
        out_ = None

        def output(i, xs, t5):
            ch, lo = i // 4, 32 * (i % 4)
            o = PS[y_banks[ch // 2]][lo:lo + 32, 256 * (ch % 2):256 * (ch % 2) + 256]
            t6 = pr.put("pe", lambda e: (e.matmul(o, CB[0][:, i // 8, i % 8, :], xs[:, 0, :], start=True, stop=False),
                                         e.matmul(o, CB[1][:, i // 8, i % 8, :], xs[:, 1, :], start=False, stop=True))[1],
                        t5, y_waits)
            xs_free[i % 2] = t6
            scanned.append(t6)

        for i in range(16):
            ch, lo = i // 4, 32 * (i % 4)
            z = i % 2
            b = bank()
            t = mm(b, [(PS[b][:, 256 * s:256 * s + 256], [(BT[s][lo:lo + 32, ch // 2, ch % 2, :],
                                                           uT[lo:lo + 32, ch, :])]) for s in range(2)], t_bt, t_p)
            if out_ is not None:
                output(*out_)
            bu = PS[b][:, :].rearrange("p (s t) -> p s t", s=2)
            cB = EC[:, i:i + 1, :].to_broadcast([128, 2, 256])
            a, bb_, zs, xs = ZA[z], ZB[z], ZS[z], XS[z]
            t1 = tt(a, bu, cB, M, t, pr.last("dve"), t_e)
            for s in range(2):
                t2 = tt(bb_[:, s, :], bu[:, 1 - s, :], ES[:, i, :], M, t)
            bank_free[b] = t2
            tt(a[:, 0, :], a[:, 0, :], bb_[:, 0, :], AD, t2)
            t2 = tt(a[:, 1, :], a[:, 1, :], bb_[:, 1, :], SU, t2)
            rb = rr[:, i:i + 1].to_broadcast([128, 256])
            for s in range(2):
                t3 = pr.put("dve", lambda e, o=zs[:, s, :], d=a[:, s, :], rb=rb:
                            e.tensor_tensor_scan(o, rb, d, 0.0, M, AD), t2)
            t4 = tt(a, zs, cB, M, t3)
            for s in range(2):
                t4 = tt(bb_[:, s, :], zs[:, 1 - s, :], ES[:, i, :], M, t3)
            tt(xs[:, 0, :], a[:, 0, :], bb_[:, 0, :], SU, t4, xs_free[z])
            t5 = tt(xs[:, 1, :], a[:, 1, :], bb_[:, 1, :], AD, t4)
            out_ = (i, xs, t5)
            yield
        output(*out_)

    scan = scans()
    t_o = attend(q, kk, vtok, lambda i: OT[:, i, :], lay, [[0], [0, 1]], 0,
                 lambda h: V("sinks", h), lambda h, qt, N: al[:, h, 256 - N:256], [t_p, t_vt],
                 lambda: next(scan, None))
    for _ in scan:
        pass
    assert lay.at <= kept_from
    pb.release = pr.last("dve")
    pr.phase()

    for ch in range(4):
        t = stt(yT[:, ch, :], uT[:, ch, :], V("ssm_d", ch), PS[y_banks[ch // 2]][:, 256 * (ch % 2):256 * (ch % 2) + 256],
                M, AD, scanned[-1], pr.last("dve"))
        bank_free[y_banks[ch // 2]] = t
        t_y = act(yT[:, ch, :], yT[:, ch, :], ACT.Gelu_apprx_tanh, t)
    kept.clear()
    for mh in range(2):
        p = weight(A["w_glu"], 256 * mh, 256)
        for mi in range(2):
            m = 2 * mh + mi
            b = bank()
            t = mm(b, [(PS[b][:, 0:256], [(p.w[:, k, 128 * mi:128 * mi + 128], yT[:, k, :]) for k in range(4)])], t_y,
                   p.here)
            p.release = t
            sg = ZA[m % 2][:, 0, :]
            t = act(sg, PS[b][:, 0:256], ACT.Sigmoid, t, pr.last("dve"), bias=V("b_glu", m))
            bank_free[b] = t
            t_m = tt(OT[:, 4 + m, :], yT[:, m, :], sg, M, t)
    t = merged(lambda h, k: OT[:, 4 * h + k, :], 256, lambda h, k: V("g_attn" if h == 0 else "g_ssm", k), ACC, rstd,
               [t_m, t_m])

    def take_w(m, b, t):
        got2["w"] = cp(ACC[:, m, 0:256], PS[b][:, 0:256], t, e="act")
        bank_free[b] = got2["w"]

    project_all(A["w_out"], [0, 256, 512, 768], 256, t, take_w)
    t2 = got2["w"]
    add_normed(ACC, "postm", 5, 1.0, rstd, t2)
    t = feed_forward(2, 6)
    s_out = pr.new_sem("s_out")
    t = pr.dma("act", s_out, out.rearrange("(k p) t -> p k t", p=128), XT[:, :, 0:256], t)
    pr.wait("act", t)

    for p in pieces:
        prev = pieces[p.n - RING].release if p.n >= RING else None
        assert p.n < RING or prev is not None, p.n
        dst = p.ap
        if len(p.src.shape) == 3:
            dst = dst.rearrange("p (k m) -> p k m", k=p.src.shape[1])
        got = pr.dma("sp", slot_sem[p.slot], dst, p.src, prev)
        assert got == p.here

    block = ctx.enter_context(nc.Block())

    @block.sync
    def _(eng):
        pr.emit("sp", eng)

    @block.tensor
    def _(eng):
        pr.emit("pe", eng)

    @block.scalar
    def _(eng):
        pr.emit("act", eng)

    @block.vector
    def _(eng):
        pr.emit("dve", eng)

    @block.gpsimd
    def _(eng):
        pr.emit("pool", eng)


def constants():
    con = np.zeros((128, CON["n"]), np.float32)

    def put(name, a):
        o, w = CON[name]
        con[:, o:o + w] = a

    put("ones", np.ones((128, 128)))
    p = np.arange(128)
    put("blk", (p[:, None] // 64 == p[None, :] // 64))
    put("ident", np.eye(128))
    rot = np.zeros((128, 128), np.float32)
    for m in range(128):
        if m % 64 < 32:
            rot[m + 32, m] = -1.0
        else:
            rot[m - 32, m] = 1.0
    put("rot", rot)
    n = 16
    inv = np.float32(10000.0) ** (-np.arange(n, dtype=np.float32) / np.float32(n))
    tok = np.arange(256)
    ang = np.concatenate([(tok // 64).astype(np.float32)[:, None] * inv, (tok % 64).astype(np.float32)[:, None] * inv], 1)
    cos, sin = np.cos(ang).astype(np.float32), np.sin(ang).astype(np.float32)
    put("cos", cos.T[p % 32])
    put("sin", sin.T[p % 32])
    put("iota", np.arange(128)[None, :])
    put("eps", np.array([[1e-6, 1e-5]]))
    sel = np.zeros((128, 2), np.float32)
    for i in range(4):
        sel[32 * i, 0] = sel[32 * i + 1, 1] = 1.0
    put("sel", sel)
    al = np.zeros((128, 8, 256), np.float32)
    dist = np.arange(128)[:, None] + 128 - np.arange(256)[None, :]
    for h in range(8):
        al[:, h] = np.where((dist >= 0) & (dist < 128), -(2.0 ** (-(h + 1))) * dist, -1e30)
    return con, al.reshape(128, 2048)


def kernel(**inputs):
    import concourse.bacc as bacc
    from concourse.bass_utils import run_bass_kernel_spmd

    I = {k: np.asarray(v) for k, v in inputs.items()}

    def cols(v):
        return v.reshape(-1, 128).T

    def heads(v):
        return v.reshape((2, 4, 64) + v.shape[1:]).swapaxes(0, 1).reshape(v.shape)

    parts = []
    for l in range(2):
        parts += [cols(I["b_mod"][l]), np.concatenate([I["q_gain"][l]] * 2)[:, None],
                  np.concatenate([I["k_gain"][l]] * 2)[:, None],
                  I["conv_w"][l].reshape(31, 4, 128).transpose(2, 1, 0).reshape(128, 124),
                  cols(I["conv_b"][l]), cols(I["ln_g"][l]), cols(I["ln_b"][l]), cols(heads(I["beta_attn"][l])),
                  cols(I["beta_conv"][l])]
    st = lambda a: a.reshape(16, 128).T
    ls = np.broadcast_to(I["ssm_log_step_2"][0][:, None], (32, 64))
    parts += [cols(I["c"][0]), cols(I["c_ctx"]), cols(I["c_2"][0]), cols(I["final_g"]), cols(I["b_ada_2"][0]),
              cols(I["g_pre_ff1_2"][0]), cols(I["g_post_ff1_2"][0]), cols(I["g_pre_mix_2"][0]),
              cols(I["g_post_mix_2"][0]), cols(I["g_pre_ff2_2"][0]), cols(I["g_post_ff2_2"][0]),
              cols(I["ssm_d_2"][0]), cols(I["ssm_b_glu_2"][0]), cols(heads(I["g_attn_out_2"][0])),
              cols(I["g_ssm_out_2"][0]), st(I["ssm_a_re_2"][0]), st(I["ssm_a_im_2"][0]), st(ls),
              np.broadcast_to(I["attn_sinks_2"], (128, 8))]
    con, al = constants()

    def in_cols(w):
        return np.concatenate([w[:, 0:512].reshape(-1, 2, 4, 64).swapaxes(1, 2).reshape(-1, 512), w[:, 512:]], 1)

    def out_rows(w):
        return np.concatenate([heads(w[0:512]), w[512:]], 0)

    bsel = lambda a: a.reshape(16, 2, 64, 16).transpose(1, 2, 0, 3).reshape(128, 256)
    csel = lambda a: a.reshape(16, 2, 16, 64).transpose(1, 3, 0, 2).reshape(128, 256)
    arrays = {
        "vec": np.concatenate(parts, 1), "con": con, "alibi": al,
        "xT": np.concatenate([I["x"][0], I["ctx"][0]], 0).T,
        "w_mod": I["w_mod"], "w_ada": I["w_ada_2"][0],
        "w_in": np.stack([in_cols(w) for w in I["w_in"]]),
        "w_o": np.stack([out_rows(w) for w in I["w_o"]]),
        "peer_wq": I["peer_wq"],
        "keysT": I["peer_keys"].transpose(0, 2, 4, 1, 3).reshape(2, 128, 1024),
        "peer_uT": I["peer_u"].reshape(2, 64, 2, 128, 8, 128).transpose(0, 1, 5, 2, 4, 3).reshape(2, 64, 128, 2048),
        "peer_v": I["peer_v"],
        "w1_gate": I["w1_gate_2"][0], "w1_up": I["w1_up_2"][0], "w1_down": I["w1_down_2"][0],
        "w2_gate": I["w2_gate_2"][0], "w2_up": I["w2_up_2"][0], "w2_down": I["w2_down_2"][0],
        "w_in2": in_cols(I["w_in_2"][0]), "w_out": out_rows(I["w_out_2"][0]), "w_glu": I["ssm_w_glu_2"][0],
        "ssm_bc": np.concatenate([bsel(I["ssm_b_re_2"][0]), bsel(I["ssm_b_im_2"][0]),
                                  csel(I["ssm_c_re_2"][0]), csel(I["ssm_c_im_2"][0])], 1),
    }
    arrays = {k: np.ascontiguousarray(v) for k, v in arrays.items()}
    nc = bacc.Bacc("TRN2", target_bir_lowering=False, num_devices=1)
    A = {k: nc.dram_tensor(f"in_{k}", v.shape, mybir.dt.from_np(v.dtype), kind="ExternalInput").ap()
         for k, v in arrays.items()}
    out = nc.dram_tensor("out_T", (1024, 256), F32, kind="ExternalOutput").ap()
    build(nc, A, out)
    r = run_bass_kernel_spmd(nc, [{f"in_{k}": v for k, v in arrays.items()}], core_ids=[0])
    return np.ascontiguousarray(r.results[0]["out_T"].T)[None]
```
